# Optimizing a Trainium2 kernel written in Bass

```python
import math
import jax, jax.numpy as jnp
from jax import lax
import numpy as np

D_MODEL = 1024
BATCH = 1
SEQ = 512
DEPTH = 1

N_MEM = 256
ROPE_THETA = 500000.0
Q_BLOCK = 128
NEG_INF = -1e30
LN_EPS = 1e-5
RMS_EPS = 1e-6

DIFF_HEADS = 4
DIFF_QK_DIM = 64
DIFF_V_DIM = 128
DIFF_ROT_DIM = DIFF_QK_DIM // 4
MLA_HEADS = 4
MLA_Q_RANK = 256
MLA_KV_RANK = 128
MLA_NOPE_DIM = 128
MLA_ROPE_DIM = 64
MLA_V_DIM = 128
MIX_WIDTH = DIFF_HEADS * DIFF_V_DIM + MLA_HEADS * MLA_V_DIM
DIFF_Q_COLS = DIFF_HEADS * 2 * DIFF_QK_DIM
DIFF_K_COLS = DIFF_HEADS * 2 * DIFF_QK_DIM
DIFF_V_COLS = DIFF_HEADS * DIFF_V_DIM
IN_COLS = DIFF_Q_COLS + DIFF_K_COLS + DIFF_V_COLS + MLA_Q_RANK + MLA_KV_RANK + MLA_ROPE_DIM
IN_SPLITS = (DIFF_Q_COLS,
             DIFF_Q_COLS + DIFF_K_COLS,
             DIFF_Q_COLS + DIFF_K_COLS + DIFF_V_COLS,
             DIFF_Q_COLS + DIFF_K_COLS + DIFF_V_COLS + MLA_Q_RANK,
             DIFF_Q_COLS + DIFF_K_COLS + DIFF_V_COLS + MLA_Q_RANK + MLA_KV_RANK)
MEM_HEADS = 4
MEM_HEAD_DIM = 128
N_EXPERTS = 64
TOP_K = 8
N_GROUPS = 8
TOPK_GROUPS = 4
EXPERT_DIM = 256
SHARED_DIM = 256
ROUTED_SCALE = 2.5
DEEPNORM_ALPHA = (2.0 * DEPTH) ** 0.25
DEEPNORM_BETA = (8.0 * DEPTH) ** -0.25

kernel_name = 'hybrid_diffattn_mla_moe_deepnorm'

def layer_norm(x, g, b):
    xf = x.astype(jnp.float32)
    mu = jnp.mean(xf, axis=-1, keepdims=True)
    var = jnp.mean(jnp.square(xf - mu), axis=-1, keepdims=True)
    return ((xf - mu) * lax.rsqrt(var + LN_EPS)).astype(x.dtype) * g + b

def rms_norm(x, g):
    xf = x.astype(jnp.float32)
    return (xf * lax.rsqrt(jnp.mean(jnp.square(xf), axis=-1, keepdims=True) + RMS_EPS)).astype(x.dtype) * g

def rope_tables(positions, dim):
    inv_freq = ROPE_THETA ** (-jnp.arange(0, dim, 2, dtype=jnp.float32) / dim)
    ang = positions.astype(jnp.float32)[..., None] * inv_freq
    return jnp.cos(ang)[:, :, None, :], jnp.sin(ang)[:, :, None, :]

def apply_rope(x, cos, sin):
    x1, x2 = jnp.split(x.astype(jnp.float32), 2, axis=-1)
    return jnp.concatenate([x1 * cos - x2 * sin, x2 * cos + x1 * sin], axis=-1).astype(x.dtype)

def partial_rope(x, cos, sin, rot_dim):
    return jnp.concatenate([apply_rope(x[..., :rot_dim], cos, sin), x[..., rot_dim:]], axis=-1)

def causal_attention(q, k, v, scale):
    B, S, H, Dk = q.shape
    Dv = v.shape[-1]
    nb = S // Q_BLOCK
    q_blocks = q.reshape(B, nb, Q_BLOCK, H, Dk).transpose(1, 0, 2, 3, 4)
    key_idx = jnp.arange(S)

    def one_block(args):
        qb, b_idx = args
        s = jnp.einsum('bqhd,bkhd->bhqk', qb, k, preferred_element_type=jnp.float32) * scale
        q_idx = b_idx * Q_BLOCK + jnp.arange(Q_BLOCK)
        s = jnp.where(key_idx[None, :] <= q_idx[:, None], s, NEG_INF)
        p = jax.nn.softmax(s, axis=-1).astype(v.dtype)
        return jnp.einsum('bhqk,bkhd->bqhd', p, v)

    out = lax.map(one_block, (q_blocks, jnp.arange(nb)))
    return out.transpose(1, 0, 2, 3, 4).reshape(B, S, H, Dv)

def hybrid_mixer(x, cos_d, sin_d, cos_m, sin_m, layer_idx, w_in, lam_q1, lam_k1, lam_q2, lam_k2,
                 diff_subln_g, mla_q_norm_g, mla_w_uq, mla_kv_norm_g, mla_w_ukv, mla_out_norm_g, w_o):
    B, S, _ = x.shape
    proj = jnp.einsum('bsd,dc->bsc', x, w_in)
    d_q, d_k, d_v, c_q, c_kv, k_rope = jnp.split(proj, IN_SPLITS, axis=-1)

    d_q = partial_rope(d_q.reshape(B, S, 2 * DIFF_HEADS, DIFF_QK_DIM), cos_d, sin_d, DIFF_ROT_DIM)
    d_k = partial_rope(d_k.reshape(B, S, 2 * DIFF_HEADS, DIFF_QK_DIM), cos_d, sin_d, DIFF_ROT_DIM)
    d_q = d_q.reshape(B, S, DIFF_HEADS, 2, DIFF_QK_DIM)
    d_k = d_k.reshape(B, S, DIFF_HEADS, 2, DIFF_QK_DIM)
    d_v = d_v.reshape(B, S, DIFF_HEADS, DIFF_V_DIM)
    lam_init = 0.8 - 0.6 * math.exp(-0.3 * layer_idx)
    lam = (jnp.exp(jnp.sum(lam_q1.astype(jnp.float32) * lam_k1.astype(jnp.float32)))
           - jnp.exp(jnp.sum(lam_q2.astype(jnp.float32) * lam_k2.astype(jnp.float32))) + lam_init)
    scale_d = DIFF_QK_DIM ** -0.5
    a1 = causal_attention(d_q[:, :, :, 0], d_k[:, :, :, 0], d_v, scale_d)
    a2 = causal_attention(d_q[:, :, :, 1], d_k[:, :, :, 1], d_v, scale_d)
    diff_out = rms_norm(a1 - lam.astype(a1.dtype) * a2, diff_subln_g) * (1.0 - lam_init)

    q = jnp.einsum('bsr,rc->bsc', rms_norm(c_q, mla_q_norm_g), mla_w_uq)
    q = q.reshape(B, S, MLA_HEADS, MLA_NOPE_DIM + MLA_ROPE_DIM)
    q_nope, q_pe = jnp.split(q, [MLA_NOPE_DIM], axis=-1)
    kv = jnp.einsum('bsr,rc->bsc', rms_norm(c_kv, mla_kv_norm_g), mla_w_ukv)
    kv = kv.reshape(B, S, MLA_HEADS, MLA_NOPE_DIM + MLA_V_DIM)
    k_nope, v_m = jnp.split(kv, [MLA_NOPE_DIM], axis=-1)
    k_pe = apply_rope(k_rope[:, :, None, :], cos_m, sin_m)
    q_m = jnp.concatenate([q_nope, apply_rope(q_pe, cos_m, sin_m)], axis=-1)
    k_m = jnp.concatenate([k_nope, jnp.broadcast_to(k_pe, (B, S, MLA_HEADS, MLA_ROPE_DIM))], axis=-1)
    mla_out = causal_attention(q_m, k_m, v_m, (MLA_NOPE_DIM + MLA_ROPE_DIM) ** -0.5)
    mla_out = rms_norm(mla_out, mla_out_norm_g)

    mixed = jnp.concatenate([diff_out.reshape(B, S, DIFF_HEADS * DIFF_V_DIM),
                             mla_out.reshape(B, S, MLA_HEADS * MLA_V_DIM)], axis=-1)
    return jnp.einsum('bsc,cd->bsd', mixed, w_o)

def memory_attention(x, mem, w_q, w_k, w_v, w_o):
    B, S, _ = x.shape
    q = jnp.einsum('bsd,dc->bsc', x, w_q).reshape(B, S, MEM_HEADS, MEM_HEAD_DIM)
    k = jnp.einsum('bmd,dc->bmc', mem, w_k).reshape(B, N_MEM, MEM_HEADS, MEM_HEAD_DIM)
    v = jnp.einsum('bmd,dc->bmc', mem, w_v).reshape(B, N_MEM, MEM_HEADS, MEM_HEAD_DIM)
    s = jnp.einsum('bshd,bmhd->bhsm', q, k, preferred_element_type=jnp.float32) * MEM_HEAD_DIM ** -0.5
    p = jax.nn.softmax(s, axis=-1).astype(v.dtype)
    o = jnp.einsum('bhsm,bmhd->bshd', p, v).reshape(B, S, MEM_HEADS * MEM_HEAD_DIM)
    return jnp.einsum('bsc,cd->bsd', o, w_o)

def moe_ffn(x, router_w, router_bias, w_gate, w_up, w_down, sh_gate, sh_up, sh_down):
    B, S, D = x.shape
    t = x.reshape(B * S, D)
    T = t.shape[0]
    scores = jax.nn.sigmoid(jnp.dot(t, router_w, preferred_element_type=jnp.float32))
    choice = scores + router_bias.astype(jnp.float32)
    group_score = lax.top_k(choice.reshape(T, N_GROUPS, N_EXPERTS // N_GROUPS), 2)[0].sum(-1)
    _, top_groups = lax.top_k(group_score, TOPK_GROUPS)
    group_mask = jnp.sum(jax.nn.one_hot(top_groups, N_GROUPS, dtype=jnp.float32), axis=1) > 0
    expert_mask = jnp.repeat(group_mask, N_EXPERTS // N_GROUPS, axis=-1)
    _, top_idx = lax.top_k(jnp.where(expert_mask, choice, NEG_INF), TOP_K)
    top_w = jnp.take_along_axis(scores, top_idx, axis=-1)
    top_w = top_w / jnp.sum(top_w, axis=-1, keepdims=True) * ROUTED_SCALE
    gates = jnp.zeros((T, N_EXPERTS), jnp.float32).at[jnp.arange(T)[:, None], top_idx].set(top_w)
    gates = gates.astype(t.dtype)
    out = jnp.dot(jax.nn.silu(t @ sh_gate) * (t @ sh_up), sh_down)
    for e in range(N_EXPERTS):
        h = jax.nn.silu(t @ w_gate[e]) * (t @ w_up[e])
        out = out + gates[:, e:e + 1] * (h @ w_down[e])
    return out.reshape(B, S, D)

def setup_inputs(seed: int = 0) -> dict:
    key = jax.random.key(seed)
    ks = iter(jax.random.split(key, 40))
    L = DEPTH

    def nrm(shape):
        return jax.random.normal(next(ks), shape, jnp.float32)

    def w(shape, fan_in, scale=1.0):
        return nrm(shape) * (scale * fan_in ** -0.5)

    def gain(shape):
        return 1.0 + 0.02 * nrm(shape)

    x = nrm((BATCH, SEQ, D_MODEL))
    mem = nrm((BATCH, N_MEM, D_MODEL))
    offset = jax.random.randint(next(ks), (BATCH, 1), 0, 1024, dtype=jnp.int32)
    positions = (offset + jnp.arange(SEQ, dtype=jnp.int32)[None, :]).astype(jnp.int32)
    return {
        'x': x,
        'mem': mem,
        'positions': positions,
        'w_in': w((L, D_MODEL, IN_COLS), D_MODEL),
        'lam_q1': 0.1 * nrm((L, DIFF_QK_DIM)),
        'lam_k1': 0.1 * nrm((L, DIFF_QK_DIM)),
        'lam_q2': 0.1 * nrm((L, DIFF_QK_DIM)),
        'lam_k2': 0.1 * nrm((L, DIFF_QK_DIM)),
        'diff_subln_g': gain((L, DIFF_V_DIM)),
        'mla_q_norm_g': gain((L, MLA_Q_RANK)),
        'mla_w_uq': w((L, MLA_Q_RANK, MLA_HEADS * (MLA_NOPE_DIM + MLA_ROPE_DIM)), MLA_Q_RANK),
        'mla_kv_norm_g': gain((L, MLA_KV_RANK)),
        'mla_w_ukv': w((L, MLA_KV_RANK, MLA_HEADS * (MLA_NOPE_DIM + MLA_V_DIM)), MLA_KV_RANK),
        'mla_out_norm_g': gain((L, MLA_V_DIM)),
        'w_o': w((L, MIX_WIDTH, D_MODEL), MIX_WIDTH, DEEPNORM_BETA),
        'ln1_g': gain((L, D_MODEL)),
        'ln1_b': 0.02 * nrm((L, D_MODEL)),
        'mem_w_q': w((L, D_MODEL, MEM_HEADS * MEM_HEAD_DIM), D_MODEL),
        'mem_w_k': w((L, D_MODEL, MEM_HEADS * MEM_HEAD_DIM), D_MODEL),
        'mem_w_v': w((L, D_MODEL, MEM_HEADS * MEM_HEAD_DIM), D_MODEL),
        'mem_w_o': w((L, MEM_HEADS * MEM_HEAD_DIM, D_MODEL), MEM_HEADS * MEM_HEAD_DIM, DEEPNORM_BETA),
        'ln2_g': gain((L, D_MODEL)),
        'ln2_b': 0.02 * nrm((L, D_MODEL)),
        'router_w': w((L, D_MODEL, N_EXPERTS), D_MODEL),
        'router_bias': 0.01 * nrm((L, N_EXPERTS)),
        'exp_w_gate': w((L, N_EXPERTS, D_MODEL, EXPERT_DIM), D_MODEL),
        'exp_w_up': w((L, N_EXPERTS, D_MODEL, EXPERT_DIM), D_MODEL),
        'exp_w_down': w((L, N_EXPERTS, EXPERT_DIM, D_MODEL), EXPERT_DIM, DEEPNORM_BETA),
        'sh_w_gate': w((L, D_MODEL, SHARED_DIM), D_MODEL),
        'sh_w_up': w((L, D_MODEL, SHARED_DIM), D_MODEL),
        'sh_w_down': w((L, SHARED_DIM, D_MODEL), SHARED_DIM, DEEPNORM_BETA),
        'ln3_g': gain((L, D_MODEL)),
        'ln3_b': 0.02 * nrm((L, D_MODEL)),
    }

def reference(x, mem, positions, w_in, lam_q1, lam_k1, lam_q2, lam_k2, diff_subln_g,
              mla_q_norm_g, mla_w_uq, mla_kv_norm_g, mla_w_ukv, mla_out_norm_g, w_o, ln1_g, ln1_b,
              mem_w_q, mem_w_k, mem_w_v, mem_w_o, ln2_g, ln2_b,
              router_w, router_bias, exp_w_gate, exp_w_up, exp_w_down,
              sh_w_gate, sh_w_up, sh_w_down, ln3_g, ln3_b):
    cos_d, sin_d = rope_tables(positions, DIFF_ROT_DIM)
    cos_m, sin_m = rope_tables(positions, MLA_ROPE_DIM)
    h = x
    for l in range(DEPTH):
        mix = hybrid_mixer(h, cos_d, sin_d, cos_m, sin_m, l, w_in[l], lam_q1[l], lam_k1[l], lam_q2[l],
                           lam_k2[l], diff_subln_g[l], mla_q_norm_g[l], mla_w_uq[l], mla_kv_norm_g[l],
                           mla_w_ukv[l], mla_out_norm_g[l], w_o[l])
        h = layer_norm(DEEPNORM_ALPHA * h + mix, ln1_g[l], ln1_b[l])
        xat = memory_attention(h, mem, mem_w_q[l], mem_w_k[l], mem_w_v[l], mem_w_o[l])
        h = layer_norm(DEEPNORM_ALPHA * h + xat, ln2_g[l], ln2_b[l])
        ffn = moe_ffn(h, router_w[l], router_bias[l], exp_w_gate[l], exp_w_up[l], exp_w_down[l],
                      sh_w_gate[l], sh_w_up[l], sh_w_down[l])
        h = layer_norm(DEEPNORM_ALPHA * h + ffn, ln3_g[l], ln3_b[l])
    return h


_drawn_inputs = setup_inputs


def setup_inputs(seed=0):
    import zlib

    import numpy as np

    out = dict(_drawn_inputs(seed))
    spreads = {}
    factors = {'diff_subln_g': 3.181, 'ln3_g': 8.426, 'ln3_b': 7.953, 'mla_out_norm_g': 2.895}
    for name, (base, spread) in spreads.items():
        noise = np.random.default_rng([zlib.crc32(name.encode()), seed]).standard_normal(out[name].shape)
        drawn = base * np.exp(spread * noise) if base else spread * noise
        out[name] = __import__('jax').numpy.asarray(drawn.astype(out[name].dtype))
    for name, factor in factors.items():
        out[name] = (out[name] * factor).astype(out[name].dtype)
    return out
```

```python
import math
from contextlib import ExitStack

import concourse.bass as bass
import numpy as np
from concourse import mybir

F32 = mybir.dt.float32
BF16 = mybir.dt.bfloat16
I32 = mybir.dt.int32
U32 = mybir.dt.uint32
ALU = mybir.AluOpType
ACT = mybir.ActivationFunctionType
AX = mybir.AxisListType

P = 128
SEQ = 512
D = 1024
NT = SEQ // P
NC = D // P
N_MEM = 256
IN_COLS = 1984
LAT = 1536
THETA = 500000.0
ROT_D = 16
ROT_M = 64
HD = 4
QK_D = 64
NOPE = 128
ROPE = 64
N_EXP = 64
F_EXP = 256
N_GRP = 8
TOPK_GRP = 4
TOP_K = 8
ROUTED_SCALE = 2.5
ALPHA = 2.0 ** 0.25
LAM_INIT = 0.8 - 0.6 * math.exp(-0.3 * 0)
LN_EPS = 1e-5
RMS_EPS = 1e-6
SCALE_D = QK_D ** -0.5
SCALE_M = (NOPE + ROPE) ** -0.5
SCALE_X = 128 ** -0.5

UNROLL = 4
MAX_EXTRA = SEQ * TOP_K // P
MAX_ITEMS = N_EXP + MAX_EXTRA
LIST_COLS = MAX_ITEMS + UNROLL
NO_TOKEN = 4096
SLOT = 3 * NC * F_EXP


class Chain:

    def __init__(self, eng, sem):
        self.eng, self.sem, self.n = eng, sem, 0

    def __call__(self, ins):
        self.n += 1
        ins.then_inc(self.sem, 1)
        self.eng.wait_ge(self.sem, self.n)

    def tell(self, ins, sem, n):
        ins.then_inc(sem, 1)
        self.eng.wait_ge(sem, n)


def build(nc, x, mem, positions, w_in, lam_q1, lam_k1, lam_q2, lam_k2, diff_subln_g, mla_q_norm_g,
          mla_w_uq, mla_kv_norm_g, mla_w_ukv, mla_out_norm_g, w_o, ln1_g, ln1_b, mem_w_q, mem_w_k,
          mem_w_v, mem_w_o, ln2_g, ln2_b, router_w, router_bias, exp_w_gate, exp_w_up, exp_w_down,
          sh_w_gate, sh_w_up, sh_w_down, ln3_g, ln3_b, out):
    h2_rows = nc.dram_tensor("h2_rows", (SEQ, D), F32, kind="Internal").ap()
    y_rows = nc.dram_tensor("y_rows", (MAX_ITEMS * P, D), F32, kind="Internal").ap()
    token_list = nc.dram_tensor("token_list", (P * LIST_COLS, 1), U32, kind="Internal").ap()

    ctx = ExitStack()
    with ctx:
        def sb(name, shape, dt=F32):
            return ctx.enter_context(nc.sbuf_tensor(name, shape, dt))

        def sem(name):
            return ctx.enter_context(nc.semaphore(name))

        E = sb("expert_slots", [P, UNROLL * SLOT])
        X = sb("residual", [P, NT, D])
        AT = sb("act_transposed", [P, NC, SEQ])
        W = sb("weights", [P, 8192])
        PR = sb("proj", [P, NT, IN_COLS])
        MKV = sb("mem_k_v", [P, 2048])
        ident = sb("ident", [P, P])
        identb = sb("ident_bf16", [P, P], BF16)
        maskb = sb("causal_mask", [P, P], BF16)
        beforeb = sb("tokens_before", [P, P], BF16)
        onesb = sb("ones", [P, P], BF16)
        tri8 = sb("groups_before", [P, N_GRP, N_GRP])
        pos_i = sb("pos_i", [P, NT], I32)
        pos_f = sb("pos_f", [P, NT])
        n_freq = ROT_D // 2 + ROT_M // 2
        cosT = sb("cos", [P, NT, n_freq])
        sinT = sb("sin", [P, NT, n_freq])
        lam_in = sb("lam_in", [P, 4, QK_D])
        lam_sc = sb("lam_sc", [P, 8])
        gcol = sb("gain_columns", [P, 6])
        half = sb("minus_half", [P, 8])
        spare = sb("spare", [P, 8])
        POWB = sb("rsqrt_io", [P, 64])
        MS = sb("max_sum", [P, 4, 8])
        ST = sb("ln_stats", [P, 2, 6])
        MV = sb("ln_mean_var", [P, 4])
        rbias = sb("router_bias", [P, N_EXP])
        e128 = sb("expert_times_128", [P, N_EXP])
        item_no = sb("item_no", [P, MAX_EXTRA])
        iota_i = sb("iota_i", [P, N_EXP], I32)
        token_id = sb("token_id", [P, NT], U32)
        lists = sb("lists", [P, LIST_COLS], U32)
        idx_col = sb("idx_col", [P, 2], U32)
        pos_u = sb("pos_u", [P, NT * TOP_K], U32)
        spos_u = sb("spos_u", [P, NT * TOP_K], U32)
        gk = sb("gate_of_choice", [P, NT * TOP_K])
        counts_i = sb("counts_i", [P, 3], I32)
        extra_i = sb("extra_experts", [P, MAX_EXTRA], I32)
        selb = sb("selected_bf16", [P, NT, N_EXP], BF16)

        banks = [ctx.enter_context(nc.psum_tensor(f"bank{i}", [P, 512], F32)) for i in range(8)]

        KMT = MKV[:, 0:1024].rearrange("p (h n) -> p h n", h=HD)
        VM = MKV[:, 1024:2048].rearrange("p (m n) -> p m n", m=2)
        RW = MKV[:, 0:512].rearrange("p (c n) -> p c n", c=NC)
        ST64 = MKV[:, 512:832].rearrange("p (i n) -> p i n", i=5)
        R8 = MKV[:, 1024:1408].rearrange("p (i n) -> p i n", i=12)
        WIN = [E[:, n * NC * 512:n * NC * 512 + NC * w].rearrange("p (c n) -> p c n", c=NC)
               for n, w in enumerate((448, 512, 512, 512))]
        MEMX = E[:, 16384:18432].rearrange("p (m d) -> p m d", m=2)
        MEMT = E[:, 18432:20480].rearrange("p (c n) -> p c n", c=NC)
        LNP = E[:, 18432:20480].rearrange("p (g d) -> p g d", g=2)
        WUQ = E[:, 20480:22016].rearrange("p (c n) -> p c n", c=2)
        WUKV = E[:, 22016:23040]
        KP = E[:, 23040:23552].rearrange("p (t n) -> p t n", t=NT)
        TMP = E[:, 23552:24576]
        QDT = E[:, 0:2048].rearrange("p (c n) -> p c n", c=4)
        KDT = E[:, 2048:4096].rearrange("p (c n) -> p c n", c=4)
        QNT = E[:, 4096:6144].rearrange("p (c n) -> p c n", c=4)
        KNT = E[:, 6144:8192].rearrange("p (c n) -> p c n", c=4)
        QPT = E[:, 8192:9216].rearrange("p (c n) -> p c n", c=2)
        KPT = E[:, 9216:9728]
        VML = E[:, 9728:11776].rearrange("p (t n) -> p t n", t=NT)
        WQ = E[:, 0:4096].rearrange("p (c n) -> p c n", c=NC)
        WO2 = E[:, 4096:8192].rearrange("p (c n) -> p c n", c=4)
        QCT = E[:, 8192:10240].rearrange("p (c n) -> p c n", c=4)
        OCT = E[:, 10240:12288].rearrange("p (c n) -> p c n", c=4)
        WK = W[:, 0:4096].rearrange("p (c n) -> p c n", c=NC)
        WV = W[:, 4096:8192].rearrange("p (c n) -> p c n", c=NC)
        WO = W[:, :].rearrange("p (c n) -> p c n", c=NC)
        CQT = AT[:, 0:2, :]
        CKVT = AT[:, 2, :]
        O = AT[:, :, :].rearrange("p c n -> p (c n)").rearrange("p (t d) -> p t d", t=NT)
        PB = [PR[:, i // 2, (i % 2) * 512:(i % 2) * 512 + 512] for i in range(4)]
        PTB = [PR[:, 2, i * 512:i * 512 + 512] for i in range(2)]
        MIXT = PR[:, 3, 0:1024].rearrange("p (c n) -> p c n", c=NC)
        OC = [PR[:, t, 1024:1536] for t in range(NT)]
        PF = PR[:, :, :].rearrange("p t n -> p (t n)")
        XG = [PF[:, i * 1024:i * 1024 + 1024] for i in range(2)]
        XGT = [PF[:, 2048 + i * 1024:3072 + i * 1024].rearrange("p (c n) -> p c n", c=NC) for i in range(2)]
        Y = [PF[:, 4096 + i * 1024:5120 + i * 1024] for i in range(2)]
        HS = [PF[:, 6144 + i * 256:6400 + i * 256] for i in range(2)]
        HT = [PF[:, 6656 + i * 256:6912 + i * 256].rearrange("p (c n) -> p c n", c=2) for i in range(2)]
        SG = [PF[:, 7168 + i * 256:7424 + i * 256] for i in range(2)]
        SEL0 = 6144
        (SC, CH, T1, T2, MC, SELM, POSM, GATE) = [
            W[:, SEL0 + i * 256:SEL0 + i * 256 + 256].rearrange("p (t e) -> p t e", t=NT) for i in range(8)]
        CG = [E[:, i * D:(i + 1) * D] for i in range(8)]
        LN3 = AT[:, 0:4, :].rearrange("p c n -> p (c n)").rearrange("p (g d) -> p g d", g=2)

        def slot_views(flat):
            n = NC * F_EXP
            return (flat[:, 0:2 * n].rearrange("p (g c n) -> p g c n", g=2, c=NC),
                    flat[:, 2 * n:3 * n].rearrange("p (c n) -> p c n", c=2))

        SLOTS = [slot_views(E[:, ((b + 2) % 4) * SLOT:((b + 2) % 4 + 1) * SLOT]) for b in range(UNROLL)]
        SHARED = slot_views(W[:, 0:SLOT])

        x_in = [sem(f"x_in{t}") for t in range(NT)]
        win_in = [sem(f"w_in_block{n}") for n in range(4)]
        mem_in, wkv_in, lat_in, wo_in = sem("mem_in"), sem("wkv_in"), sem("lat_in"), sem("wo_in")
        small_in, ln1_in, ln2_in, ln3_in = sem("small_in"), sem("ln1_in"), sem("ln2_in"), sem("ln3_in")
        wq_in, wo2_in, sh_in, rw_in = sem("wq_in"), sem("wo2_in"), sem("shared_in"), sem("router_in")
        slot_in = [sem(f"slot_in{b}") for b in range(UNROLL)]
        const_ready, pool_step = sem("const_ready"), sem("pool_step")
        dve_step, act_step = sem("dve_step"), sem("act_step")
        range_ready, trig_ready, lam_dots, lam_exps, lam_ready = (
            sem("range_ready"), sem("trig_ready"), sem("lam_dots"), sem("lam_exps"), sem("lam_ready"))
        gains_ready = sem("gains_ready")
        pow_asked, pow_done = sem("pow_asked"), sem("pow_done")
        grp_done, grp_act, grp_dve = sem("group_done"), sem("group_copied_act"), sem("group_copied_dve")
        lat_normed, kp_ready, rope_ready, qp_ready = (
            sem("lat_normed"), sem("k_pe_ready"), sem("rope_ready"), sem("q_pe_ready"))
        scores_done, negmax_ready, exp_done, mixed_p = (
            sem("scores_done"), sem("negmax_ready"), sem("exp_done"), sem("mixed_p"))
        pt_done, pt_copied, o_done, o_copied = sem("pt_done"), sem("pt_copied"), sem("o_done"), sem("o_copied")
        o_normed, mixt_done, mixt_copied = sem("o_normed"), sem("mixt_done"), sem("mixt_copied")
        res_done, ln_done = sem("out_proj_done"), sem("ln_done")
        h_done, h_act, h_dve = sem("hT_done"), sem("hT_copied_act"), sem("hT_copied_dve")
        qc_done, qc_act = sem("qc_done"), sem("qc_copied")
        h2_stored = sem("h2_stored")
        logits_done, sig_done, sel_ready, rank_done = (
            sem("logits_done"), sem("sigmoid_done"), sem("selection_ready"), sem("rank_done"))
        spos_ready, counts_ready, list_filled, listed, lists_in = (
            sem("list_places_ready"), sem("counts_ready"), sem("list_filled"), sem("listed"), sem("lists_in"))
        kp_rotated = sem("k_pe_rotated")
        gu_done, silu_done, h_ready, ht_done, ht_copied, down_done = (
            sem("gate_up_done"), sem("silu_done"), sem("h_ready"), sem("h_transposed"), sem("ht_copied"),
            sem("down_done"))
        sh_added = sem("shared_added")
        xg_in = [sem("xg_in0"), sem("xg_in1")]
        xg_zero = sem("xg_zeroed")
        xt_done, xt_act, xt_dve = sem("xg_transposed"), sem("xgt_copied_act"), sem("xgt_copied_dve")
        y_act, y_dve = sem("y_copied_act"), sem("y_copied_dve")
        y_free = [sem("y_free0"), sem("y_free1")]
        idx_ready, rows_zeroed = sem("idx_ready"), sem("rows_zeroed")
        cg_in = [sem(f"choice_in{i}") for i in range(8)]
        cg_used, out_stored = sem("choice_used"), sem("out_stored")

        FRONT = ([("xT", t, h) for t in range(NT) for h in range(2)]
                 + [("proj", n, t) for n in range(4) for t in range(NT)]
                 + [("cqT", 0), ("cqT", 1), ("ckvT",), ("kpT",)]
                 + [("qkT", c) for c in range(8)]
                 + [("memT", m, h) for m in range(2) for h in range(2)]
                 + [("kmem", i) for i in range(2)] + [("vmem", m) for m in range(2)]
                 + [("qn", h) for h in range(HD)] + [("kn", h) for h in range(HD)]
                 + [("vm", t) for t in range(NT)] + [("qp", t) for t in range(NT)]
                 + [("qpT", 0), ("qpT", 1)])
        AT_GROUP = {g: j for j, g in enumerate(FRONT)}

        def on_dve(j):
            return j % 2 == 1 or FRONT[j][0] in ("qp", "cqT")

        def copied(eng, j):
            same = on_dve(j)
            n = sum(on_dve(i) == same for i in range(j + 1))
            eng.wait_ge(grp_dve if same else grp_act, n)

        POW, at = {}, 0
        for name in ([("lat", t) for t in range(NT)]
                     + [(n, t) for t in range(NT) for n in ("mix", "ln1")]
                     + [("ln2", t) for t in range(NT)] + [("ln3", t) for t in range(NT)]):
            width = {"lat": 2, "mix": 8}.get(name[0], 1)
            POW[name] = (len(POW), at, width)
            at += width

        def power(name):
            n, c, w = POW[name]
            return n, POWB[:, c:c + w]

        MIX_UNITS = [(k, t, h) for t in range(NT) for k in "dm" for h in range(HD)]
        MEM_UNITS = [("x", t, h) for t in range(NT) for h in range(HD)]
        UNITS = MIX_UNITS + MEM_UNITS
        STEP0, s = [], 0
        for kind, _, _ in UNITS:
            STEP0.append(s)
            s += 2 if kind == "d" else 1
        UNIT_OF_STEP = [u for u, (k, _, _) in enumerate(UNITS) for _ in range(2 if k == "d" else 1)]

        def steps(u):
            return range(STEP0[u], STEP0[u] + (2 if UNITS[u][0] == "d" else 1))

        def keys(u):
            kind, t, _ = UNITS[u]
            return N_MEM if kind == "x" else (t + 1) * P

        MIX_HOOKS = {8 * t + 9: ("mixT", t) for t in range(NT)}
        MIX_HOOKS.update({8 * t + 11: ("out", t) for t in range(NT)})
        MEM_HOOKS = {32 + 4 * t + 4: ("mixT", t) for t in range(NT)}
        MEM_HOOKS.update({32 + 4 * t + 5: ("out", t) for t in range(NT)})

        def pipeline(first, last, hooks, ahead, middle, behind, hook):
            ahead(first)
            for u in range(first, last + 1):
                if u + 1 < last:
                    ahead(u + 1)
                if u < last:
                    middle(u)
                if u > first:
                    behind(u - 1)
                if u in hooks and u <= last - 1:
                    hook(*hooks[u])
            for k in sorted(hooks):
                if k > last - 1:
                    hook(*hooks[k])

        def front_dest(eng, j, copy):
            g = FRONT[j]
            bank = banks[j % 8]
            four = bank[:, :].rearrange("p (c n) -> p c n", c=4)
            if g[0] == "xT":
                copy(AT[:, 4 * g[2]:4 * g[2] + 4, g[1] * P:(g[1] + 1) * P], four, None)
            elif g[0] == "proj":
                c0, w = [(LAT, 448), (0, 512), (512, 512), (1024, 512)][g[1]]
                copy(PR[:, g[2], c0:c0 + w], bank[:, 0:w], None)
            elif g[0] == "cqT":
                copy(CQT[:, g[1], :], bank[:, :], gcol[:, g[1]:g[1] + 1])
            elif g[0] == "ckvT":
                copy(CKVT, bank[:, :], gcol[:, 2:3])
            elif g[0] == "kpT":
                copy(KPT, bank[:, :], None)
            elif g[0] == "qkT":
                copy((QDT if g[1] < 4 else KDT)[:, g[1] % 4, :], bank[:, :], None)
            elif g[0] == "memT":
                copy(MEMT[:, 4 * g[2]:4 * g[2] + 4, g[1] * P:(g[1] + 1) * P], four, None)
            elif g[0] == "kmem":
                copy(KMT[:, 2 * g[1]:2 * g[1] + 2, :], bank[:, :].rearrange("p (h n) -> p h n", h=2), None)
            elif g[0] == "vmem":
                copy(VM[:, g[1], :], bank[:, :], None)
            elif g[0] == "qn":
                copy(QNT[:, g[1], :], bank[:, :], None)
            elif g[0] == "kn":
                copy(KNT[:, g[1], :], bank[:, :], None)
            elif g[0] == "vm":
                copy(VML[:, g[1], :], bank[:, :], None)
            elif g[0] == "qpT":
                copy(QPT[:, g[1], :], bank[:, :], None)

        block = ctx.enter_context(nc.Block())

        def expert_weights(eng, b, e):
            gu, dn = SLOTS[b]
            for g, w in enumerate((exp_w_gate, exp_w_up)):
                eng.dma_start(gu[:, g, :, :], w[0, e, :, :].rearrange("(p c) n -> p c n", c=NC)
                              ).then_inc(slot_in[b], 16)
            eng.dma_start(dn[:, :, :], exp_w_down[0, e, :, :].rearrange("(p c) n -> p c n", c=2)
                          ).then_inc(slot_in[b], 16)

        @block.sync
        def _(sp):
            sp.dma_start(X[:, 0, :], x[0, 0:P, :]).then_inc(x_in[0], 16)
            blocks = [(LAT, 448), (0, 512), (512, 512), (1024, 512)]
            for n, (c0, w) in enumerate(blocks):
                sp.dma_start(WIN[n][:, :, :], w_in[0, :, c0:c0 + w].rearrange("(p c) n -> p c n", c=NC)
                             ).then_inc(win_in[n], 16)
                if n == 0:
                    for t in range(1, NT):
                        sp.dma_start(X[:, t, :], x[0, t * P:(t + 1) * P, :]).then_inc(x_in[t], 16)
            sp.dma_start(MEMX, mem[0, :, :].rearrange("(m p) d -> p m d", p=P)).then_inc(mem_in, 16)
            for w, dst in ((mem_w_k, WK), (mem_w_v, WV)):
                sp.dma_start(dst, w[0, :, :].rearrange("(p c) n -> p c n", c=NC)).then_inc(wkv_in, 16)
            sp.dma_start(WUQ, mla_w_uq[0, :, :].rearrange("(c p) n -> p c n", c=2)).then_inc(lat_in, 16)
            sp.dma_start(WUKV, mla_w_ukv[0, :, :]).then_inc(lat_in, 16)
            sp.wait_ge(grp_done, AT_GROUP[("vmem", 1)] + 1)
            sp.dma_start(WO, w_o[0, :, :].rearrange("(c p) n -> p c n", c=NC)).then_inc(wo_in, 16)
            for i, g in enumerate((ln1_g, ln1_b)):
                sp.dma_start(LNP[:, i, :], g[0:1, :].partition_broadcast(P)).then_inc(ln1_in, 16)
            expert_weights(sp, 0, 0)
            sp.wait_ge(o_done, len(MIX_UNITS))
            sp.dma_start(WQ, mem_w_q[0, :, :].rearrange("(p c) n -> p c n", c=NC)).then_inc(wq_in, 16)
            sp.dma_start(WO2, mem_w_o[0, :, :].rearrange("(c p) n -> p c n", c=4)).then_inc(wo2_in, 16)
            sp.wait_ge(res_done, 2 * NT)
            for g, w in enumerate((sh_w_gate, sh_w_up)):
                sp.dma_start(SHARED[0][:, g, :, :], w[0, :, :].rearrange("(p c) n -> p c n", c=NC)
                             ).then_inc(sh_in, 16)
            sp.dma_start(SHARED[1], sh_w_down[0, :, :].rearrange("(p c) n -> p c n", c=2)).then_inc(sh_in, 16)
            sp.wait_ge(ln_done, NT)
            for i, g in enumerate((ln2_g, ln2_b)):
                sp.dma_start(LNP[:, i, :], g[0:1, :].partition_broadcast(P)).then_inc(ln2_in, 16)
            sp.wait_ge(o_done, len(UNITS))
            sp.dma_start(RW[:, :, :], router_w[0, :, :].rearrange("(p c) n -> p c n", c=NC)).then_inc(rw_in, 16)
            sp.wait_ge(res_done, 4 * NT)
            expert_weights(sp, 2, 2)
            expert_weights(sp, 3, 3)
            sp.wait_ge(ln_done, 2 * NT)
            expert_weights(sp, 1, 1)

            def store(i, b):
                sp.wait_ge(y_act, i + 2)
                sp.wait_ge(y_dve, i + 2)
                sp.dma_start(y_rows.rearrange("(i p) d -> i p d", p=P)[bass.ds(i, 1), :, :]
                             .rearrange("i p d -> (i p) d"), Y[b % 2]).then_inc(y_free[b % 2], 16)

            n_body = N_EXP // UNROLL
            with sp.Fori(0, n_body - 1) as it:
                for b in range(UNROLL):
                    sp.wait_ge(down_done, it * UNROLL + (b + NT + 1))
                    gu, dn = SLOTS[b]
                    e = bass.ds(it * UNROLL + (b + UNROLL), 1)
                    for g, w in enumerate((exp_w_gate, exp_w_up)):
                        sp.dma_start(gu[:, g, :, :], w[0, e, :, :].rearrange("e (p c) n -> (e p) c n", c=NC)
                                     ).then_inc(slot_in[b], 16)
                    sp.dma_start(dn[:, :, :], exp_w_down[0, e, :, :].rearrange("e (p c) n -> (e p) c n", c=2)
                                 ).then_inc(slot_in[b], 16)
                    store(it * UNROLL + b, b)
            sp.wait_ge(counts_ready, 1)
            last = sp.value_load(counts_i[0:1, 2:3], min_val=n_body - 1, max_val=MAX_ITEMS // UNROLL - 1)
            with sp.If(last > n_body - 1):
                sp.wait_ge(rows_zeroed, 16)
                with sp.Fori(n_body - 1, last) as it:
                    for b in range(UNROLL):
                        sp.wait_ge(down_done, it * UNROLL + (b + NT + 1))
                        ex = sp.value_load(extra_i[0:1, bass.ds(it * UNROLL + (b + UNROLL - N_EXP), 1)],
                                           min_val=0, max_val=N_EXP - 1)
                        gu, dn = SLOTS[b]
                        e = bass.ds(ex, 1)
                        for g, w in enumerate((exp_w_gate, exp_w_up)):
                            sp.dma_start(gu[:, g, :, :], w[0, e, :, :].rearrange("e (p c) n -> (e p) c n", c=NC)
                                         ).then_inc(slot_in[b], 16)
                        sp.dma_start(dn[:, :, :], exp_w_down[0, e, :, :].rearrange("e (p c) n -> (e p) c n", c=2)
                                     ).then_inc(slot_in[b], 16)
                        store(it * UNROLL + b, b)
            for b in range(UNROLL):
                store(last * UNROLL + b, b)
            for t in range(NT):
                sp.wait_ge(ln_done, 2 * NT + t + 1)
                sp.dma_start(out[0, t * P:(t + 1) * P, :], X[:, t, :]).then_inc(out_stored, 16)
            sp.wait_ge(out_stored, 16 * NT)

        @block.gpsimd
        def _(pool):
            step = Chain(pool, pool_step)
            step(pool.memset(ident[:, :], 0.0))
            step(pool.affine_select(out=ident[:, :], in_=ident[:, :], compare_op=ALU.not_equal, fill=1.0,
                                    base=0, pattern=[[-1, P]], channel_multiplier=1))
            pool.memset(half[:, :], -0.5).then_inc(const_ready, 1)
            step(pool.memset(identb[:, :], 0.0))
            step(pool.affine_select(out=identb[:, :], in_=identb[:, :], compare_op=ALU.not_equal, fill=1.0,
                                    base=0, pattern=[[-1, P]], channel_multiplier=1))
            step(pool.memset(maskb[:, :], 0.0))
            step(pool.affine_select(out=maskb[:, :], in_=maskb[:, :], compare_op=ALU.is_ge, fill=-1e30,
                                    base=0, pattern=[[-1, P]], channel_multiplier=1))
            step(pool.memset(beforeb[:, :], 1.0))
            step(pool.affine_select(out=beforeb[:, :], in_=beforeb[:, :], compare_op=ALU.is_gt, fill=0.0,
                                    base=0, pattern=[[1, P]], channel_multiplier=-1))
            step(pool.memset(onesb[:, :], 1.0))
            step(pool.memset(tri8[:, :, :], 1.0))
            step(pool.affine_select(out=tri8[:, :, :], in_=tri8[:, :, :], compare_op=ALU.is_gt, fill=0.0,
                                    base=0, pattern=[[1, N_GRP], [-1, N_GRP]], channel_multiplier=0))
            step(pool.iota(iota_i[:, 0:N_EXP], pattern=[[P, N_EXP]], base=0, channel_multiplier=0))
            step(pool.tensor_copy(e128[:, :], iota_i[:, 0:N_EXP]))
            step(pool.iota(iota_i[:, 0:MAX_EXTRA], pattern=[[1, MAX_EXTRA]], base=0, channel_multiplier=0))
            step(pool.tensor_copy(item_no[:, :], iota_i[:, 0:MAX_EXTRA]))
            step(pool.iota(token_id[:, :], pattern=[[P, NT]], base=0, channel_multiplier=1))
            step(pool.memset(lists[:, :], NO_TOKEN))
            pool.nop().then_inc(const_ready, 1)
            pool.dma_start(token_list.rearrange("(p c) o -> p (c o)", p=P), lists[:, :]).then_inc(list_filled, 16)

            def powers(names):
                for name in names:
                    n, cols = power(name)
                    pool.wait_ge(pow_asked, n + 1)
                    pool.tensor_tensor(cols, cols, half[:, 0:cols.shape[1]], ALU.pow).then_inc(pow_done, 1)

            powers([k for k in POW if k[0] in ("lat", "mix", "ln1")])
            for t in range(NT):
                powers([("ln2", t)])
                pool.wait_ge(ln_done, NT + t + 1)
                pool.dma_start(h2_rows[t * P:(t + 1) * P, :], X[:, t, :]).then_inc(h2_stored, 16)
            pool.wait_ge(res_done, 4 * NT)
            for i in range(2):
                pool.memset(XG[i], 0.0).then_inc(xg_zero, 1)
            for i in range(2):
                pool.memset(Y[i], 0.0).then_inc(y_free[i], 16)
            pool.wait_ge(list_filled, 16)
            pool.wait_ge(spos_ready, 1)
            for j in range(NT * TOP_K):
                pool.indirect_dma_start(
                    out=token_list, out_offset=bass.IndirectOffsetOnAxis(ap=spos_u[:, j:j + 1], axis=0),
                    in_=token_id[:, j // TOP_K:j // TOP_K + 1], in_offset=None,
                    bounds_check=P * LIST_COLS - 1, oob_is_err=False).then_inc(listed, 16)
            pool.wait_ge(listed, 16 * NT * TOP_K)
            pool.dma_start(lists[:, :], token_list.rearrange("(p c) o -> p (c o)", p=P)).then_inc(lists_in, 16)
            pool.wait_ge(lists_in, 16)
            pool.wait_ge(h2_stored, 16 * NT)

            def gather(i, b):
                p = b % 2
                pool.tensor_copy(idx_col[:, p:p + 1], lists[:, bass.ds(i, 1)]).then_inc(idx_ready, 1)
                pool.wait_ge(idx_ready, 1)
                pool.sem_clear(idx_ready)
                pool.indirect_dma_start(
                    out=XG[p], out_offset=None, in_=h2_rows,
                    in_offset=bass.IndirectOffsetOnAxis(ap=idx_col[:, p:p + 1], axis=0),
                    bounds_check=last_token, oob_is_err=False).then_inc(xg_in[p], 16)

            n_body = N_EXP // UNROLL
            last_token = pool.to_reg(SEQ - 1)
            last_row = pool.to_reg(MAX_ITEMS * P - 1)
            pool.wait_ge(xg_zero, 2)
            pool.wait_ge(counts_ready, 1)
            last = pool.value_load(counts_i[0:1, 2:3], min_val=n_body - 1, max_val=MAX_ITEMS // UNROLL - 1)
            with pool.If(last > n_body - 1):
                pool.dma_start(y_rows[N_EXP * P:, :].rearrange("(i p) d -> p i d", p=P),
                               XG[0].unsqueeze(1).to_broadcast([P, MAX_EXTRA, D])).then_inc(rows_zeroed, 16)
                pool.wait_ge(rows_zeroed, 16)
            gather(0, 0)
            gather(1, 1)
            n_iter = pool.value_load(counts_i[0:1, 1:2], min_val=n_body, max_val=MAX_ITEMS // UNROLL)
            with pool.Fori(0, n_iter) as it:
                for b in range(UNROLL):
                    pool.wait_ge(xt_done, it * UNROLL + (b + 1))
                    gather(it * UNROLL + (b + 2), b)
            for p in range(2):
                pool.wait_ge(xg_in[p], n_iter * 32 + 16)
            for p in range(2):
                pool.wait_ge(y_free[p], n_iter * 32 + 16)
            pool.tensor_tensor(spare[:, :], half[:, :], half[:, :], ALU.add).then_inc(pool_step, 1)
            pool.wait_ge(pool_step, step.n + 1)

            def take_choices(rows):
                for j in range(NT * TOP_K):
                    if j >= 8:
                        pool.wait_ge(cg_used, j - 7)
                    pool.indirect_dma_start(
                        out=CG[j % 8], out_offset=None, in_=rows,
                        in_offset=bass.IndirectOffsetOnAxis(ap=pos_u[:, j:j + 1], axis=0),
                        bounds_check=last_row, oob_is_err=False).then_inc(cg_in[j % 8], 16)
                    if j % TOP_K == TOP_K - 1 and j > TOP_K:
                        powers([("ln3", j // TOP_K - 1)])
                powers([("ln3", NT - 1)])

            with pool.If(last > n_body - 1):
                take_choices(y_rows)
            with pool.Else():
                take_choices(y_rows[0:N_EXP * P, :])

        @block.scalar
        def _(act):
            with nc.allow_non_contiguous_dma(reason="a few hundred words"):
                act.dma_start(pos_i[:, :], positions[0, :].rearrange("(t p) -> p t", p=P)).then_inc(small_in, 16)
                for i, v in enumerate((lam_q1, lam_k1, lam_q2, lam_k2)):
                    act.dma_start(lam_in[:, i, :], v[0:1, :].partition_broadcast(P)).then_inc(small_in, 16)
                act.dma_start(gcol[:, 0:2], mla_q_norm_g[0, :].rearrange("(c p) -> p c", p=P)).then_inc(small_in, 16)
                for i, v in enumerate((mla_kv_norm_g, diff_subln_g, mla_out_norm_g)):
                    act.dma_start(gcol[:, 2 + i:3 + i], v[0, :].rearrange("(p c) -> p c", c=1)).then_inc(small_in, 16)
            act.dma_start(rbias[:, :], router_bias[0:1, :].partition_broadcast(P)).then_inc(small_in, 16)

            def copy(dst, src, s, scale=1.0):
                act.activation(dst, src, ACT.Copy, scale=scale).then_inc(s, 1)

            def drain_group(j):
                act.wait_ge(grp_done, j + 1)
                front_dest(act, j, lambda dst, src, g: copy(dst, src, grp_act, 1.0 if g is None else g))

            def lam():
                act.wait_ge(lam_dots, 1)
                act.activation(lam_sc[:, 2:4], lam_sc[:, 0:2], ACT.Exp).then_inc(lam_exps, 1)

            for j in range(len(FRONT)):
                if not on_dve(j):
                    drain_group(j)
                if FRONT[j] == ("proj", 0, 0):
                    act.wait_ge(range_ready, 1)
                    act.activation(sinT[:, :, :], sinT[:, :, :], ACT.Sin).then_inc(trig_ready, 1)
                    act.activation(cosT[:, :, :], cosT[:, :, :], ACT.Sin).then_inc(trig_ready, 1)
                    lam()

            def exps(u):
                kind = UNITS[u][0]
                n = keys(u)
                scale = {"d": SCALE_D, "m": SCALE_M, "x": SCALE_X}[kind]
                for s in steps(u):
                    act.wait_ge(negmax_ready, s + 1)
                    if s >= 4:
                        act.wait_ge(pt_done, UNIT_OF_STEP[s - 4] + 1)
                    act.activation(PB[s % 4][:, 0:n], banks[s % 3][:, 0:n], ACT.Exp,
                                   bias=MS[:, 1, s % 8:s % 8 + 1], scale=scale,
                                   accum_out=MS[:, 2, s % 8:s % 8 + 1]).then_inc(exp_done, 1)

            def pt_copy(u):
                act.wait_ge(pt_done, u + 1)
                if u >= 2:
                    act.wait_ge(o_done, u - 1)
                copy(PTB[u % 2][:, 0:keys(u)], banks[3 + u % 2][:, 0:keys(u)], pt_copied)

            def mix_hook(what, t):
                if what == "mixT":
                    for g in range(2):
                        act.wait_ge(mixt_done, 2 * t + g + 1)
                        if t >= 1 and g == 0:
                            act.wait_ge(res_done, 2 * t)
                        copy(MIXT[:, 4 * g:4 * g + 4, :], banks[6 + g][:, :].rearrange("p (c n) -> p c n", c=4),
                             mixt_copied, gcol[:, 5 - g:6 - g])

            def mem_hook(what, t):
                if what == "mixT":
                    act.wait_ge(mixt_done, 2 * NT + t + 1)
                    copy(OCT[:, :, t * P:(t + 1) * P], banks[6 + t % 2][:, :].rearrange("p (c n) -> p c n", c=4),
                         mixt_copied)

            act.wait_ge(gains_ready, 1)
            nm, nx = len(MIX_UNITS), len(UNITS)
            pipeline(0, nm, MIX_HOOKS, exps, pt_copy, lambda u: None, mix_hook)

            def h_copy(first, t):
                act.wait_ge(h_done, 2 * (first + t) + 1)
                copy(AT[:, 0:4, t * P:(t + 1) * P], banks[0 + 2 * (t % 2)][:, :].rearrange("p (c n) -> p c n", c=4), h_act)

            for t in range(NT):
                h_copy(0, t)
            for h in range(HD):
                act.wait_ge(qc_done, h + 1)
                copy(QCT[:, h, :], banks[4 + h][:, :], qc_act)
            pipeline(nm, nx, MEM_HOOKS, exps, pt_copy, lambda u: None, mem_hook)
            for i, g in enumerate((0, 1)):
                pass
            for t in range(NT):
                h_copy(NT, t)
            act.wait_ge(logits_done, 1)
            act.activation(SC[:, :, :], banks[4][:, 0:NT * N_EXP].rearrange("p (t e) -> p t e", t=NT),
                           ACT.Sigmoid).then_inc(sig_done, 1)

            def silu(q, b):
                act.wait_ge(gu_done, q + 1)
                if not isinstance(q, int) or q >= 2:
                    act.wait_ge(h_ready, q + -1)
                act.activation(SG[b % 2], banks[b % 2][:, 0:F_EXP], ACT.Silu).then_inc(silu_done, 1)

            def ht_copy(q, b):
                act.wait_ge(ht_done, q + 1)
                if not isinstance(q, int) or q >= 2:
                    act.wait_ge(down_done, q + -1)
                copy(HT[b % 2], banks[7][:, 0:256].rearrange("p (c n) -> p c n", c=2), ht_copied)

            def xgt_copy(i, b):
                act.wait_ge(xt_done, i + 1)
                act.wait_ge(gu_done, i + 3)
                copy(XGT[b % 2][:, 0:4, :], banks[2][:, :].rearrange("p (c n) -> p c n", c=4), xt_act)

            def y_copy(it, b):
                i = it * UNROLL + b
                act.wait_ge(down_done, i + (NT + 1))
                act.wait_ge(y_free[b % 2], it * 32 + 16 * (b // 2 + 1))
                copy(Y[b % 2][:, 0:512], banks[4][:, :], y_act)

            act.wait_ge(sh_in, 48)
            for q in range(NT):
                silu(q, q)
                if q:
                    ht_copy(q - 1, q - 1)
            xgt_copy(0, 0)
            ht_copy(NT - 1, NT - 1)
            act.wait_ge(gu_done, NT)
            for i, g in enumerate((ln3_g, ln3_b)):
                act.dma_start(LN3[:, i, :], g[0:1, :].partition_broadcast(P)).then_inc(ln3_in, 16)
            act.wait_ge(counts_ready, 1)
            n_iter = act.value_load(counts_i[0:1, 1:2], min_val=N_EXP // UNROLL, max_val=MAX_ITEMS // UNROLL)
            with act.Fori(0, n_iter) as it:
                for b in range(UNROLL):
                    i = it * UNROLL + b
                    silu(it * UNROLL + (b + NT), b)
                    if b:
                        ht_copy(it * UNROLL + (b + NT - 1), b - 1)
                    xgt_copy(it * UNROLL + (b + 1), b + 1)
                    if b:
                        y_copy(it, b - 1)
                ht_copy(it * UNROLL + (2 * NT - 1), UNROLL - 1)
                y_copy(it, UNROLL - 1)

        @block.vector
        def _(dve):
            step = Chain(dve, dve_step)

            def drain_group(j):
                dve.wait_ge(grp_done, j + 1)

                def copy(dst, src, gain):
                    if gain is None:
                        dve.tensor_copy(dst, src).then_inc(grp_dve, 1)
                    else:
                        dve.tensor_scalar(dst, src, gain, None, ALU.mult).then_inc(grp_dve, 1)
                front_dest(dve, j, copy)

            def trig_ranges():
                dve.wait_ge(small_in, 16 * 10)
                step(dve.tensor_copy(pos_f[:, :], pos_i[:, :]))
                freqs = [np.float32(THETA ** (-i / n)) for n in (ROT_D, ROT_M) for i in range(0, n, 2)]
                for j, f in enumerate(freqs):
                    last = dve.tensor_scalar(sinT[:, :, j], pos_f[:, :], float(f), None, ALU.mult)
                    last.then_inc(dve_step, 1)
                    step.n += 1
                dve.wait_ge(dve_step, step.n)
                magic = 1.5 * 2.0 ** 23
                turns = TMP[:, 0:NT * n_freq].rearrange("p (t j) -> p t j", t=NT)
                step(dve.tensor_scalar(turns, sinT[:, :, :], 1.0 / (2 * math.pi), magic, ALU.mult, ALU.add))
                step(dve.tensor_scalar(turns, turns, magic, None, ALU.subtract))
                c1 = 6.28125
                c2 = float(np.float32(2 * math.pi - c1).view(np.uint32) & np.uint32(0xFFFFF000))
                c2 = float(np.uint32(int(c2)).view(np.float32))
                c3 = 2 * math.pi - c1 - c2
                for c in (c1, c2, c3):
                    step(dve.scalar_tensor_tensor(sinT[:, :, :], turns, -c, sinT[:, :, :], ALU.mult, ALU.add))
                top = 3.1415925
                step(dve.tensor_scalar(sinT[:, :, :], sinT[:, :, :], top, -top, ALU.min, ALU.max))
                step(dve.tensor_scalar(cosT[:, :, :], sinT[:, :, :], -1.0, None, ALU.mult))
                step(dve.tensor_tensor(cosT[:, :, :], cosT[:, :, :], sinT[:, :, :], ALU.min))
                dve.tensor_scalar(cosT[:, :, :], cosT[:, :, :], math.pi / 2, None, ALU.add).then_inc(range_ready, 1)

            def lam_products():
                for i in range(2):
                    step(dve.tensor_tensor_reduce(out=TMP[:, 256:256 + QK_D], in0=lam_in[:, 2 * i, :],
                                                  in1=lam_in[:, 2 * i + 1, :], scale=1.0, scalar=0.0,
                                                  op0=ALU.mult, op1=ALU.add, accum_out=lam_sc[:, i:i + 1]))
                dve.nop().then_inc(lam_dots, 1)

            def lam_final():
                dve.wait_ge(lam_exps, 1)
                step(dve.tensor_tensor(lam_sc[:, 4:5], lam_sc[:, 3:4], lam_sc[:, 2:3], ALU.subtract))
                step(dve.tensor_scalar(lam_sc[:, 5:6], lam_sc[:, 4:5], -LAM_INIT, None, ALU.add))
                dve.tensor_scalar(gcol[:, 5:6], gcol[:, 3:4], 1.0 - LAM_INIT, None, ALU.mult).then_inc(gains_ready, 1)

            def rsqrt(name):
                n, cols = power(name)
                dve.wait_ge(pow_done, n + 1)
                return cols

            def latent_norms():
                for t in range(NT):
                    copied(dve, AT_GROUP[("proj", 0, t)])
                    n, cols = power(("lat", t))
                    for i, (c0, w) in enumerate(((LAT, 256), (LAT + 256, 128))):
                        v = PR[:, t, c0:c0 + w]
                        step(dve.tensor_tensor_reduce(out=TMP[:, 0:w], in0=v, in1=v, scale=1.0 / w, scalar=RMS_EPS,
                                                      op0=ALU.mult, op1=ALU.add, accum_out=cols[:, i:i + 1]))
                    dve.nop().then_inc(pow_asked, 1)
                for t in range(NT):
                    cols = rsqrt(("lat", t))
                    for i, (c0, w) in enumerate(((LAT, 256), (LAT + 256, 128))):
                        v = PR[:, t, c0:c0 + w]
                        dve.tensor_scalar(v, v, cols[:, i:i + 1], None, ALU.mult).then_inc(lat_normed, 1)

            def rotate(a, b, cos, sin, t1, t2, t3, outa, outb, s):
                step(dve.tensor_tensor(t1, a, cos, ALU.mult))
                step(dve.tensor_tensor(t2, b, sin, ALU.mult))
                step(dve.tensor_tensor(t3, a, sin, ALU.mult))
                step(dve.tensor_tensor(outa, t1, t2, ALU.subtract))
                step(dve.tensor_tensor(t1, b, cos, ALU.mult))
                last = dve.tensor_tensor(outb, t1, t3, ALU.add)
                step.tell(last, *s)

            def temps(shape, *names):
                size = math.prod(shape)
                return [TMP[:, i * size:(i + 1) * size] for i in range(3)]

            def key_rotation():
                dve.wait_ge(trig_ready, 2)
                cos, sin = cosT[:, :, 8:40], sinT[:, :, 8:40]
                t1, t2, t3 = [v.rearrange("p (t j) -> p t j", t=NT) for v in temps((NT, 32))]
                a, b = PR[:, :, 1920:1952], PR[:, :, 1952:1984]
                rotate(a, b, cos, sin, t1, t2, t3, KP[:, :, 0:32], KP[:, :, 32:64],
                       (kp_rotated, 1))
                dve.tensor_copy(KP[:, :, 64:128], KP[:, :, 0:64]).then_inc(kp_ready, 1)

            def head_rotation():
                for t in range(NT):
                    for n in (1, 2):
                        copied(dve, AT_GROUP[("proj", n, t)])
                    v = PR[:, t, 0:1024].rearrange("p (h n) -> p h n", n=QK_D)
                    cos = cosT[:, t, 0:8].unsqueeze(1).to_broadcast([P, 16, 8])
                    sin = sinT[:, t, 0:8].unsqueeze(1).to_broadcast([P, 16, 8])
                    t1, t2, t3 = [w.rearrange("p (h j) -> p h j", j=8) for w in temps((16, 8))]
                    rotate(v[:, :, 0:8], v[:, :, 8:16], cos, sin, t1, t2, t3, v[:, :, 0:8], v[:, :, 8:16],
                           (rope_ready, t + 1))

            def query_rotation(t, j):
                dve.wait_ge(grp_done, j + 1)
                v = banks[j % 8][:, 0:HD * ROPE].rearrange("p (h n) -> p h n", n=ROPE)
                o = PR[:, t, LAT:LAT + HD * ROPE].rearrange("p (h n) -> p h n", n=ROPE)
                cos = cosT[:, t, 8:40].unsqueeze(1).to_broadcast([P, HD, 32])
                sin = sinT[:, t, 8:40].unsqueeze(1).to_broadcast([P, HD, 32])
                t1, t2, t3 = [w.rearrange("p (h j) -> p h j", j=32) for w in temps((HD, 32))]
                rotate(v[:, :, 0:32], v[:, :, 32:64], cos, sin, t1, t2, t3, o[:, :, 0:32], o[:, :, 32:64],
                       (grp_dve, sum(map(on_dve, range(j + 1)))))

            for j in range(len(FRONT)):
                if FRONT[j][0] == "qp":
                    query_rotation(FRONT[j][1], j)
                elif on_dve(j):
                    drain_group(j)
                if FRONT[j] == ("proj", 0, 1):
                    trig_ranges()
                    lam_products()
                if FRONT[j] == ("proj", 0, 3):
                    lam_final()
                    latent_norms()
                    key_rotation()
                if FRONT[j] == ("proj", 3, 1):
                    head_rotation()

            def maxima(u):
                kind = UNITS[u][0]
                scale = {"d": SCALE_D, "m": SCALE_M, "x": SCALE_X}[kind]
                for s in steps(u):
                    c = slice(s % 8, s % 8 + 1)
                    dve.wait_ge(scores_done, s + 1)
                    step(dve.reduce_max(MS[:, 0, c], banks[s % 3][:, 0:keys(u)], AX.X))
                    dve.tensor_scalar(MS[:, 1, c], MS[:, 0, c], -scale, None, ALU.mult).then_inc(negmax_ready, 1)

            def probabilities(u):
                s0 = STEP0[u]
                c0 = slice(s0 % 8, s0 % 8 + 1)
                if UNITS[u][0] != "d":
                    dve.wait_ge(exp_done, s0 + 1)
                    dve.reciprocal(MS[:, 3, c0], MS[:, 2, c0]).then_inc(mixed_p, 1)
                    return
                c1 = slice((s0 + 1) % 8, (s0 + 1) % 8 + 1)
                n = keys(u)
                dve.wait_ge(exp_done, s0 + 2)
                step(dve.reciprocal(MS[:, 3, c0], MS[:, 2, c0]))
                step(dve.reciprocal(MS[:, 3, c1], MS[:, 2, c1]))
                step(dve.tensor_scalar(PB[(s0 + 1) % 4][:, 0:n], PB[(s0 + 1) % 4][:, 0:n], MS[:, 3, c1],
                                       lam_sc[:, 5:6], ALU.mult, ALU.mult))
                dve.scalar_tensor_tensor(PB[s0 % 4][:, 0:n], PB[s0 % 4][:, 0:n], MS[:, 3, c0],
                                         PB[(s0 + 1) % 4][:, 0:n], ALU.mult, ALU.add).then_inc(mixed_p, 1)

            def values(u):
                kind, t, h = UNITS[u]
                o = banks[5][:, 0:P]
                s0 = STEP0[u]
                r = MS[:, 3, s0 % 8:s0 % 8 + 1]
                dve.wait_ge(o_done, u + 1)
                if kind == "x":
                    dve.wait_ge(mixed_p, u + 1)
                    dve.tensor_scalar(OC[t][:, h * P:(h + 1) * P], o, r, None, ALU.mult).then_inc(o_copied, 1)
                    return
                g = h + (4 if kind == "m" else 0)
                dst = O[:, t, g * P:(g + 1) * P]
                if kind == "d":
                    step(dve.tensor_copy(dst, o))
                else:
                    dve.wait_ge(mixed_p, u + 1)
                    step(dve.tensor_scalar(dst, o, r, None, ALU.mult))
                n, cols = power(("mix", t))
                dve.tensor_tensor_reduce(out=TMP[:, 0:P], in0=dst, in1=dst, scale=1.0 / P, scalar=RMS_EPS,
                                         op0=ALU.mult, op1=ALU.add, accum_out=cols[:, g:g + 1]).then_inc(o_copied, 1)
                dve.wait_ge(o_copied, u + 1)
                if u % 8 == 7:
                    dve.nop().then_inc(pow_asked, 1)

            def norm_heads(t):
                cols = rsqrt(("mix", t))
                v = O[:, t, :].rearrange("p (g n) -> p g n", g=8)
                dve.tensor_tensor(v, v, cols.unsqueeze(2).to_broadcast([P, 8, P]), ALU.mult).then_inc(o_normed, 1)

            def layer_norm(name, t, rows, loaded, done):
                v = X[:, t, :]
                for i in range(2):
                    step(dve.bn_stats(ST[:, i, :], v[:, i * 512:(i + 1) * 512]))
                step(dve.bn_aggr(MV[:, 0:2], ST[:, :, :]))
                n, cols = power((name, t))
                dve.tensor_scalar(cols, MV[:, 1:2], LN_EPS, None, ALU.add).then_inc(pow_asked, 1)
                dve.wait_ge(pow_done, n + 1)
                step(dve.tensor_scalar(MV[:, 2:3], MV[:, 0:1], cols, -1.0, ALU.mult, ALU.mult))
                step(dve.tensor_scalar(v, v, cols, MV[:, 2:3], ALU.mult, ALU.add))
                dve.wait_ge(loaded, 32)
                step(dve.tensor_tensor(v, v, rows[:, 0, :], ALU.mult))
                dve.tensor_tensor(v, v, rows[:, 1, :], ALU.add).then_inc(ln_done, 1)
                dve.wait_ge(ln_done, done)

            def residual(t, n0):
                for i in range(2):
                    dve.wait_ge(res_done, n0 + 2 * t + i + 1)
                    v = X[:, t, i * 512:(i + 1) * 512]
                    step(dve.scalar_tensor_tensor(v, v, ALPHA, banks[6 + i][:, :], ALU.mult, ALU.add))

            def mix_hook(what, t):
                if what == "mixT":
                    norm_heads(t)
                else:
                    residual(t, 0)
                    layer_norm("ln1", t, LNP, ln1_in, t + 1)

            def mem_hook(what, t):
                if what == "out":
                    residual(t, 2 * NT)
                    layer_norm("ln2", t, LNP, ln2_in, NT + t + 1)

            nm, nx = len(MIX_UNITS), len(UNITS)
            pipeline(0, nm, MIX_HOOKS, maxima, probabilities, values, mix_hook)

            def h_copy(first, t):
                dve.wait_ge(h_done, 2 * (first + t) + 2)
                dve.tensor_copy(AT[:, 4:8, t * P:(t + 1) * P],
                                banks[1 + 2 * (t % 2)][:, :].rearrange("p (c n) -> p c n", c=4)).then_inc(h_dve, 1)

            for t in range(NT):
                h_copy(0, t)
            pipeline(nm, nx, MEM_HOOKS, maxima, probabilities, values, mem_hook)
            for t in range(NT):
                h_copy(NT, t)

            def small(i, w=NT * N_GRP):
                return R8[:, i, 0:w]

            def grouped(v):
                return v.rearrange("p t (g e) -> p (t g) e", g=N_GRP)

            def per_group(v):
                return v.unsqueeze(2).to_broadcast([P, NT * N_GRP, N_GRP])

            dve.wait_ge(sig_done, 1)
            big = 1e30
            step(dve.tensor_tensor(CH[:, :, :], SC[:, :, :], rbias[:, :].unsqueeze(1).to_broadcast([P, NT, N_EXP]),
                                   ALU.add))
            step(dve.reduce_max(small(0), grouped(CH), AX.X))
            step(dve.tensor_tensor(grouped(T1), grouped(CH), per_group(small(0)), ALU.is_equal))
            step(dve.tensor_reduce(small(1), grouped(T1), AX.X, ALU.add))
            step(dve.scalar_tensor_tensor(T2[:, :, :], T1[:, :, :], -big, CH[:, :, :], ALU.mult, ALU.add))
            step(dve.reduce_max(small(2), grouped(T2), AX.X))
            step(dve.tensor_scalar(small(1), small(1), 1.5, None, ALU.is_ge))
            step(dve.tensor_scalar(small(1), small(1), -1.0, big, ALU.add, ALU.mult))
            step(dve.tensor_tensor(small(1), small(1), small(0), ALU.add))
            step(dve.tensor_tensor(small(2), small(2), small(1), ALU.max))
            step(dve.tensor_tensor(small(0), small(0), small(2), ALU.add))
            gs = small(0).rearrange("p (t g) -> p t g", t=NT)
            for t in range(NT):
                mine = gs[:, t, :].unsqueeze(2).to_broadcast([P, N_GRP, N_GRP])
                others = gs[:, t, :].unsqueeze(1).to_broadcast([P, N_GRP, N_GRP])
                a = T1[:, t, :].rearrange("p (g k) -> p g k", g=N_GRP)
                b = T2[:, t, :].rearrange("p (g k) -> p g k", g=N_GRP)
                step(dve.tensor_tensor(a, others, mine, ALU.is_gt))
                step(dve.tensor_tensor(b, others, mine, ALU.is_equal))
                step(dve.tensor_tensor(b, b, tri8[:, :, :], ALU.mult))
            step(dve.tensor_tensor(T1[:, :, :], T1[:, :, :], T2[:, :, :], ALU.add))
            step(dve.tensor_reduce(small(3), grouped(T1), AX.X, ALU.add))
            step(dve.tensor_scalar(small(3), small(3), TOPK_GRP - 0.5, None, ALU.is_le))
            step(dve.tensor_tensor(grouped(MC), grouped(CH), per_group(small(3)), ALU.mult))
            step(dve.tensor_scalar(small(4), small(3), -1.0, big, ALU.add, ALU.mult))
            step(dve.tensor_tensor(grouped(MC), grouped(MC), per_group(small(4)), ALU.add))
            for t in range(NT):
                step(dve.max(R8[:, 5, t * 8:t * 8 + 8], MC[:, t, :]))
                step(dve.match_replace(T1[:, t, :], R8[:, 5, t * 8:t * 8 + 8], MC[:, t, :], -2.0 * big))
            step(dve.tensor_scalar(SELM[:, :, :], T1[:, :, :], -1.5 * big, None, ALU.is_le))
            dve.tensor_copy(selb[:, :, :], SELM[:, :, :]).then_inc(sel_ready, 1)
            step(dve.tensor_tensor(GATE[:, :, :], SC[:, :, :], SELM[:, :, :], ALU.mult))
            step(dve.tensor_reduce(R8[:, 6, 0:NT], GATE[:, :, :], AX.X, ALU.add))
            step(dve.reciprocal(R8[:, 6, 4:4 + NT], R8[:, 6, 0:NT]))
            for t in range(NT):
                step(dve.tensor_scalar(GATE[:, t, :], GATE[:, t, :], R8[:, 6, 4 + t:5 + t], ROUTED_SCALE,
                                       ALU.mult, ALU.mult))
            dve.wait_ge(rank_done, 1)
            ranks = banks[5][:, 0:NT * N_EXP].rearrange("p (t e) -> p t e", t=NT)
            size = banks[5][:, NT * N_EXP:(NT + 1) * N_EXP]
            ex, cum, start, base, tmp = (ST64[:, i, :] for i in range(5))
            step(dve.tensor_scalar(ex, size, P + 0.5, None, ALU.is_ge))
            for lim in (2 * P, 3 * P):
                step(dve.scalar_tensor_tensor(ex, size, lim + 0.5, ex, ALU.is_ge, ALU.add))
            step(dve.memset(tmp, 0.0))
            step(dve.tensor_tensor_scan(cum, ex, tmp, 0.0, ALU.add, ALU.add))
            step(dve.tensor_tensor(start, cum, ex, ALU.subtract))
            step(dve.tensor_scalar(base, start, N_EXP - 1.0, float(P), ALU.add, ALU.mult))
            step(dve.tensor_tensor(tmp, e128[:, :], base, ALU.subtract))
            wide = lambda v: v.unsqueeze(1).to_broadcast([P, NT, N_EXP])
            step(dve.tensor_scalar(T1[:, :, :], ranks, P - 0.5, None, ALU.is_le))
            step(dve.tensor_tensor(T1[:, :, :], T1[:, :, :], wide(tmp), ALU.mult))
            step(dve.tensor_tensor(T1[:, :, :], T1[:, :, :], wide(base), ALU.add))
            step(dve.scalar_tensor_tensor(T1[:, :, :], ranks, 1.0, T1[:, :, :], ALU.add, ALU.add))
            step(dve.tensor_tensor(POSM[:, :, :], T1[:, :, :], SELM[:, :, :], ALU.mult))
            posk = R8[:, 7, :]
            for t in range(NT):
                step(dve.max(posk[:, t * 8:t * 8 + 8], POSM[:, t, :]))
            step(dve.tensor_scalar(pos_u[:, :], posk, -1.0, None, ALU.add))
            item_u, slot_u = R8[:, 8, :].bitcast(U32), R8[:, 9, :].bitcast(U32)
            step(dve.tensor_scalar(item_u, pos_u[:, :], 7, None, ALU.logical_shift_right))
            step(dve.tensor_scalar(slot_u, pos_u[:, :], P - 1, None, ALU.bitwise_and))
            step(dve.tensor_copy(R8[:, 10, :], item_u))
            step(dve.tensor_copy(R8[:, 11, :], slot_u))
            dve.scalar_tensor_tensor(spos_u[:, :], R8[:, 11, :], float(LIST_COLS), R8[:, 10, :], ALU.mult,
                                     ALU.add).then_inc(spos_ready, 1)
            step(dve.tensor_scalar(counts_i[:, 0:1], cum[:, N_EXP - 1:N_EXP], float(N_EXP + UNROLL - 1), None, ALU.add))
            step(dve.tensor_scalar(counts_i[:, 1:2], counts_i[:, 0:1], 2, None, ALU.logical_shift_right))
            step(dve.tensor_scalar(counts_i[:, 2:3], counts_i[:, 1:2], -1.0, None, ALU.add))
            for k in range(MAX_EXTRA // 4):
                four = T2[:, :, :]
                step(dve.tensor_tensor(four, wide(cum), item_no[:, 4 * k:4 * k + 4].unsqueeze(2).to_broadcast([P, 4, N_EXP]),
                                       ALU.is_le))
                step(dve.tensor_reduce(R8[:, 5, 4 * k:4 * k + 4], four, AX.X, ALU.add))
            step(dve.tensor_scalar(extra_i[:, :], R8[:, 5, 0:MAX_EXTRA], N_EXP - 1.0, None, ALU.min))
            dve.nop().then_inc(counts_ready, 1)

            def gate_of_choices():
                for t in range(NT):
                    for k in range(TOP_K):
                        j = t * TOP_K + k
                        step(dve.scalar_tensor_tensor(T2[:, t, :], POSM[:, t, :], posk[:, j:j + 1], GATE[:, t, :],
                                                      ALU.is_equal, ALU.mult, accum_out=gk[:, j:j + 1]))

            def hidden(q, b):
                dve.wait_ge(silu_done, q + 1)
                if not isinstance(q, int) or q >= 2:
                    dve.wait_ge(ht_done, q + -1)
                dve.tensor_tensor(HS[b % 2], SG[b % 2], banks[b % 2][:, F_EXP:2 * F_EXP], ALU.mult).then_inc(h_ready, 1)

            def xgt_copy(i, b):
                dve.wait_ge(xt_done, i + 1)
                dve.wait_ge(gu_done, i + 3)
                dve.tensor_copy(XGT[b % 2][:, 4:8, :], banks[3][:, :].rearrange("p (c n) -> p c n", c=4)).then_inc(xt_dve, 1)

            def y_copy(it, b):
                i = it * UNROLL + b
                dve.wait_ge(down_done, i + (NT + 1))
                dve.wait_ge(y_free[b % 2], it * 32 + 16 * (b // 2 + 1))
                dve.tensor_copy(Y[b % 2][:, 512:1024], banks[5][:, :]).then_inc(y_dve, 1)

            def shared_add(t):
                dve.wait_ge(down_done, t + 1)
                for i in range(2):
                    v = X[:, t, i * 512:(i + 1) * 512]
                    if t == 0 and i == 0:
                        dve.wait_ge(h2_stored, 16 * NT)
                    dve.scalar_tensor_tensor(v, v, ALPHA, banks[4 + i][:, :], ALU.mult, ALU.add
                                             ).then_inc(sh_added if t < NT - 1 else (y_act, y_dve)[i], 1)

            for q in range(NT):
                hidden(q, q)
                if q == 0:
                    gate_of_choices()
                if q:
                    shared_add(q - 1)
            xgt_copy(0, 0)
            shared_add(NT - 1)
            n_iter = dve.value_load(counts_i[0:1, 1:2], min_val=N_EXP // UNROLL, max_val=MAX_ITEMS // UNROLL)
            with dve.Fori(0, n_iter) as it:
                for b in range(UNROLL):
                    hidden(it * UNROLL + (b + NT), b)
                    xgt_copy(it * UNROLL + (b + 1), b + 1)
                    if b:
                        y_copy(it, b - 1)
                y_copy(it, UNROLL - 1)
            dve.wait_ge(sh_added, 2 * NT - 2)
            dve.wait_ge(y_act, 1)
            dve.wait_ge(y_dve, 1)
            for t in range(NT):
                for k in range(TOP_K):
                    j = t * TOP_K + k
                    dve.wait_ge(cg_in[j % 8], 16 * (j // 8 + 1))
                    dve.scalar_tensor_tensor(X[:, t, :], CG[j % 8], gk[:, j:j + 1], X[:, t, :], ALU.mult,
                                             ALU.add).then_inc(cg_used, 1)
                    dve.wait_ge(cg_used, j + 1)
                layer_norm("ln3", t, LN3, ln3_in, 2 * NT + t + 1)

        @block.tensor
        def _(pe):
            pe.wait_ge(const_ready, 2)

            def product(out_ap, pairs):
                for c, (a, b) in enumerate(pairs):
                    last = nc.tensor.matmul(out_ap, a, b, start=(c == 0), stop=(c == len(pairs) - 1))
                return last

            def transposes(bank, blocks, width=P):
                for c, a in enumerate(blocks):
                    last = nc.tensor.transpose(bank[:, c * P:(c + 1) * P], a, ident[:, :])
                return last

            for j, g in enumerate(FRONT):
                bank = banks[j % 8]
                if j >= 8:
                    copied(pe, j - 8)
                kind = g[0]
                if kind == "xT":
                    pe.wait_ge(x_in[g[1]], 16)
                    v = X[:, g[1], :].rearrange("p (m c) -> p c m", c=NC)
                    last = transposes(bank, [v[:, 4 * g[2] + c, :] for c in range(4)])
                elif kind == "proj":
                    n, t = g[1:]
                    if n == 0:
                        for h in range(2):
                            copied(pe, AT_GROUP[("xT", t, h)])
                    if t == 0:
                        pe.wait_ge(win_in[n], 16)
                    w = 448 if n == 0 else 512
                    last = product(bank[:, 0:w], [(AT[:, c, t * P:(t + 1) * P], WIN[n][:, c, :]) for c in range(NC)])
                elif kind in ("cqT", "ckvT"):
                    pe.wait_ge(lat_normed, 2 * NT)
                    c0 = LAT + 128 * (2 if kind == "ckvT" else g[1])
                    last = transposes(bank, [PR[:, t, c0:c0 + P] for t in range(NT)])
                elif kind == "kpT":
                    pe.wait_ge(kp_ready, 1)
                    last = transposes(bank, [KP[:, t, :] for t in range(NT)])
                elif kind == "qkT":
                    pe.wait_ge(rope_ready, NT)
                    last = transposes(bank, [PR[:, t, g[1] * P:(g[1] + 1) * P] for t in range(NT)])
                elif kind == "memT":
                    pe.wait_ge(mem_in, 16)
                    v = MEMX[:, g[1], :].rearrange("p (m c) -> p c m", c=NC)
                    last = transposes(bank, [v[:, 4 * g[2] + c, :] for c in range(4)])
                elif kind == "kmem":
                    pe.wait_ge(wkv_in, 32)
                    for i in range(4):
                        copied(pe, AT_GROUP[("memT", i // 2, i % 2)])
                    for i in range(2):
                        h = 2 * g[1] + i
                        last = product(bank[:, i * N_MEM:(i + 1) * N_MEM],
                                       [(WK[:, c, h * P:(h + 1) * P], MEMT[:, c, :]) for c in range(NC)])
                elif kind == "vmem":
                    last = product(bank[:, :], [(MEMT[:, c, g[1] * P:(g[1] + 1) * P], WV[:, c, :]) for c in range(NC)])
                elif kind == "qn":
                    pe.wait_ge(lat_in, 32)
                    for i in range(2):
                        copied(pe, AT_GROUP[("cqT", i)])
                    c0 = g[1] * (NOPE + ROPE)
                    last = product(bank[:, :], [(WUQ[:, c, c0:c0 + NOPE], CQT[:, c, :]) for c in range(2)])
                elif kind == "kn":
                    copied(pe, AT_GROUP[("ckvT",)])
                    c0 = g[1] * 2 * P
                    last = product(bank[:, :], [(WUKV[:, c0:c0 + P], CKVT)])
                elif kind == "vm":
                    v = WUKV.rearrange("p (h k n) -> p h k n", h=HD, k=2)[:, :, 1, :]
                    last = product(bank[:, :], [(CKVT[:, g[1] * P:(g[1] + 1) * P], v)])
                elif kind == "qp":
                    v = WUQ.rearrange("p c (h n) -> p c h n", h=HD)
                    last = product(bank[:, 0:HD * ROPE], [(CQT[:, c, g[1] * P:(g[1] + 1) * P], v[:, c, :, NOPE:NOPE + ROPE])
                                                          for c in range(2)])
                elif kind == "qpT":
                    for t in range(NT):
                        copied(pe, AT_GROUP[("qp", t)])
                    c0 = LAT + g[1] * P
                    last = transposes(bank, [PR[:, t, c0:c0 + P] for t in range(NT)])
                last.then_inc(grp_done, 1)
            for j in range(len(FRONT) - 8, len(FRONT)):
                copied(pe, j)

            def scores(u):
                kind, t, h = UNITS[u]
                q = slice(t * P, (t + 1) * P)
                n = keys(u)
                for k, s in enumerate(steps(u)):
                    if s >= 3:
                        pe.wait_ge(exp_done, s - 2)
                    bank = banks[s % 3]
                    if kind == "d":
                        r = slice(k * QK_D, (k + 1) * QK_D)
                        pairs = [(QDT[r, h, q], KDT[r, h, 0:n])]
                    elif kind == "m":
                        r = slice((h % 2) * ROPE, (h % 2 + 1) * ROPE)
                        pairs = [(QNT[:, h, q], KNT[:, h, 0:n]), (QPT[r, h // 2, q], KPT[r, 0:n])]
                    else:
                        pairs = [(QCT[:, h, q], KMT[:, h, :])]
                    for c, (a, b) in enumerate(pairs):
                        last = nc.tensor.matmul(bank[:, 0:n], a, b, start=(c == 0),
                                                stop=(kind == "x"), skip_group_check=True)
                    if kind != "x":
                        last = nc.tensor.matmul(bank[:, n - P:n], identb[:, :], maskb[:, :], start=False, stop=True,
                                                skip_group_check=True)
                    last.then_inc(scores_done, 1)

            def p_transposes(u):
                pe.wait_ge(mixed_p, u + 1)
                if u >= 2:
                    pe.wait_ge(pt_copied, u - 1)
                p = PB[STEP0[u] % 4]
                transposes(banks[3 + u % 2], [p[:, c * P:(c + 1) * P] for c in range(keys(u) // P)]).then_inc(pt_done, 1)

            def values(u):
                kind, t, h = UNITS[u]
                pe.wait_ge(pt_copied, u + 1)
                if u >= 1:
                    pe.wait_ge(o_copied, u)
                pt = PTB[u % 2]
                if kind == "d":
                    v = [PR[:, c, 1024 + h * P:1024 + (h + 1) * P] for c in range(t + 1)]
                elif kind == "m":
                    v = [VML[:, c, h * P:(h + 1) * P] for c in range(t + 1)]
                else:
                    v = [VM[:, c, h * P:(h + 1) * P] for c in range(2)]
                product(banks[5][:, 0:P],
                        [(pt[:, c * P:(c + 1) * P], b) for c, b in enumerate(v)]).then_inc(o_done, 1)

            def free_pair(t, n0):
                if t >= 1:
                    pe.wait_ge(ln_done, n0 + t)

            def mix_hook(what, t):
                if what == "mixT":
                    pe.wait_ge(o_normed, t + 1)
                    free_pair(t, 0)
                    for g in range(2):
                        transposes(banks[6 + g], [O[:, t, (4 * g + c) * P:(4 * g + c + 1) * P] for c in range(4)]
                                   ).then_inc(mixt_done, 1)
                else:
                    pe.wait_ge(mixt_copied, 2 * t + 2)
                    pe.wait_ge(wo_in, 16)
                    for i in range(2):
                        product(banks[6 + i][:, :], [(MIXT[:, c, :], WO[:, c, i * 512:(i + 1) * 512]) for c in range(NC)]
                                ).then_inc(res_done, 1)

            def mem_hook(what, t):
                if what == "mixT":
                    pe.wait_ge(o_copied, len(MIX_UNITS) + 4 * t + 4)
                    free_pair(t + (0 if t else 0), NT)
                    transposes(banks[6 + t % 2], [OC[t][:, c * P:(c + 1) * P] for c in range(4)]).then_inc(mixt_done, 1)
                else:
                    pe.wait_ge(mixt_copied, 2 * NT + t + 1)
                    pe.wait_ge(wo2_in, 16)
                    for i in range(2):
                        product(banks[6 + i][:, :], [(OCT[:, c, t * P:(t + 1) * P], WO2[:, c, i * 512:(i + 1) * 512])
                                                     for c in range(4)]).then_inc(res_done, 1)

            nm, nx = len(MIX_UNITS), len(UNITS)
            pipeline(0, nm, MIX_HOOKS, scores, p_transposes, values, mix_hook)

            def h_transposes(first, t):
                pe.wait_ge(ln_done, first + t + 1)
                v = X[:, t, :].rearrange("p (m c) -> p c m", c=NC)
                for g in range(2):
                    if t >= 2:
                        pe.wait_ge((h_act, h_dve)[g], first + t - 1)
                    transposes(banks[2 * (t % 2) + g], [v[:, 4 * g + c, :] for c in range(4)]).then_inc(h_done, 1)

            pe.wait_ge(exp_done, STEP0[nm])
            for t in range(NT):
                h_transposes(0, t)
            pe.wait_ge(wq_in, 16)
            pe.wait_ge(h_act, NT)
            pe.wait_ge(h_dve, NT)
            pe.wait_ge(o_copied, nm)
            for h in range(HD):
                product(banks[4 + h][:, :], [(WQ[:, c, h * P:(h + 1) * P], AT[:, c, :]) for c in range(NC)]
                        ).then_inc(qc_done, 1)
            pe.wait_ge(qc_act, HD)
            pipeline(nm, nx, MEM_HOOKS, scores, p_transposes, values, mem_hook)
            pe.wait_ge(exp_done, STEP0[-1] + 1)
            for t in range(NT):
                h_transposes(NT, t)

            pe.wait_ge(h_act, 2 * NT)
            pe.wait_ge(h_dve, 2 * NT)
            pe.wait_ge(pt_copied, nx)
            pe.wait_ge(rw_in, 16)
            for t in range(NT):
                last = product(banks[4][:, t * N_EXP:(t + 1) * N_EXP],
                               [(AT[:, c, t * P:(t + 1) * P], RW[:, c, :]) for c in range(NC)])
            last.then_inc(logits_done, 1)

            def gate_up(bank, xt, w):
                return product(bank[:, :], [(xt[c], w[:, :, c, :]) for c in range(NC)])

            def h_transpose(q, b):
                pe.wait_ge(h_ready, q + 1)
                pe.wait_ge(ht_copied, q)
                v = HS[b % 2].rearrange("p (m c) -> p c m", c=2)
                transposes(banks[7], [v[:, c, :] for c in range(2)]).then_inc(ht_done, 1)

            def down(q, b, w):
                pe.wait_ge(ht_copied, q + 1)
                for i in range(2):
                    last = product(banks[4 + i][:, :], [(HT[b % 2][:, c, :], w[:, c, i * 512:(i + 1) * 512])
                                                        for c in range(2)])
                last.then_inc(down_done, 1)

            def xg_transpose(i, b, arrivals):
                pe.wait_ge(xg_in[b % 2], arrivals)
                v = XG[b % 2].rearrange("p (m c) -> p c m", c=NC)
                for g in range(2):
                    last = transposes(banks[2 + g], [v[:, 4 * g + c, :] for c in range(4)])
                last.then_inc(xt_done, 1)

            pe.wait_ge(sh_in, 48)
            pe.wait_ge(ln_done, 2 * NT)

            def shared_gate_up(t):
                if t >= 2:
                    pe.wait_ge(h_ready, t - 1)
                gate_up(banks[t % 2], [AT[:, c, t * P:(t + 1) * P] for c in range(NC)], SHARED[0]).then_inc(gu_done, 1)

            shared_gate_up(0)
            pe.wait_ge(sel_ready, 1)
            for t in range(NT):
                pairs = [(beforeb[:, :], selb[:, t, :])] + [(onesb[:, :], selb[:, k, :]) for k in range(t)]
                product(banks[5][:, t * N_EXP:(t + 1) * N_EXP], pairs)
            product(banks[5][:, NT * N_EXP:(NT + 1) * N_EXP],
                    [(onesb[:, :], selb[:, k, :]) for k in range(NT)]).then_inc(rank_done, 1)
            pe.wait_ge(spos_ready, 1)
            for t in range(1, NT + 1):
                if t < NT:
                    shared_gate_up(t)
                else:
                    xg_transpose(0, 0, 16)
                h_transpose(t - 1, t - 1)
                if t >= 2:
                    pe.wait_ge(sh_added, 2 * (t - 1))
                down(t - 1, t - 1, SHARED[1])
            pe.wait_ge(counts_ready, 1)
            n_iter = pe.value_load(counts_i[0:1, 1:2], min_val=N_EXP // UNROLL, max_val=MAX_ITEMS // UNROLL)
            with pe.Fori(0, n_iter) as it:
                def down_item(b):
                    pe.wait_ge(y_act, it * UNROLL + (b + 1))
                    pe.wait_ge(y_dve, it * UNROLL + (b + 1))
                    down(it * UNROLL + (b + NT), b, SLOTS[b][1])

                for b in range(UNROLL):
                    pe.wait_ge(slot_in[b], it * 48 + 48)
                    pe.wait_ge(xt_act, it * UNROLL + (b + 1))
                    pe.wait_ge(xt_dve, it * UNROLL + (b + 1))
                    pe.wait_ge(h_ready, it * UNROLL + (b + NT - 1))
                    gate_up(banks[b % 2], [XGT[b % 2][:, c, :] for c in range(NC)], SLOTS[b][0]).then_inc(gu_done, 1)
                    if b:
                        h_transpose(it * UNROLL + (b + NT - 1), b - 1)
                    xg_transpose(None, b + 1, it * 32 + 16 * ((b + 1) // 2 + 1))
                    if b:
                        down_item(b - 1)
                h_transpose(it * UNROLL + (2 * NT - 1), UNROLL - 1)
                down_item(UNROLL - 1)


_INS = ["x", "mem", "positions", "w_in", "lam_q1", "lam_k1", "lam_q2", "lam_k2", "diff_subln_g", "mla_q_norm_g",
        "mla_w_uq", "mla_kv_norm_g", "mla_w_ukv", "mla_out_norm_g", "w_o", "ln1_g", "ln1_b", "mem_w_q", "mem_w_k",
        "mem_w_v", "mem_w_o", "ln2_g", "ln2_b", "router_w", "router_bias", "exp_w_gate", "exp_w_up", "exp_w_down",
        "sh_w_gate", "sh_w_up", "sh_w_down", "ln3_g", "ln3_b"]


def kernel(**inputs):
    import concourse.bacc as bacc
    from concourse.bass_utils import run_bass_kernel_spmd

    nc = bacc.Bacc("TRN2", target_bir_lowering=False, num_devices=1)
    arrays, args = {}, []
    for name in _INS:
        a = np.ascontiguousarray(inputs[name])
        arrays[f"in_{name}"] = a
        args.append(nc.dram_tensor(f"in_{name}", a.shape, mybir.dt.from_np(a.dtype), kind="ExternalInput").ap())
    args.append(nc.dram_tensor("layer_out", (1, SEQ, D), F32, kind="ExternalOutput").ap())
    build(nc, *args)
    r = run_bass_kernel_spmd(nc, [arrays], core_ids=[0])
    return r.results[0]["layer_out"]
```

```python
import math
from contextlib import ExitStack

import concourse.bass as bass
import numpy as np
from concourse import mybir

F32 = mybir.dt.float32
BF16 = mybir.dt.bfloat16
I32 = mybir.dt.int32
U32 = mybir.dt.uint32
ALU = mybir.AluOpType
ACT = mybir.ActivationFunctionType
AX = mybir.AxisListType

P = 128
SEQ = 512
D = 1024
NT = SEQ // P
NC = D // P
N_MEM = 256
IN_COLS = 1984
LAT = 1536
THETA = 500000.0
ROT_D = 16
ROT_M = 64
HD = 4
QK_D = 64
NOPE = 128
ROPE = 64
N_EXP = 64
F_EXP = 256
N_GRP = 8
TOPK_GRP = 4
TOP_K = 8
ROUTED_SCALE = 2.5
ALPHA = 2.0 ** 0.25
LAM_INIT = 0.8 - 0.6 * math.exp(-0.3 * 0)
LN_EPS = 1e-5
RMS_EPS = 1e-6
SCALE_D = QK_D ** -0.5
SCALE_M = (NOPE + ROPE) ** -0.5
SCALE_X = 128 ** -0.5

OUT0, LN1A, LN1B, HTA, QCA = 10.2, 13.3, 14.3, 16.5, 17.6
XU, M2T, OUT2, LN2A, LN2B = 20.5, 25.15, 27.5, 29.7, 30.7
H2T_AT = (42.8, 39.2, 47.2, 55.2)
SHARED_AT = ((43.3, 44.3, 45.0), )
EARLY = len(SHARED_AT)
LOGITS_AT = (47.3, 55.4)

UNROLL = 4
MAX_EXTRA = SEQ * TOP_K // P
MAX_ITEMS = N_EXP + MAX_EXTRA
LIST_COLS = MAX_ITEMS + UNROLL
NO_TOKEN = 4096
SLOT = 3 * NC * F_EXP


class Chain:

    def __init__(self, eng, sem):
        self.eng, self.sem, self.n = eng, sem, 0

    def __call__(self, ins):
        self.n += 1
        ins.then_inc(self.sem, 1)
        self.eng.wait_ge(self.sem, self.n)

    def tell(self, ins, sem, n):
        ins.then_inc(sem, 1)
        self.eng.wait_ge(sem, n)


def build(nc, x, mem, positions, w_in, lam_q1, lam_k1, lam_q2, lam_k2, diff_subln_g, mla_q_norm_g,
          mla_w_uq, mla_kv_norm_g, mla_w_ukv, mla_out_norm_g, w_o, ln1_g, ln1_b, mem_w_q, mem_w_k,
          mem_w_v, mem_w_o, ln2_g, ln2_b, router_w, router_bias, exp_w_gate, exp_w_up, exp_w_down,
          sh_w_gate, sh_w_up, sh_w_down, ln3_g, ln3_b, out):
    h2_rows = nc.dram_tensor("h2_rows", (SEQ, D), F32, kind="Internal").ap()
    y_rows = nc.dram_tensor("y_rows", (MAX_ITEMS * P, D), F32, kind="Internal").ap()
    token_list = nc.dram_tensor("token_list", (P * LIST_COLS, 1), U32, kind="Internal").ap()

    ctx = ExitStack()
    with ctx:
        def sb(name, shape, dt=F32):
            return ctx.enter_context(nc.sbuf_tensor(name, shape, dt))

        def sem(name):
            return ctx.enter_context(nc.semaphore(name))

        E = sb("expert_slots", [P, UNROLL * SLOT])
        X = sb("residual", [P, NT, D])
        AT = sb("act_transposed", [P, NC, SEQ])
        W = sb("weights", [P, 8192])
        PR = sb("proj", [P, NT, IN_COLS])
        MKV = sb("mem_k_v", [P, 2048])
        RW = sb("router_w", [P, NC, N_EXP])
        ident = sb("ident", [P, P])
        identb = sb("ident_bf16", [P, P], BF16)
        maskb = sb("causal_mask", [P, P], BF16)
        beforeb = sb("tokens_before", [P, P], BF16)
        onesb = sb("ones", [P, P], BF16)
        tri8 = sb("groups_before", [P, N_GRP, N_GRP])
        pos_i = sb("pos_i", [P, NT], I32)
        pos_f = sb("pos_f", [P, NT])
        n_freq = ROT_D // 2 + ROT_M // 2
        cosT = sb("cos", [P, NT, n_freq])
        sinT = sb("sin", [P, NT, n_freq])
        lam_in = sb("lam_in", [P, 4, QK_D])
        lam_sc = sb("lam_sc", [P, 8])
        gcol = sb("gain_columns", [P, 6])
        half = sb("minus_half", [P, 8])
        spare = sb("spare", [P, 8])
        POWB = sb("rsqrt_io", [P, 64])
        MS = sb("max_sum", [P, 4, 16])
        ST = sb("ln_stats", [P, 2, 6])
        MV = sb("ln_mean_var", [P, 8])
        rbias = sb("router_bias", [P, N_EXP])
        e128 = sb("expert_times_128", [P, N_EXP])
        item_no = sb("item_no", [P, MAX_EXTRA])
        iota_i = sb("iota_i", [P, N_EXP], I32)
        token_id = sb("token_id", [P, NT], U32)
        lists = sb("lists", [P, LIST_COLS], U32)
        idx_col = sb("idx_col", [P, 2], U32)
        pos_u = sb("pos_u", [P, NT * TOP_K], U32)
        spos_u = sb("spos_u", [P, NT * TOP_K], U32)
        gk = sb("gate_of_choice", [P, NT * TOP_K])
        counts_i = sb("counts_i", [P, 3], I32)
        extra_i = sb("extra_experts", [P, MAX_EXTRA], I32)

        banks = [ctx.enter_context(nc.psum_tensor(f"bank{i}", [P, 512], F32)) for i in range(8)]

        KMT = MKV[:, 0:1024].rearrange("p (h n) -> p h n", h=HD)
        VM = MKV[:, 1024:2048].rearrange("p (m n) -> p m n", m=2)
        ST64 = MKV[:, 512:832].rearrange("p (i n) -> p i n", i=5)
        R8 = MKV[:, 1024:1408].rearrange("p (i n) -> p i n", i=12)
        selb = MKV[:, 1408:1536].bitcast(BF16).rearrange("p (t e) -> p t e", t=NT)
        WIN = [E[:, n * NC * 512:n * NC * 512 + NC * w].rearrange("p (c n) -> p c n", c=NC)
               for n, w in enumerate((448, 512, 512, 512))]
        MEMX = E[:, 16384:18432].rearrange("p (m d) -> p m d", m=2)
        MEMT = E[:, 18432:20480].rearrange("p (c n) -> p c n", c=NC)
        WUQ = E[:, 20480:22016].rearrange("p (c n) -> p c n", c=2)
        WUKV = E[:, 22016:23040]
        KP = E[:, 23040:23552].rearrange("p (t n) -> p t n", t=NT)
        TMP = E[:, 23552:24576]
        QDT = E[:, 0:2048].rearrange("p (c n) -> p c n", c=4)
        KDT = E[:, 2048:4096].rearrange("p (c n) -> p c n", c=4)
        QNT = E[:, 4096:6144].rearrange("p (c n) -> p c n", c=4)
        KNT = E[:, 6144:8192].rearrange("p (c n) -> p c n", c=4)
        QPT = E[:, 8192:9216].rearrange("p (c n) -> p c n", c=2)
        KPT = E[:, 9216:9728]
        VML = E[:, 9728:11776].rearrange("p (t n) -> p t n", t=NT)
        WQ = E[:, 12288:16384].rearrange("p (c n) -> p c n", c=NC)
        WO2 = E[:, 16384:20480].rearrange("p (c n) -> p c n", c=4)
        LN1 = E[:, 20480:22528].rearrange("p (g d) -> p g d", g=2)
        LN2 = E[:, 22528:24576].rearrange("p (g d) -> p g d", g=2)
        WK = W[:, 0:4096].rearrange("p (c n) -> p c n", c=NC)
        WV = W[:, 4096:8192].rearrange("p (c n) -> p c n", c=NC)
        WO = W[:, :].rearrange("p (c n) -> p c n", c=NC)
        CQT = AT[:, 0:2, :]
        CKVT = AT[:, 2, :]
        H1T = AT[:, :, 0:P]
        O = [AT[:, :, (1 + i) * P:(2 + i) * P] for i in range(2)]
        QCT = AT[:, 0:4, 3 * P:4 * P]
        OCT = AT[:, 4:8, 3 * P:4 * P]
        PB = [PR[:, i // 2, (i % 2) * 512:(i % 2) * 512 + 512] for i in range(4)]
        PTB = [PR[:, 2, i * 512:i * 512 + 512] for i in range(2)]
        MIXT = PR[:, 3, 0:1024].rearrange("p (c n) -> p c n", c=NC)
        OC = PR[:, :, LAT:LAT + P]
        SQ = PR[:, 3, LAT + 192:LAT + 192 + P]
        PF = PR[:, :, :].rearrange("p t n -> p (t n)")
        XG = [PF[:, i * 1024:i * 1024 + 1024] for i in range(2)]
        XGT = [PF[:, 2048 + i * 1024:3072 + i * 1024].rearrange("p (c n) -> p c n", c=NC) for i in range(2)]
        Y = [PF[:, 4096 + i * 1024:5120 + i * 1024] for i in range(2)]
        HS = [PF[:, 6144 + i * 256:6400 + i * 256] for i in range(2)]
        HT = [PF[:, 6656 + i * 256:6912 + i * 256].rearrange("p (c n) -> p c n", c=2) for i in range(2)]
        SG = [PF[:, 7168 + i * 256:7424 + i * 256] for i in range(2)]
        SEL0 = 6144
        (SC, CH, T1, T2, MC, SELM, POSM, GATE) = [
            W[:, SEL0 + i * 256:SEL0 + i * 256 + 256].rearrange("p (t e) -> p t e", t=NT) for i in range(8)]
        CG = [E[:, i * D:(i + 1) * D] for i in range(8)]
        LN3 = AT[:, 0:4, :].rearrange("p c n -> p (c n)").rearrange("p (g d) -> p g d", g=2)

        def slot_views(flat):
            n = NC * F_EXP
            return (flat[:, 0:2 * n].rearrange("p (g c n) -> p g c n", g=2, c=NC),
                    flat[:, 2 * n:3 * n].rearrange("p (c n) -> p c n", c=2))

        SLOTS = [slot_views(E[:, b * SLOT:(b + 1) * SLOT]) for b in range(UNROLL)]
        SHARED = slot_views(W[:, 0:SLOT])

        x_in = [sem(f"x_in{t}") for t in range(NT)]
        win_in = [sem(f"w_in_block{n}") for n in range(4)]
        mem_in, wkv_in, lat_in, wo_in = sem("mem_in"), sem("wkv_in"), sem("lat_in"), sem("wo_in")
        small_in, ln1_in, ln2_in, ln3_in = sem("small_in"), sem("ln1_in"), sem("ln2_in"), sem("ln3_in")
        wq_in, wo2_in, sh_in, rw_in = sem("wq_in"), sem("wo2_in"), sem("shared_in"), sem("router_in")
        slot_in = [sem(f"slot_in{b}") for b in range(UNROLL)]
        const_ready, pool_step = sem("const_ready"), sem("pool_step")
        dve_step, act_step = sem("dve_step"), sem("act_step")
        range_ready, trig_ready, lam_dots, lam_exps, lam_ready = (
            sem("range_ready"), sem("trig_ready"), sem("lam_dots"), sem("lam_exps"), sem("lam_ready"))
        gains_ready = sem("gains_ready")
        pow_asked, pow_done = sem("pow_asked"), sem("pow_done")
        grp_done, grp_act, grp_dve = sem("group_done"), sem("group_copied_act"), sem("group_copied_dve")
        lat_normed, kp_ready, rope_ready, qp_ready = (
            sem("lat_normed"), sem("k_pe_ready"), sem("rope_ready"), sem("q_pe_ready"))
        scores_done, negmax_ready, exp_done, mixed_p = (
            sem("scores_done"), sem("negmax_ready"), sem("exp_done"), sem("mixed_p"))
        pt_done, pt_copied, o_done, o_copied = sem("pt_done"), sem("pt_copied"), sem("o_done"), sem("o_copied")
        o_normed = sem("o_normed")
        aux_done, aux_act, aux_dve = sem("projection_done"), sem("projection_copied_act"), sem("projection_copied_dve")
        ln1_done, ln2_done, ln3_done = sem("ln1_done"), sem("ln2_done"), sem("ln3_done")
        h2_stored = [sem(f"h2_stored{t}") for t in range(NT)]
        sel_ready, rank_done = sem("selection_ready"), sem("rank_done")
        spos_ready, counts_ready, list_filled, listed, lists_in = (
            sem("list_places_ready"), sem("counts_ready"), sem("list_filled"), sem("listed"), sem("lists_in"))
        kp_rotated = sem("k_pe_rotated")
        gu_done, silu_done, h_ready, ht_done, ht_copied, down_done = (
            sem("gate_up_done"), sem("silu_done"), sem("h_ready"), sem("h_transposed"), sem("ht_copied"),
            sem("down_done"))
        sh_silu, sh_added = sem("shared_silu_done"), sem("shared_added")
        xg_in = [sem("xg_in0"), sem("xg_in1")]
        xg_zero = sem("xg_zeroed")
        xt_done, xt_act, xt_dve = sem("xg_transposed"), sem("xgt_copied_act"), sem("xgt_copied_dve")
        y_act, y_dve = sem("y_copied_act"), sem("y_copied_dve")
        y_free = [sem("y_free0"), sem("y_free1")]
        idx_ready, zeros_ready, rows_zeroed = sem("idx_ready"), sem("zeros_ready"), sem("rows_zeroed")
        cg_in = [sem(f"choice_in{i}") for i in range(8)]
        cg_used, out_stored = sem("choice_used"), sem("out_stored")

        FRONT = ([("xT", t, h) for t in range(NT) for h in range(2)]
                 + [("proj", n, t) for n in range(4) for t in range(NT)]
                 + [("cqT", 0), ("cqT", 1), ("ckvT",), ("kpT",)]
                 + [("qkT", c) for c in range(8)]
                 + [("memT", m, h) for m in range(2) for h in range(2)]
                 + [("kmem", i) for i in range(2)] + [("vmem", m) for m in range(2)]
                 + [("qn", h) for h in range(HD)] + [("kn", h) for h in range(HD)]
                 + [("vm", t) for t in range(NT)] + [("qp", t) for t in range(NT)]
                 + [("qpT", 0), ("qpT", 1)])
        AT_GROUP = {g: j for j, g in enumerate(FRONT)}

        def on_dve(j):
            return j % 2 == 1 or FRONT[j][0] in ("qp", "cqT")

        def copied(eng, j):
            same = on_dve(j)
            n = sum(on_dve(i) == same for i in range(j + 1))
            eng.wait_ge(grp_dve if same else grp_act, n)

        timed = sorted([(8.0 * t + k, ("dm"[k // 4], t, k % 4)) for t in range(NT) for k in range(8)]
                       + [(8 * t + XU + k, ("x", t, k)) for t in range(NT) for k in range(4)])
        UNITS = [unit for _, unit in timed]
        UNIT = {unit: u for u, unit in enumerate(UNITS)}
        EVENTS = []
        for u, (at, unit) in enumerate(timed):
            two_ahead = max(at - 2, timed[u - 2][0]) if u >= 2 else at - 2
            EVENTS += [(two_ahead, "scores", unit), (at - 0.1, "probabilities", unit),
                       (at + 0.4, "transpose", unit), (at + 1.1, "values", unit)]
        for t in range(NT):
            b = 8 * t
            EVENTS += [(b + 8.6, "norm_heads", t), (b + LN1A, "ln1_stats", t), (b + LN1B, "ln1_rows", t),
                       (b + LN2A, "ln2_stats", t), (b + LN2B, "ln2_rows", t)]
            for at, job, part in ([(b + 9.5, ("mixT", t, g), None) for g in range(2)]
                                  + [(b + OUT0 + i * 2 + k, ("out", t, i), k) for i in range(2) for k in range(2)]
                                  + [(b + HTA, ("hT", t, g), None) for g in range(2)]
                                  + [(b + QCA + 0.5 * k, ("qc", t), k) for k in range(2)]
                                  + [(b + M2T, ("mix2T", t), None)]
                                  + [(b + OUT2 + 2 * i, ("out2", t, i), None) for i in range(2)]
                                  + [(H2T_AT[t], ("h2T", t, g), None) for g in range(2)]):
                EVENTS.append((at, "aux", (job, part)))
        for t in range(EARLY):
            EVENTS += [(SHARED_AT[t][0], "aux", (("gate_up", t), None)), (SHARED_AT[t][1], "aux", (("hidden", t), None))]
            EVENTS += [(SHARED_AT[t][2], "aux", (("down", t, i), None)) for i in range(2)]
        EVENTS += [(LOGITS_AT[k], "aux", (("logits", k), None)) for k in range(2)]
        EVENTS.sort(key=lambda e: e[0])
        for what in ("scores", "transpose", "values"):
            assert UNITS == [e[2] for e in EVENTS if e[1] == what]
        JOBS = [e[2][0] for e in EVENTS if e[1] == "aux" and e[2][1] in (None, 1)]
        JOB = {job: j for j, job in enumerate(JOBS)}
        assert [e[2][0] for e in EVENTS if e[1] == "aux" and e[2][1] in (None, 0)] == JOBS

        def job_on_dve(job):
            return job[0] in ("out", "out2", "gate_up", "down") or (job[0] in ("hT", "h2T") and job[2] == 1)

        def job_copied(eng, job):
            j, same = JOB[job], job_on_dve(job)
            n = sum(job_on_dve(i) == same for i in JOBS[:j + 1])
            eng.wait_ge(aux_dve if same else aux_act, n)

        POW, col = {}, 0
        asks = [("lat", t) for t in range(NT)]
        for _, what, arg in EVENTS:
            if what == "values" and arg[0] == "m" and arg[2] == HD - 1:
                asks.append(("mix", arg[1]))
            elif what in ("ln1_stats", "ln2_stats"):
                asks.append((what[:3], arg))
        asks += [("ln3", t) for t in range(NT)]
        for name in asks:
            width = {"lat": 2, "mix": 8}.get(name[0], 1)
            POW[name] = (len(POW), col, width)
            col += width

        def power(name):
            n, c, w = POW[name]
            return n, POWB[:, c:c + w]

        STEP0, s = [], 0
        for kind, _, _ in UNITS:
            STEP0.append(s)
            s += 2 if kind == "d" else 1
        UNIT_OF_STEP = [u for u, (k, _, _) in enumerate(UNITS) for _ in range(2 if k == "d" else 1)]

        def steps(u):
            return range(STEP0[u], STEP0[u] + (2 if UNITS[u][0] == "d" else 1))

        def keys(u):
            kind, t, _ = UNITS[u]
            return N_MEM if kind == "x" else (t + 1) * P

        def front_dest(eng, j, copy):
            g = FRONT[j]
            bank = banks[j % 8]
            four = bank[:, :].rearrange("p (c n) -> p c n", c=4)
            if g[0] == "xT":
                copy(AT[:, 4 * g[2]:4 * g[2] + 4, g[1] * P:(g[1] + 1) * P], four, None)
            elif g[0] == "proj":
                c0, w = [(LAT, 448), (0, 512), (512, 512), (1024, 512)][g[1]]
                copy(PR[:, g[2], c0:c0 + w], bank[:, 0:w], None)
            elif g[0] == "cqT":
                copy(CQT[:, g[1], :], bank[:, :], gcol[:, g[1]:g[1] + 1])
            elif g[0] == "ckvT":
                copy(CKVT, bank[:, :], gcol[:, 2:3])
            elif g[0] == "kpT":
                copy(KPT, bank[:, :], None)
            elif g[0] == "qkT":
                copy((QDT if g[1] < 4 else KDT)[:, g[1] % 4, :], bank[:, :], None)
            elif g[0] == "memT":
                copy(MEMT[:, 4 * g[2]:4 * g[2] + 4, g[1] * P:(g[1] + 1) * P], four, None)
            elif g[0] == "kmem":
                eng.wait_ge(rows_zeroed, 16)
                copy(KMT[:, 2 * g[1]:2 * g[1] + 2, :], bank[:, :].rearrange("p (h n) -> p h n", h=2), None)
            elif g[0] == "vmem":
                copy(VM[:, g[1], :], bank[:, :], None)
            elif g[0] == "qn":
                copy(QNT[:, g[1], :], bank[:, :], None)
            elif g[0] == "kn":
                copy(KNT[:, g[1], :], bank[:, :], None)
            elif g[0] == "vm":
                copy(VML[:, g[1], :], bank[:, :], None)
            elif g[0] == "qpT":
                copy(QPT[:, g[1], :], bank[:, :], None)

        block = ctx.enter_context(nc.Block())

        def expert_weights(eng, b, e):
            gu, dn = SLOTS[b]
            for g, w in enumerate((exp_w_gate, exp_w_up)):
                eng.dma_start(gu[:, g, :, :], w[0, e, :, :].rearrange("(p c) n -> p c n", c=NC)
                              ).then_inc(slot_in[b], 16)
            eng.dma_start(dn[:, :, :], exp_w_down[0, e, :, :].rearrange("(p c) n -> p c n", c=2)
                          ).then_inc(slot_in[b], 16)

        @block.sync
        def _(sp):
            sp.dma_start(X[:, 0, :], x[0, 0:P, :]).then_inc(x_in[0], 16)
            blocks = [(LAT, 448), (0, 512), (512, 512), (1024, 512)]
            for n, (c0, w) in enumerate(blocks):
                sp.dma_start(WIN[n][:, :, :], w_in[0, :, c0:c0 + w].rearrange("(p c) n -> p c n", c=NC)
                             ).then_inc(win_in[n], 16)
                if n == 0:
                    for t in range(1, NT):
                        sp.dma_start(X[:, t, :], x[0, t * P:(t + 1) * P, :]).then_inc(x_in[t], 16)
            sp.dma_start(MEMX, mem[0, :, :].rearrange("(m p) d -> p m d", p=P)).then_inc(mem_in, 16)
            for w, dst in ((mem_w_k, WK), (mem_w_v, WV)):
                sp.dma_start(dst, w[0, :, :].rearrange("(p c) n -> p c n", c=NC)).then_inc(wkv_in, 16)
            sp.dma_start(WUQ, mla_w_uq[0, :, :].rearrange("(c p) n -> p c n", c=2)).then_inc(lat_in, 16)
            sp.dma_start(WUKV, mla_w_ukv[0, :, :]).then_inc(lat_in, 16)
            sp.wait_ge(grp_done, AT_GROUP[("vmem", 1)] + 1)
            sp.dma_start(WO, w_o[0, :, :].rearrange("(c p) n -> p c n", c=NC)).then_inc(wo_in, 16)
            sp.wait_ge(grp_done, len(FRONT))
            copied(sp, AT_GROUP[("qp", NT - 1)])
            for i, g in enumerate((ln1_g, ln1_b)):
                sp.dma_start(LN1[:, i, :], g[0:1, :].partition_broadcast(P)).then_inc(ln1_in, 16)
            sp.dma_start(WQ, mem_w_q[0, :, :].rearrange("(p c) n -> p c n", c=NC)).then_inc(wq_in, 16)
            sp.dma_start(WO2, mem_w_o[0, :, :].rearrange("(c p) n -> p c n", c=4)).then_inc(wo2_in, 16)
            for i, g in enumerate((ln2_g, ln2_b)):
                sp.dma_start(LN2[:, i, :], g[0:1, :].partition_broadcast(P)).then_inc(ln2_in, 16)
            sp.dma_start(RW[:, :, :], router_w[0, :, :].rearrange("(p c) n -> p c n", c=NC)).then_inc(rw_in, 16)
            sp.wait_ge(o_done, UNIT[("m", NT - 1, HD - 1)] + 1)
            expert_weights(sp, 0, 0)
            expert_weights(sp, 1, 1)
            sp.wait_ge(aux_done, JOB[("out", NT - 1, 1)] + 1)
            for g, w in enumerate((sh_w_gate, sh_w_up)):
                sp.dma_start(SHARED[0][:, g, :, :], w[0, :, :].rearrange("(p c) n -> p c n", c=NC)
                             ).then_inc(sh_in, 16)
            sp.dma_start(SHARED[1], sh_w_down[0, :, :].rearrange("(p c) n -> p c n", c=2)).then_inc(sh_in, 16)
            sp.wait_ge(aux_done, JOB[("out2", NT - 1, 1)] + 1)
            expert_weights(sp, 2, 2)
            sp.wait_ge(ln2_done, NT)
            expert_weights(sp, 3, 3)

            def store(i, b):
                sp.wait_ge(y_act, i + 2)
                sp.wait_ge(y_dve, i + 2)
                sp.dma_start(y_rows.rearrange("(i p) d -> i p d", p=P)[bass.ds(i, 1), :, :]
                             .rearrange("i p d -> (i p) d"), Y[b % 2]).then_inc(y_free[b % 2], 16)

            n_body = N_EXP // UNROLL
            with sp.Fori(0, n_body - 1) as it:
                for b in range(UNROLL):
                    sp.wait_ge(down_done, it * UNROLL + (b + NT + 1))
                    gu, dn = SLOTS[b]
                    e = bass.ds(it * UNROLL + (b + UNROLL), 1)
                    for g, w in enumerate((exp_w_gate, exp_w_up)):
                        sp.dma_start(gu[:, g, :, :], w[0, e, :, :].rearrange("e (p c) n -> (e p) c n", c=NC)
                                     ).then_inc(slot_in[b], 16)
                    sp.dma_start(dn[:, :, :], exp_w_down[0, e, :, :].rearrange("e (p c) n -> (e p) c n", c=2)
                                 ).then_inc(slot_in[b], 16)
                    store(it * UNROLL + b, b)
            sp.wait_ge(counts_ready, 1)
            last = sp.value_load(counts_i[0:1, 2:3], min_val=n_body - 1, max_val=MAX_ITEMS // UNROLL - 1)
            with sp.If(last > n_body - 1):
                with sp.Fori(n_body - 1, last) as it:
                    for b in range(UNROLL):
                        sp.wait_ge(down_done, it * UNROLL + (b + NT + 1))
                        ex = sp.value_load(extra_i[0:1, bass.ds(it * UNROLL + (b + UNROLL - N_EXP), 1)],
                                           min_val=0, max_val=N_EXP - 1)
                        gu, dn = SLOTS[b]
                        e = bass.ds(ex, 1)
                        for g, w in enumerate((exp_w_gate, exp_w_up)):
                            sp.dma_start(gu[:, g, :, :], w[0, e, :, :].rearrange("e (p c) n -> (e p) c n", c=NC)
                                         ).then_inc(slot_in[b], 16)
                        sp.dma_start(dn[:, :, :], exp_w_down[0, e, :, :].rearrange("e (p c) n -> (e p) c n", c=2)
                                     ).then_inc(slot_in[b], 16)
                        store(it * UNROLL + b, b)
            for b in range(UNROLL):
                store(last * UNROLL + b, b)
            for t in range(NT):
                sp.wait_ge(ln3_done, t + 1)
                sp.dma_start(out[0, t * P:(t + 1) * P, :], X[:, t, :]).then_inc(out_stored, 16)
            sp.wait_ge(out_stored, 16 * NT)

        @block.gpsimd
        def _(pool):
            step = Chain(pool, pool_step)
            step(pool.memset(ident[:, :], 0.0))
            step(pool.affine_select(out=ident[:, :], in_=ident[:, :], compare_op=ALU.not_equal, fill=1.0,
                                    base=0, pattern=[[-1, P]], channel_multiplier=1))
            pool.memset(half[:, :], -0.5).then_inc(const_ready, 1)
            step(pool.memset(identb[:, :], 0.0))
            step(pool.affine_select(out=identb[:, :], in_=identb[:, :], compare_op=ALU.not_equal, fill=1.0,
                                    base=0, pattern=[[-1, P]], channel_multiplier=1))
            step(pool.memset(maskb[:, :], 0.0))
            step(pool.affine_select(out=maskb[:, :], in_=maskb[:, :], compare_op=ALU.is_ge, fill=-1e30,
                                    base=0, pattern=[[-1, P]], channel_multiplier=1))
            step(pool.memset(beforeb[:, :], 1.0))
            step(pool.affine_select(out=beforeb[:, :], in_=beforeb[:, :], compare_op=ALU.is_gt, fill=0.0,
                                    base=0, pattern=[[1, P]], channel_multiplier=-1))
            step(pool.memset(onesb[:, :], 1.0))
            step(pool.memset(tri8[:, :, :], 1.0))
            step(pool.affine_select(out=tri8[:, :, :], in_=tri8[:, :, :], compare_op=ALU.is_gt, fill=0.0,
                                    base=0, pattern=[[1, N_GRP], [-1, N_GRP]], channel_multiplier=0))
            step(pool.iota(iota_i[:, 0:N_EXP], pattern=[[P, N_EXP]], base=0, channel_multiplier=0))
            step(pool.tensor_copy(e128[:, :], iota_i[:, 0:N_EXP]))
            step(pool.iota(iota_i[:, 0:MAX_EXTRA], pattern=[[1, MAX_EXTRA]], base=0, channel_multiplier=0))
            step(pool.tensor_copy(item_no[:, :], iota_i[:, 0:MAX_EXTRA]))
            step(pool.iota(token_id[:, :], pattern=[[P, NT]], base=0, channel_multiplier=1))
            step(pool.memset(lists[:, :], NO_TOKEN))
            pool.nop().then_inc(const_ready, 1)
            pool.dma_start(token_list.rearrange("(p c) o -> p (c o)", p=P), lists[:, :]).then_inc(list_filled, 16)

            def powers(names):
                for name in names:
                    n, cols = power(name)
                    pool.wait_ge(pow_asked, n + 1)
                    pool.tensor_tensor(cols, cols, half[:, 0:cols.shape[1]], ALU.pow).then_inc(pow_done, 1)

            def store_h2(t):
                pool.wait_ge(ln2_done, t + 1)
                pool.dma_start(h2_rows[t * P:(t + 1) * P, :], X[:, t, :]).then_inc(h2_stored[t], 16)

            powers([("lat", t) for t in range(NT)])
            pool.memset(MKV[:, 0:D], 0.0).then_inc(zeros_ready, 1)
            pool.wait_ge(zeros_ready, 1)
            pool.wait_ge(lat_in, 32)
            pool.dma_start(y_rows[N_EXP * P:, :].rearrange("(i p) d -> p i d", p=P),
                           MKV[:, 0:D].unsqueeze(1).to_broadcast([P, MAX_EXTRA, D])).then_inc(rows_zeroed, 16)

            due = None
            for name in POW:
                if name[0] == "lat":
                    continue
                if name[0] == "ln3":
                    break
                powers([name])
                if due is not None:
                    store_h2(due)
                due = name[1] if name[0] == "ln2" else None
            pool.wait_ge(aux_done, JOB[("out2", NT - 1, 1)] + 1)
            store_h2(NT - 1)
            for i in range(2):
                pool.memset(XG[i], 0.0).then_inc(xg_zero, 1)
            for i in range(2):
                pool.memset(Y[i], 0.0).then_inc(y_free[i], 16)
            pool.wait_ge(list_filled, 16)
            pool.wait_ge(spos_ready, 1)
            for j in range(NT * TOP_K):
                pool.indirect_dma_start(
                    out=token_list, out_offset=bass.IndirectOffsetOnAxis(ap=spos_u[:, j:j + 1], axis=0),
                    in_=token_id[:, j // TOP_K:j // TOP_K + 1], in_offset=None,
                    bounds_check=P * LIST_COLS - 1, oob_is_err=False).then_inc(listed, 16)
            pool.wait_ge(listed, 16 * NT * TOP_K)
            pool.dma_start(lists[:, :], token_list.rearrange("(p c) o -> p (c o)", p=P)).then_inc(lists_in, 16)
            pool.wait_ge(lists_in, 16)
            for t in range(NT):
                pool.wait_ge(h2_stored[t], 16)

            def gather(i, b):
                p = b % 2
                pool.tensor_copy(idx_col[:, p:p + 1], lists[:, bass.ds(i, 1)]).then_inc(idx_ready, 1)
                pool.wait_ge(idx_ready, 1)
                pool.sem_clear(idx_ready)
                pool.indirect_dma_start(
                    out=XG[p], out_offset=None, in_=h2_rows,
                    in_offset=bass.IndirectOffsetOnAxis(ap=idx_col[:, p:p + 1], axis=0),
                    bounds_check=last_token, oob_is_err=False).then_inc(xg_in[p], 16)

            n_body = N_EXP // UNROLL
            last_token = pool.to_reg(SEQ - 1)
            last_row = pool.to_reg(MAX_ITEMS * P - 1)
            pool.wait_ge(xg_zero, 2)
            pool.wait_ge(counts_ready, 1)
            gather(0, 0)
            gather(1, 1)
            n_iter = pool.value_load(counts_i[0:1, 1:2], min_val=n_body, max_val=MAX_ITEMS // UNROLL)
            with pool.Fori(0, n_iter) as it:
                for b in range(UNROLL):
                    pool.wait_ge(xt_done, it * UNROLL + (b + 1))
                    gather(it * UNROLL + (b + 2), b)
            for p in range(2):
                pool.wait_ge(xg_in[p], n_iter * 32 + 16)
            for p in range(2):
                pool.wait_ge(y_free[p], n_iter * 32 + 16)
            pool.tensor_tensor(spare[:, :], half[:, :], half[:, :], ALU.add).then_inc(pool_step, 1)
            pool.wait_ge(pool_step, step.n + 1)

            def take_choices(rows):
                for j in range(NT * TOP_K):
                    if j >= 8:
                        pool.wait_ge(cg_used, j - 7)
                    pool.indirect_dma_start(
                        out=CG[j % 8], out_offset=None, in_=rows,
                        in_offset=bass.IndirectOffsetOnAxis(ap=pos_u[:, j:j + 1], axis=0),
                        bounds_check=last_row, oob_is_err=False).then_inc(cg_in[j % 8], 16)
                    if j % TOP_K == TOP_K - 1 and j > TOP_K:
                        powers([("ln3", j // TOP_K - 1)])
                powers([("ln3", NT - 1)])

            take_choices(y_rows)

        @block.scalar
        def _(act):
            with nc.allow_non_contiguous_dma(reason="a few hundred words"):
                act.dma_start(pos_i[:, :], positions[0, :].rearrange("(t p) -> p t", p=P)).then_inc(small_in, 16)
                for i, v in enumerate((lam_q1, lam_k1, lam_q2, lam_k2)):
                    act.dma_start(lam_in[:, i, :], v[0:1, :].partition_broadcast(P)).then_inc(small_in, 16)
                act.dma_start(gcol[:, 0:2], mla_q_norm_g[0, :].rearrange("(c p) -> p c", p=P)).then_inc(small_in, 16)
                for i, v in enumerate((mla_kv_norm_g, diff_subln_g, mla_out_norm_g)):
                    act.dma_start(gcol[:, 2 + i:3 + i], v[0, :].rearrange("(p c) -> p c", c=1)).then_inc(small_in, 16)
            act.dma_start(rbias[:, :], router_bias[0:1, :].partition_broadcast(P)).then_inc(small_in, 16)

            def copy(dst, src, s, scale=1.0):
                act.activation(dst, src, ACT.Copy, scale=scale).then_inc(s, 1)

            def drain_group(j):
                act.wait_ge(grp_done, j + 1)
                front_dest(act, j, lambda dst, src, g: copy(dst, src, grp_act, 1.0 if g is None else g))

            def lam():
                act.wait_ge(lam_dots, 1)
                act.activation(lam_sc[:, 2:4], lam_sc[:, 0:2], ACT.Exp).then_inc(lam_exps, 1)

            for j in range(len(FRONT)):
                if not on_dve(j):
                    drain_group(j)
                if FRONT[j] == ("proj", 0, 0):
                    act.wait_ge(range_ready, 1)
                    act.activation(sinT[:, :, :], sinT[:, :, :], ACT.Sin).then_inc(trig_ready, 1)
                    act.activation(cosT[:, :, :], cosT[:, :, :], ACT.Sin).then_inc(trig_ready, 1)
                    lam()

            def exps(u):
                kind = UNITS[u][0]
                n = keys(u)
                scale = {"d": SCALE_D, "m": SCALE_M, "x": SCALE_X}[kind]
                for s in steps(u):
                    act.wait_ge(negmax_ready, s + 1)
                    if s >= 4:
                        act.wait_ge(pt_done, UNIT_OF_STEP[s - 4] + 1)
                    act.activation(PB[s % 4][:, 0:n], banks[s % 4][:, 0:n], ACT.Exp,
                                   bias=MS[:, 1, s % 16:s % 16 + 1], scale=scale,
                                   accum_out=MS[:, 2, s % 16:s % 16 + 1]).then_inc(exp_done, 1)

            def pt_copy(u):
                act.wait_ge(pt_done, u + 1)
                if u >= 2:
                    act.wait_ge(o_done, u - 1)
                copy(PTB[u % 2][:, 0:keys(u)], banks[4][:, 0:keys(u)], pt_copied)

            def copy_job(job):
                j = JOB[job]
                act.wait_ge(aux_done, j + 1)
                v = banks[6 + j % 2][:, :].rearrange("p (c n) -> p c n", c=4)
                if job[0] == "mixT":
                    g = job[2]
                    copy(MIXT[:, 4 * g:4 * g + 4, :], v, aux_act, gcol[:, 5 - g:6 - g])
                elif job[0] == "hT":
                    copy(H1T[:, 0:4, :], v, aux_act)
                elif job[0] == "qc":
                    copy(QCT, v, aux_act)
                elif job[0] == "mix2T":
                    copy(OCT, v, aux_act)
                elif job[0] == "gate_up":
                    act.activation(SG[job[1] % 2], banks[6 + j % 2][:, 0:F_EXP], ACT.Silu).then_inc(sh_silu, 1)
                elif job[0] == "hidden":
                    copy(HT[job[1] % 2], banks[6 + j % 2][:, 0:F_EXP].rearrange("p (c n) -> p c n", c=2), aux_act)
                elif job[0] == "logits":
                    t0, n = (0, NT - 1) if job[1] == 0 else (NT - 1, 1)
                    act.activation(SC[:, t0:t0 + n, :], banks[6 + j % 2][:, 0:n * N_EXP]
                                   .rearrange("p (t e) -> p t e", t=n), ACT.Sigmoid).then_inc(aux_act, 1)
                else:
                    copy(AT[:, 0:4, job[1] * P:(job[1] + 1) * P], v, aux_act)

            act.wait_ge(gains_ready, 1)
            for _, what, arg in EVENTS:
                if what == "scores":
                    exps(UNIT[arg])
                elif what == "transpose":
                    pt_copy(UNIT[arg])
                elif what == "aux" and arg[1] in (None, 1) and (not job_on_dve(arg[0]) or arg[0][0] == "gate_up"):
                    copy_job(arg[0])
            act.nop().then_inc(silu_done, EARLY)
            act.nop().then_inc(ht_copied, EARLY)

            def silu(q, b):
                act.wait_ge(gu_done, q + 1)
                if not isinstance(q, int) or q >= 2:
                    act.wait_ge(h_ready, q + -1)
                act.activation(SG[b % 2], banks[b % 2][:, 0:F_EXP], ACT.Silu).then_inc(silu_done, 1)

            def ht_copy(q, b):
                act.wait_ge(ht_done, q + 1)
                if not isinstance(q, int) or q >= 2:
                    act.wait_ge(down_done, q + -1)
                copy(HT[b % 2], banks[7][:, 0:256].rearrange("p (c n) -> p c n", c=2), ht_copied)

            def xgt_copy(i, b):
                act.wait_ge(xt_done, i + 1)
                act.wait_ge(gu_done, i + 3)
                copy(XGT[b % 2][:, 0:4, :], banks[2][:, :].rearrange("p (c n) -> p c n", c=4), xt_act)

            def y_copy(it, b):
                i = it * UNROLL + b
                act.wait_ge(down_done, i + (NT + 1))
                act.wait_ge(y_free[b % 2], it * 32 + 16 * (b // 2 + 1))
                copy(Y[b % 2][:, 0:512], banks[4][:, :], y_act)

            for q in range(EARLY, NT):
                silu(q, q)
                if q > EARLY:
                    ht_copy(q - 1, q - 1)
            ht_copy(NT - 1, NT - 1)
            xgt_copy(0, 0)
            act.wait_ge(gu_done, NT)
            for i, g in enumerate((ln3_g, ln3_b)):
                act.dma_start(LN3[:, i, :], g[0:1, :].partition_broadcast(P)).then_inc(ln3_in, 16)
            act.wait_ge(counts_ready, 1)
            n_iter = act.value_load(counts_i[0:1, 1:2], min_val=N_EXP // UNROLL, max_val=MAX_ITEMS // UNROLL)
            with act.Fori(0, n_iter) as it:
                for b in range(UNROLL):
                    i = it * UNROLL + b
                    silu(it * UNROLL + (b + NT), b)
                    if b:
                        ht_copy(it * UNROLL + (b + NT - 1), b - 1)
                    xgt_copy(it * UNROLL + (b + 1), b + 1)
                    if b:
                        y_copy(it, b - 1)
                ht_copy(it * UNROLL + (2 * NT - 1), UNROLL - 1)
                y_copy(it, UNROLL - 1)

        @block.vector
        def _(dve):
            step = Chain(dve, dve_step)

            def drain_group(j):
                dve.wait_ge(grp_done, j + 1)

                def copy(dst, src, gain):
                    if gain is None:
                        dve.tensor_copy(dst, src).then_inc(grp_dve, 1)
                    else:
                        dve.tensor_scalar(dst, src, gain, None, ALU.mult).then_inc(grp_dve, 1)
                front_dest(dve, j, copy)

            def trig_ranges():
                dve.wait_ge(small_in, 16 * 10)
                step(dve.tensor_copy(pos_f[:, :], pos_i[:, :]))
                freqs = [np.float32(THETA ** (-i / n)) for n in (ROT_D, ROT_M) for i in range(0, n, 2)]
                for j, f in enumerate(freqs):
                    last = dve.tensor_scalar(sinT[:, :, j], pos_f[:, :], float(f), None, ALU.mult)
                    last.then_inc(dve_step, 1)
                    step.n += 1
                dve.wait_ge(dve_step, step.n)
                magic = 1.5 * 2.0 ** 23
                turns = TMP[:, 0:NT * n_freq].rearrange("p (t j) -> p t j", t=NT)
                step(dve.tensor_scalar(turns, sinT[:, :, :], 1.0 / (2 * math.pi), magic, ALU.mult, ALU.add))
                step(dve.tensor_scalar(turns, turns, magic, None, ALU.subtract))
                c1 = 6.28125
                c2 = float(np.float32(2 * math.pi - c1).view(np.uint32) & np.uint32(0xFFFFF000))
                c2 = float(np.uint32(int(c2)).view(np.float32))
                c3 = 2 * math.pi - c1 - c2
                for c in (c1, c2, c3):
                    step(dve.scalar_tensor_tensor(sinT[:, :, :], turns, -c, sinT[:, :, :], ALU.mult, ALU.add))
                top = 3.1415925
                step(dve.tensor_scalar(sinT[:, :, :], sinT[:, :, :], top, -top, ALU.min, ALU.max))
                step(dve.tensor_scalar(cosT[:, :, :], sinT[:, :, :], -1.0, None, ALU.mult))
                step(dve.tensor_tensor(cosT[:, :, :], cosT[:, :, :], sinT[:, :, :], ALU.min))
                dve.tensor_scalar(cosT[:, :, :], cosT[:, :, :], math.pi / 2, None, ALU.add).then_inc(range_ready, 1)

            def lam_products():
                for i in range(2):
                    step(dve.tensor_tensor_reduce(out=TMP[:, 256:256 + QK_D], in0=lam_in[:, 2 * i, :],
                                                  in1=lam_in[:, 2 * i + 1, :], scale=1.0, scalar=0.0,
                                                  op0=ALU.mult, op1=ALU.add, accum_out=lam_sc[:, i:i + 1]))
                dve.nop().then_inc(lam_dots, 1)

            def lam_final():
                dve.wait_ge(lam_exps, 1)
                step(dve.tensor_tensor(lam_sc[:, 4:5], lam_sc[:, 3:4], lam_sc[:, 2:3], ALU.subtract))
                step(dve.tensor_scalar(lam_sc[:, 5:6], lam_sc[:, 4:5], -LAM_INIT, None, ALU.add))
                dve.tensor_scalar(gcol[:, 5:6], gcol[:, 3:4], 1.0 - LAM_INIT, None, ALU.mult).then_inc(gains_ready, 1)

            def rsqrt(name):
                n, cols = power(name)
                dve.wait_ge(pow_done, n + 1)
                return cols

            def latent_norms():
                for t in range(NT):
                    copied(dve, AT_GROUP[("proj", 0, t)])
                    n, cols = power(("lat", t))
                    for i, (c0, w) in enumerate(((LAT, 256), (LAT + 256, 128))):
                        v = PR[:, t, c0:c0 + w]
                        step(dve.tensor_tensor_reduce(out=TMP[:, 0:w], in0=v, in1=v, scale=1.0 / w, scalar=RMS_EPS,
                                                      op0=ALU.mult, op1=ALU.add, accum_out=cols[:, i:i + 1]))
                    dve.nop().then_inc(pow_asked, 1)
                for t in range(NT):
                    cols = rsqrt(("lat", t))
                    for i, (c0, w) in enumerate(((LAT, 256), (LAT + 256, 128))):
                        v = PR[:, t, c0:c0 + w]
                        dve.tensor_scalar(v, v, cols[:, i:i + 1], None, ALU.mult).then_inc(lat_normed, 1)

            def rotate(a, b, cos, sin, t1, t2, t3, outa, outb, s):
                step(dve.tensor_tensor(t1, a, cos, ALU.mult))
                step(dve.tensor_tensor(t2, b, sin, ALU.mult))
                step(dve.tensor_tensor(t3, a, sin, ALU.mult))
                step(dve.tensor_tensor(outa, t1, t2, ALU.subtract))
                step(dve.tensor_tensor(t1, b, cos, ALU.mult))
                last = dve.tensor_tensor(outb, t1, t3, ALU.add)
                step.tell(last, *s)

            def temps(shape, *names):
                size = math.prod(shape)
                return [TMP[:, i * size:(i + 1) * size] for i in range(3)]

            def key_rotation():
                dve.wait_ge(trig_ready, 2)
                cos, sin = cosT[:, :, 8:40], sinT[:, :, 8:40]
                t1, t2, t3 = [v.rearrange("p (t j) -> p t j", t=NT) for v in temps((NT, 32))]
                a, b = PR[:, :, 1920:1952], PR[:, :, 1952:1984]
                rotate(a, b, cos, sin, t1, t2, t3, KP[:, :, 0:32], KP[:, :, 32:64],
                       (kp_rotated, 1))
                dve.tensor_copy(KP[:, :, 64:128], KP[:, :, 0:64]).then_inc(kp_ready, 1)

            def head_rotation():
                for t in range(NT):
                    for n in (1, 2):
                        copied(dve, AT_GROUP[("proj", n, t)])
                    v = PR[:, t, 0:1024].rearrange("p (h n) -> p h n", n=QK_D)
                    cos = cosT[:, t, 0:8].unsqueeze(1).to_broadcast([P, 16, 8])
                    sin = sinT[:, t, 0:8].unsqueeze(1).to_broadcast([P, 16, 8])
                    t1, t2, t3 = [w.rearrange("p (h j) -> p h j", j=8) for w in temps((16, 8))]
                    rotate(v[:, :, 0:8], v[:, :, 8:16], cos, sin, t1, t2, t3, v[:, :, 0:8], v[:, :, 8:16],
                           (rope_ready, t + 1))

            def query_rotation(t, j):
                dve.wait_ge(grp_done, j + 1)
                v = banks[j % 8][:, 0:HD * ROPE].rearrange("p (h n) -> p h n", n=ROPE)
                o = PR[:, t, LAT:LAT + HD * ROPE].rearrange("p (h n) -> p h n", n=ROPE)
                cos = cosT[:, t, 8:40].unsqueeze(1).to_broadcast([P, HD, 32])
                sin = sinT[:, t, 8:40].unsqueeze(1).to_broadcast([P, HD, 32])
                t1, t2, t3 = [w.rearrange("p (h j) -> p h j", j=32) for w in temps((HD, 32))]
                rotate(v[:, :, 0:32], v[:, :, 32:64], cos, sin, t1, t2, t3, o[:, :, 0:32], o[:, :, 32:64],
                       (grp_dve, sum(map(on_dve, range(j + 1)))))

            for j in range(len(FRONT)):
                if FRONT[j][0] == "qp":
                    query_rotation(FRONT[j][1], j)
                elif on_dve(j):
                    drain_group(j)
                if FRONT[j] == ("proj", 0, 1):
                    trig_ranges()
                    lam_products()
                if FRONT[j] == ("proj", 0, 3):
                    lam_final()
                    latent_norms()
                    key_rotation()
                if FRONT[j] == ("proj", 3, 1):
                    head_rotation()

            def maxima(u):
                kind = UNITS[u][0]
                scale = {"d": SCALE_D, "m": SCALE_M, "x": SCALE_X}[kind]
                for s in steps(u):
                    c = slice(s % 16, s % 16 + 1)
                    dve.wait_ge(scores_done, s + 1)
                    step(dve.reduce_max(MS[:, 0, c], banks[s % 4][:, 0:keys(u)], AX.X))
                    dve.tensor_scalar(MS[:, 1, c], MS[:, 0, c], -scale, None, ALU.mult).then_inc(negmax_ready, 1)

            def probabilities(u):
                s0 = STEP0[u]
                c0 = slice(s0 % 16, s0 % 16 + 1)
                if UNITS[u][0] != "d":
                    dve.wait_ge(exp_done, s0 + 1)
                    dve.reciprocal(MS[:, 3, c0], MS[:, 2, c0]).then_inc(mixed_p, 1)
                    return
                c1 = slice((s0 + 1) % 16, (s0 + 1) % 16 + 1)
                n = keys(u)
                dve.wait_ge(exp_done, s0 + 2)
                dve.reciprocal(MS[:, 3, c0], MS[:, 2, c0]).then_inc(dve_step, 1)
                step.n += 1
                step(dve.reciprocal(MS[:, 3, c1], MS[:, 2, c1]))
                step(dve.tensor_scalar(PB[(s0 + 1) % 4][:, 0:n], PB[(s0 + 1) % 4][:, 0:n], MS[:, 3, c1],
                                       lam_sc[:, 5:6], ALU.mult, ALU.mult))
                dve.scalar_tensor_tensor(PB[s0 % 4][:, 0:n], PB[s0 % 4][:, 0:n], MS[:, 3, c0],
                                         PB[(s0 + 1) % 4][:, 0:n], ALU.mult, ALU.add).then_inc(mixed_p, 1)

            def values(u):
                kind, t, h = UNITS[u]
                o = banks[5][:, 0:P]
                s0 = STEP0[u]
                r = MS[:, 3, s0 % 16:s0 % 16 + 1]
                dve.wait_ge(o_done, u + 1)
                if kind == "x":
                    dve.wait_ge(mixed_p, u + 1)
                    if t and h == 0:
                        dve.wait_ge(aux_done, JOB[("mix2T", t - 1)] + 1)
                    dve.tensor_scalar(OC[:, h, :], o, r, None, ALU.mult).then_inc(o_copied, 1)
                    return
                g = h + (4 if kind == "m" else 0)
                dst = O[t % 2][:, g, :]
                if t >= 2 and g == 0:
                    dve.wait_ge(aux_done, JOB[("mixT", t - 2, 1)] + 1)
                if kind == "d":
                    step(dve.tensor_copy(dst, o))
                else:
                    dve.wait_ge(mixed_p, u + 1)
                    step(dve.tensor_scalar(dst, o, r, None, ALU.mult))
                n, cols = power(("mix", t))
                dve.tensor_tensor_reduce(out=SQ, in0=dst, in1=dst, scale=1.0 / P, scalar=RMS_EPS,
                                         op0=ALU.mult, op1=ALU.add, accum_out=cols[:, g:g + 1]).then_inc(o_copied, 1)
                dve.wait_ge(o_copied, u + 1)
                if g == 7:
                    dve.nop().then_inc(pow_asked, 1)

            def norm_heads(t):
                cols = rsqrt(("mix", t))
                v = O[t % 2]
                dve.tensor_tensor(v, v, cols.unsqueeze(2).to_broadcast([P, 8, P]), ALU.mult).then_inc(o_normed, 1)

            def norm_stats(name, t):
                for i in range(2):
                    step(dve.bn_stats(ST[:, i, :], X[:, t, i * 512:(i + 1) * 512]))
                mv = MV[:, 4 * (name == "ln2"):]
                step(dve.bn_aggr(mv[:, 0:2], ST[:, :, :]))
                n, cols = power((name, t))
                dve.tensor_scalar(cols, mv[:, 1:2], LN_EPS, None, ALU.add).then_inc(pow_asked, 1)

            def norm_rows(name, t, rows, loaded, done):
                v = X[:, t, :]
                cols = rsqrt((name, t))
                mv = MV[:, 4 * (name == "ln2"):]
                step(dve.tensor_scalar(mv[:, 2:3], mv[:, 0:1], cols, -1.0, ALU.mult, ALU.mult))
                step(dve.tensor_scalar(v, v, cols, mv[:, 2:3], ALU.mult, ALU.add))
                dve.wait_ge(loaded, 32)
                step(dve.tensor_tensor(v, v, rows[:, 0, :], ALU.mult))
                dve.tensor_tensor(v, v, rows[:, 1, :], ALU.add).then_inc(done, 1)
                dve.wait_ge(done, t + 1)

            def copy_job(job):
                j = JOB[job]
                dve.wait_ge(aux_done, j + 1)
                bank = banks[6 + j % 2]
                t, i = job[1], job[-1]
                if job[0] in ("out", "out2", "down"):
                    if job[0] == "down":
                        dve.wait_ge(h2_stored[t], 16)
                    v = X[:, t, i * 512:(i + 1) * 512]
                    step.tell(dve.scalar_tensor_tensor(v, v, ALPHA, bank[:, :], ALU.mult, ALU.add),
                              aux_dve, sum(map(job_on_dve, JOBS[:j + 1])))
                elif job[0] == "gate_up":
                    dve.wait_ge(sh_silu, t + 1)
                    dve.tensor_tensor(HS[t % 2], SG[t % 2], bank[:, F_EXP:2 * F_EXP], ALU.mult).then_inc(aux_dve, 1)
                else:
                    dst = H1T[:, 4:8, :] if job[0] == "hT" else AT[:, 4:8, t * P:(t + 1) * P]
                    dve.tensor_copy(dst, bank[:, :].rearrange("p (c n) -> p c n", c=4)).then_inc(aux_dve, 1)

            for _, what, arg in EVENTS:
                if what == "scores":
                    maxima(UNIT[arg])
                elif what == "probabilities":
                    probabilities(UNIT[arg])
                elif what == "values":
                    values(UNIT[arg])
                elif what == "norm_heads":
                    norm_heads(arg)
                elif what in ("ln1_stats", "ln2_stats"):
                    norm_stats(what[:3], arg)
                elif what == "ln1_rows":
                    norm_rows("ln1", arg, LN1, ln1_in, ln1_done)
                elif what == "ln2_rows":
                    norm_rows("ln2", arg, LN2, ln2_in, ln2_done)
                elif what == "aux" and arg[1] in (None, 1) and job_on_dve(arg[0]):
                    copy_job(arg[0])

            def hidden(q, b):
                dve.wait_ge(silu_done, q + 1)
                if not isinstance(q, int) or q >= 2:
                    dve.wait_ge(ht_done, q + -1)
                dve.tensor_tensor(HS[b % 2], SG[b % 2], banks[b % 2][:, F_EXP:2 * F_EXP], ALU.mult).then_inc(h_ready, 1)

            def small(i, w=NT * N_GRP):
                return R8[:, i, 0:w]

            def grouped(v):
                return v.rearrange("p t (g e) -> p (t g) e", g=N_GRP)

            def per_group(v):
                return v.unsqueeze(2).to_broadcast([P, NT * N_GRP, N_GRP])

            dve.nop().then_inc(h_ready, EARLY)
            job_copied(dve, ("logits", 0))
            job_copied(dve, ("logits", 1))
            big = 1e30
            step(dve.tensor_tensor(CH[:, :, :], SC[:, :, :], rbias[:, :].unsqueeze(1).to_broadcast([P, NT, N_EXP]),
                                   ALU.add))
            step(dve.reduce_max(small(0), grouped(CH), AX.X))
            step(dve.tensor_tensor(grouped(T1), grouped(CH), per_group(small(0)), ALU.is_equal))
            step(dve.tensor_reduce(small(1), grouped(T1), AX.X, ALU.add))
            step(dve.scalar_tensor_tensor(T2[:, :, :], T1[:, :, :], -big, CH[:, :, :], ALU.mult, ALU.add))
            step(dve.reduce_max(small(2), grouped(T2), AX.X))
            step(dve.tensor_scalar(small(1), small(1), 1.5, None, ALU.is_ge))
            step(dve.tensor_scalar(small(1), small(1), -1.0, big, ALU.add, ALU.mult))
            step(dve.tensor_tensor(small(1), small(1), small(0), ALU.add))
            step(dve.tensor_tensor(small(2), small(2), small(1), ALU.max))
            step(dve.tensor_tensor(small(0), small(0), small(2), ALU.add))
            gs = small(0).rearrange("p (t g) -> p t g", t=NT)
            for t in range(NT):
                mine = gs[:, t, :].unsqueeze(2).to_broadcast([P, N_GRP, N_GRP])
                others = gs[:, t, :].unsqueeze(1).to_broadcast([P, N_GRP, N_GRP])
                a = T1[:, t, :].rearrange("p (g k) -> p g k", g=N_GRP)
                b = T2[:, t, :].rearrange("p (g k) -> p g k", g=N_GRP)
                step(dve.tensor_tensor(a, others, mine, ALU.is_gt))
                step(dve.tensor_tensor(b, others, mine, ALU.is_equal))
                step(dve.tensor_tensor(b, b, tri8[:, :, :], ALU.mult))
            step(dve.tensor_tensor(T1[:, :, :], T1[:, :, :], T2[:, :, :], ALU.add))
            step(dve.tensor_reduce(small(3), grouped(T1), AX.X, ALU.add))
            step(dve.tensor_scalar(small(3), small(3), TOPK_GRP - 0.5, None, ALU.is_le))
            step(dve.tensor_tensor(grouped(MC), grouped(CH), per_group(small(3)), ALU.mult))
            step(dve.tensor_scalar(small(4), small(3), -1.0, big, ALU.add, ALU.mult))
            step(dve.tensor_tensor(grouped(MC), grouped(MC), per_group(small(4)), ALU.add))
            for t in range(NT):
                step(dve.max(R8[:, 5, t * 8:t * 8 + 8], MC[:, t, :]))
                step(dve.match_replace(T1[:, t, :], R8[:, 5, t * 8:t * 8 + 8], MC[:, t, :], -2.0 * big))
            step(dve.tensor_scalar(SELM[:, :, :], T1[:, :, :], -1.5 * big, None, ALU.is_le))
            dve.tensor_copy(selb[:, :, :], SELM[:, :, :]).then_inc(sel_ready, 1)
            hidden(EARLY, EARLY)
            step(dve.tensor_tensor(GATE[:, :, :], SC[:, :, :], SELM[:, :, :], ALU.mult))
            step(dve.tensor_reduce(R8[:, 6, 0:NT], GATE[:, :, :], AX.X, ALU.add))
            step(dve.reciprocal(R8[:, 6, 4:4 + NT], R8[:, 6, 0:NT]))
            for t in range(NT):
                step(dve.tensor_scalar(GATE[:, t, :], GATE[:, t, :], R8[:, 6, 4 + t:5 + t], ROUTED_SCALE,
                                       ALU.mult, ALU.mult))
            dve.wait_ge(rank_done, 1)
            ranks = banks[5][:, 0:NT * N_EXP].rearrange("p (t e) -> p t e", t=NT)
            size = banks[5][:, NT * N_EXP:(NT + 1) * N_EXP]
            ex, cum, start, base, tmp = (ST64[:, i, :] for i in range(5))
            step(dve.tensor_scalar(ex, size, P + 0.5, None, ALU.is_ge))
            for lim in (2 * P, 3 * P):
                step(dve.scalar_tensor_tensor(ex, size, lim + 0.5, ex, ALU.is_ge, ALU.add))
            step(dve.memset(tmp, 0.0))
            step(dve.tensor_tensor_scan(cum, ex, tmp, 0.0, ALU.add, ALU.add))
            step(dve.tensor_tensor(start, cum, ex, ALU.subtract))
            step(dve.tensor_scalar(base, start, N_EXP - 1.0, float(P), ALU.add, ALU.mult))
            step(dve.tensor_tensor(tmp, e128[:, :], base, ALU.subtract))
            wide = lambda v: v.unsqueeze(1).to_broadcast([P, NT, N_EXP])
            step(dve.tensor_scalar(T1[:, :, :], ranks, P - 0.5, None, ALU.is_le))
            step(dve.tensor_tensor(T1[:, :, :], T1[:, :, :], wide(tmp), ALU.mult))
            step(dve.tensor_tensor(T1[:, :, :], T1[:, :, :], wide(base), ALU.add))
            step(dve.scalar_tensor_tensor(T1[:, :, :], ranks, 1.0, T1[:, :, :], ALU.add, ALU.add))
            step(dve.tensor_tensor(POSM[:, :, :], T1[:, :, :], SELM[:, :, :], ALU.mult))
            posk = R8[:, 7, :]
            for t in range(NT):
                step(dve.max(posk[:, t * 8:t * 8 + 8], POSM[:, t, :]))
            step(dve.tensor_scalar(pos_u[:, :], posk, -1.0, None, ALU.add))
            item_u, slot_u = R8[:, 8, :].bitcast(U32), R8[:, 9, :].bitcast(U32)
            step(dve.tensor_scalar(item_u, pos_u[:, :], 7, None, ALU.logical_shift_right))
            step(dve.tensor_scalar(slot_u, pos_u[:, :], P - 1, None, ALU.bitwise_and))
            step(dve.tensor_copy(R8[:, 10, :], item_u))
            step(dve.tensor_copy(R8[:, 11, :], slot_u))
            dve.scalar_tensor_tensor(spos_u[:, :], R8[:, 11, :], float(LIST_COLS), R8[:, 10, :], ALU.mult,
                                     ALU.add).then_inc(spos_ready, 1)
            step(dve.tensor_scalar(counts_i[:, 0:1], cum[:, N_EXP - 1:N_EXP], float(N_EXP + UNROLL - 1), None, ALU.add))
            step(dve.tensor_scalar(counts_i[:, 1:2], counts_i[:, 0:1], 2, None, ALU.logical_shift_right))
            step(dve.tensor_scalar(counts_i[:, 2:3], counts_i[:, 1:2], -1.0, None, ALU.add))
            for k in range(MAX_EXTRA // 4):
                four = T2[:, :, :]
                step(dve.tensor_tensor(four, wide(cum), item_no[:, 4 * k:4 * k + 4].unsqueeze(2).to_broadcast([P, 4, N_EXP]),
                                       ALU.is_le))
                step(dve.tensor_reduce(R8[:, 5, 4 * k:4 * k + 4], four, AX.X, ALU.add))
            step(dve.tensor_scalar(extra_i[:, :], R8[:, 5, 0:MAX_EXTRA], N_EXP - 1.0, None, ALU.min))
            dve.nop().then_inc(counts_ready, 1)

            def gate_of_choices():
                for t in range(NT):
                    for k in range(TOP_K):
                        j = t * TOP_K + k
                        step(dve.scalar_tensor_tensor(T2[:, t, :], POSM[:, t, :], posk[:, j:j + 1], GATE[:, t, :],
                                                      ALU.is_equal, ALU.mult, accum_out=gk[:, j:j + 1]))

            def xgt_copy(i, b):
                dve.wait_ge(xt_done, i + 1)
                dve.wait_ge(gu_done, i + 3)
                dve.tensor_copy(XGT[b % 2][:, 4:8, :], banks[3][:, :].rearrange("p (c n) -> p c n", c=4)).then_inc(xt_dve, 1)

            def y_copy(it, b):
                i = it * UNROLL + b
                dve.wait_ge(down_done, i + (NT + 1))
                dve.wait_ge(y_free[b % 2], it * 32 + 16 * (b // 2 + 1))
                dve.tensor_copy(Y[b % 2][:, 512:1024], banks[5][:, :]).then_inc(y_dve, 1)

            def shared_add(t):
                dve.wait_ge(down_done, t + 1)
                dve.wait_ge(h2_stored[t], 16)
                for i in range(2):
                    v = X[:, t, i * 512:(i + 1) * 512]
                    dve.scalar_tensor_tensor(v, v, ALPHA, banks[4 + i][:, :], ALU.mult, ALU.add
                                             ).then_inc(sh_added if t < NT - 1 else (y_act, y_dve)[i], 1)

            for q in range(EARLY, NT):
                if q > EARLY:
                    hidden(q, q)
                    shared_add(q - 1)
            gate_of_choices()
            shared_add(NT - 1)
            xgt_copy(0, 0)
            n_iter = dve.value_load(counts_i[0:1, 1:2], min_val=N_EXP // UNROLL, max_val=MAX_ITEMS // UNROLL)
            with dve.Fori(0, n_iter) as it:
                for b in range(UNROLL):
                    hidden(it * UNROLL + (b + NT), b)
                    xgt_copy(it * UNROLL + (b + 1), b + 1)
                    if b:
                        y_copy(it, b - 1)
                y_copy(it, UNROLL - 1)
            dve.wait_ge(y_act, 1)
            dve.wait_ge(y_dve, 1)
            for t in range(NT):
                for k in range(TOP_K):
                    j = t * TOP_K + k
                    dve.wait_ge(cg_in[j % 8], 16 * (j // 8 + 1))
                    dve.scalar_tensor_tensor(X[:, t, :], CG[j % 8], gk[:, j:j + 1], X[:, t, :], ALU.mult,
                                             ALU.add).then_inc(cg_used, 1)
                    dve.wait_ge(cg_used, j + 1)
                norm_stats("ln3", t)
                norm_rows("ln3", t, LN3, ln3_in, ln3_done)

        @block.tensor
        def _(pe):
            pe.wait_ge(const_ready, 2)

            def product(out_ap, pairs):
                for c, (a, b) in enumerate(pairs):
                    last = nc.tensor.matmul(out_ap, a, b, start=(c == 0), stop=(c == len(pairs) - 1))
                return last

            def transposes(bank, blocks, width=P):
                for c, a in enumerate(blocks):
                    last = nc.tensor.transpose(bank[:, c * P:(c + 1) * P], a, ident[:, :])
                return last

            for j, g in enumerate(FRONT):
                bank = banks[j % 8]
                if j >= 8:
                    copied(pe, j - 8)
                kind = g[0]
                if kind == "xT":
                    pe.wait_ge(x_in[g[1]], 16)
                    v = X[:, g[1], :].rearrange("p (m c) -> p c m", c=NC)
                    last = transposes(bank, [v[:, 4 * g[2] + c, :] for c in range(4)])
                elif kind == "proj":
                    n, t = g[1:]
                    if n == 0:
                        for h in range(2):
                            copied(pe, AT_GROUP[("xT", t, h)])
                    if t == 0:
                        pe.wait_ge(win_in[n], 16)
                    w = 448 if n == 0 else 512
                    last = product(bank[:, 0:w], [(AT[:, c, t * P:(t + 1) * P], WIN[n][:, c, :]) for c in range(NC)])
                elif kind in ("cqT", "ckvT"):
                    pe.wait_ge(lat_normed, 2 * NT)
                    c0 = LAT + 128 * (2 if kind == "ckvT" else g[1])
                    last = transposes(bank, [PR[:, t, c0:c0 + P] for t in range(NT)])
                elif kind == "kpT":
                    pe.wait_ge(kp_ready, 1)
                    last = transposes(bank, [KP[:, t, :] for t in range(NT)])
                elif kind == "qkT":
                    pe.wait_ge(rope_ready, NT)
                    last = transposes(bank, [PR[:, t, g[1] * P:(g[1] + 1) * P] for t in range(NT)])
                elif kind == "memT":
                    pe.wait_ge(mem_in, 16)
                    v = MEMX[:, g[1], :].rearrange("p (m c) -> p c m", c=NC)
                    last = transposes(bank, [v[:, 4 * g[2] + c, :] for c in range(4)])
                elif kind == "kmem":
                    pe.wait_ge(wkv_in, 32)
                    for i in range(4):
                        copied(pe, AT_GROUP[("memT", i // 2, i % 2)])
                    for i in range(2):
                        h = 2 * g[1] + i
                        last = product(bank[:, i * N_MEM:(i + 1) * N_MEM],
                                       [(WK[:, c, h * P:(h + 1) * P], MEMT[:, c, :]) for c in range(NC)])
                elif kind == "vmem":
                    last = product(bank[:, :], [(MEMT[:, c, g[1] * P:(g[1] + 1) * P], WV[:, c, :]) for c in range(NC)])
                elif kind == "qn":
                    pe.wait_ge(lat_in, 32)
                    for i in range(2):
                        copied(pe, AT_GROUP[("cqT", i)])
                    c0 = g[1] * (NOPE + ROPE)
                    last = product(bank[:, :], [(WUQ[:, c, c0:c0 + NOPE], CQT[:, c, :]) for c in range(2)])
                elif kind == "kn":
                    copied(pe, AT_GROUP[("ckvT",)])
                    c0 = g[1] * 2 * P
                    last = product(bank[:, :], [(WUKV[:, c0:c0 + P], CKVT)])
                elif kind == "vm":
                    v = WUKV.rearrange("p (h k n) -> p h k n", h=HD, k=2)[:, :, 1, :]
                    last = product(bank[:, :], [(CKVT[:, g[1] * P:(g[1] + 1) * P], v)])
                elif kind == "qp":
                    v = WUQ.rearrange("p c (h n) -> p c h n", h=HD)
                    last = product(bank[:, 0:HD * ROPE], [(CQT[:, c, g[1] * P:(g[1] + 1) * P], v[:, c, :, NOPE:NOPE + ROPE])
                                                          for c in range(2)])
                elif kind == "qpT":
                    for t in range(NT):
                        copied(pe, AT_GROUP[("qp", t)])
                    c0 = LAT + g[1] * P
                    last = transposes(bank, [PR[:, t, c0:c0 + P] for t in range(NT)])
                last.then_inc(grp_done, 1)
            for j in range(len(FRONT) - 8, len(FRONT)):
                copied(pe, j)

            def scores(u):
                kind, t, h = UNITS[u]
                q = slice(t * P, (t + 1) * P)
                n = keys(u)
                if kind == "x" and h == 0:
                    job_copied(pe, ("qc", t))
                for k, s in enumerate(steps(u)):
                    if s >= 4:
                        pe.wait_ge(exp_done, s - 3)
                    bank = banks[s % 4]
                    if kind == "d":
                        r = slice(k * QK_D, (k + 1) * QK_D)
                        pairs = [(QDT[r, h, q], KDT[r, h, 0:n])]
                    elif kind == "m":
                        r = slice((h % 2) * ROPE, (h % 2 + 1) * ROPE)
                        pairs = [(QNT[:, h, q], KNT[:, h, 0:n]), (QPT[r, h // 2, q], KPT[r, 0:n])]
                    else:
                        pairs = [(QCT[:, h, :], KMT[:, h, :])]
                    for c, (a, b) in enumerate(pairs):
                        last = nc.tensor.matmul(bank[:, 0:n], a, b, start=(c == 0),
                                                stop=(kind == "x"), skip_group_check=True)
                    if kind != "x":
                        last = nc.tensor.matmul(bank[:, n - P:n], identb[:, :], maskb[:, :], start=False, stop=True,
                                                skip_group_check=True)
                    last.then_inc(scores_done, 1)

            def p_transposes(u):
                pe.wait_ge(mixed_p, u + 1)
                if u >= 1:
                    pe.wait_ge(pt_copied, u)
                p = PB[STEP0[u] % 4]
                transposes(banks[4], [p[:, c * P:(c + 1) * P] for c in range(keys(u) // P)]).then_inc(pt_done, 1)

            def values(u):
                kind, t, h = UNITS[u]
                pe.wait_ge(pt_copied, u + 1)
                if u >= 1:
                    pe.wait_ge(o_copied, u)
                pt = PTB[u % 2]
                if kind == "d":
                    v = [PR[:, c, 1024 + h * P:1024 + (h + 1) * P] for c in range(t + 1)]
                elif kind == "m":
                    v = [VML[:, c, h * P:(h + 1) * P] for c in range(t + 1)]
                else:
                    v = [VM[:, c, h * P:(h + 1) * P] for c in range(2)]
                product(banks[5][:, 0:P],
                        [(pt[:, c * P:(c + 1) * P], b) for c, b in enumerate(v)]).then_inc(o_done, 1)

            def aux_job(job, part):
                kind, t = job[:2]
                j = JOB[job]
                bank = banks[6 + j % 2]
                if j >= 2 and part in (None, 0):
                    job_copied(pe, JOBS[j - 2])
                if kind == "mixT":
                    pe.wait_ge(o_normed, t + 1)
                    last = transposes(bank, [O[t % 2][:, 4 * job[2] + c, :] for c in range(4)])
                elif kind == "out":
                    if part == 0:
                        for g in range(2):
                            job_copied(pe, ("mixT", t, g))
                        pe.wait_ge(wo_in, 16)
                    n0 = job[2] * 512
                    for c in range(4 * part, 4 * part + 4):
                        last = nc.tensor.matmul(bank[:, :], MIXT[:, c, :], WO[:, c, n0:n0 + 512],
                                                start=(c == 0), stop=(c == NC - 1))
                elif kind in ("hT", "h2T"):
                    pe.wait_ge(ln1_done if kind == "hT" else ln2_done, t + 1)
                    v = X[:, t, :].rearrange("p (m c) -> p c m", c=NC)
                    last = transposes(bank, [v[:, 4 * job[2] + c, :] for c in range(4)])
                elif kind == "qc":
                    if part == 0:
                        for g in range(2):
                            job_copied(pe, ("hT", t, g))
                        pe.wait_ge(wq_in, 16)
                    for h in (2 * part, 2 * part + 1):
                        last = product(bank[:, h * P:(h + 1) * P],
                                       [(WQ[:, c, h * P:(h + 1) * P], H1T[:, c, :]) for c in range(NC)])
                elif kind == "mix2T":
                    pe.wait_ge(o_copied, UNIT[("x", t, HD - 1)] + 1)
                    last = transposes(bank, [OC[:, c, :] for c in range(4)])
                elif kind == "out2":
                    job_copied(pe, ("mix2T", t))
                    pe.wait_ge(wo2_in, 16)
                    n0 = job[2] * 512
                    last = product(bank[:, :], [(OCT[:, c, :], WO2[:, c, n0:n0 + 512]) for c in range(4)])
                elif kind == "gate_up":
                    for g in range(2):
                        job_copied(pe, ("h2T", t, g))
                    pe.wait_ge(sh_in, 48)
                    last = gate_up(bank, [AT[:, c, t * P:(t + 1) * P] for c in range(NC)], SHARED[0])
                elif kind == "hidden":
                    job_copied(pe, ("gate_up", t))
                    v = HS[t % 2].rearrange("p (m c) -> p c m", c=2)
                    last = transposes(bank, [v[:, c, :] for c in range(2)])
                elif kind == "down":
                    job_copied(pe, ("hidden", t))
                    n0 = job[2] * 512
                    last = product(bank[:, :], [(HT[t % 2][:, c, :], SHARED[1][:, c, n0:n0 + 512]) for c in range(2)])
                elif kind == "logits":
                    pe.wait_ge(rw_in, 16)
                    t0, n = (0, NT - 1) if job[1] == 0 else (NT - 1, 1)
                    for t in range(t0, t0 + n):
                        for g in range(2):
                            job_copied(pe, ("h2T", t, g))
                        last = product(bank[:, (t - t0) * N_EXP:(t - t0 + 1) * N_EXP],
                                       [(AT[:, c, t * P:(t + 1) * P], RW[:, c, :]) for c in range(NC)])
                if part in (None, 1):
                    last.then_inc(aux_done, 1)

            def gate_up(bank, xt, w):
                return product(bank[:, :], [(xt[c], w[:, :, c, :]) for c in range(NC)])

            for _, what, arg in EVENTS:
                if what == "scores":
                    scores(UNIT[arg])
                elif what == "transpose":
                    p_transposes(UNIT[arg])
                elif what == "values":
                    values(UNIT[arg])
                elif what == "aux":
                    aux_job(*arg)
            pe.wait_ge(exp_done, STEP0[-1] + 1)

            for j in JOBS[-2:]:
                job_copied(pe, j)
            pe.wait_ge(pt_copied, len(UNITS))
            pe.nop().then_inc(gu_done, EARLY)
            pe.nop().then_inc(ht_done, EARLY)
            pe.nop().then_inc(down_done, EARLY)

            def h_transpose(q, b):
                pe.wait_ge(h_ready, q + 1)
                pe.wait_ge(ht_copied, q)
                v = HS[b % 2].rearrange("p (m c) -> p c m", c=2)
                transposes(banks[7], [v[:, c, :] for c in range(2)]).then_inc(ht_done, 1)

            def down(q, b, w):
                pe.wait_ge(ht_copied, q + 1)
                for i in range(2):
                    last = product(banks[4 + i][:, :], [(HT[b % 2][:, c, :], w[:, c, i * 512:(i + 1) * 512])
                                                        for c in range(2)])
                last.then_inc(down_done, 1)

            def xg_transpose(i, b, arrivals):
                pe.wait_ge(xg_in[b % 2], arrivals)
                v = XG[b % 2].rearrange("p (m c) -> p c m", c=NC)
                for g in range(2):
                    last = transposes(banks[2 + g], [v[:, 4 * g + c, :] for c in range(4)])
                last.then_inc(xt_done, 1)

            def shared_gate_up(t):
                if t >= 2:
                    pe.wait_ge(h_ready, t - 1)
                gate_up(banks[t % 2], [AT[:, c, t * P:(t + 1) * P] for c in range(NC)], SHARED[0]).then_inc(gu_done, 1)

            pe.wait_ge(sh_in, 48)
            shared_gate_up(EARLY)
            pe.wait_ge(sel_ready, 1)
            for t in range(NT):
                pairs = [(beforeb[:, :], selb[:, t, :])] + [(onesb[:, :], selb[:, k, :]) for k in range(t)]
                product(banks[5][:, t * N_EXP:(t + 1) * N_EXP], pairs)
            product(banks[5][:, NT * N_EXP:(NT + 1) * N_EXP],
                    [(onesb[:, :], selb[:, k, :]) for k in range(NT)]).then_inc(rank_done, 1)
            for t in range(EARLY + 1, NT + 1):
                if t < NT:
                    shared_gate_up(t)
                h_transpose(t - 1, t - 1)
                if t == EARLY + 1:
                    pe.wait_ge(spos_ready, 1)
                else:
                    pe.wait_ge(sh_added, 2 * (t - 1 - EARLY))
                down(t - 1, t - 1, SHARED[1])
            xg_transpose(0, 0, 16)
            pe.wait_ge(counts_ready, 1)
            n_iter = pe.value_load(counts_i[0:1, 1:2], min_val=N_EXP // UNROLL, max_val=MAX_ITEMS // UNROLL)
            with pe.Fori(0, n_iter) as it:
                def down_item(b):
                    pe.wait_ge(y_act, it * UNROLL + (b + 1))
                    pe.wait_ge(y_dve, it * UNROLL + (b + 1))
                    down(it * UNROLL + (b + NT), b, SLOTS[b][1])

                for b in range(UNROLL):
                    pe.wait_ge(slot_in[b], it * 48 + 48)
                    pe.wait_ge(xt_act, it * UNROLL + (b + 1))
                    pe.wait_ge(xt_dve, it * UNROLL + (b + 1))
                    pe.wait_ge(h_ready, it * UNROLL + (b + NT - 1))
                    gate_up(banks[b % 2], [XGT[b % 2][:, c, :] for c in range(NC)], SLOTS[b][0]).then_inc(gu_done, 1)
                    if b:
                        h_transpose(it * UNROLL + (b + NT - 1), b - 1)
                    xg_transpose(None, b + 1, it * 32 + 16 * ((b + 1) // 2 + 1))
                    if b:
                        down_item(b - 1)
                h_transpose(it * UNROLL + (2 * NT - 1), UNROLL - 1)
                down_item(UNROLL - 1)


_INS = ["x", "mem", "positions", "w_in", "lam_q1", "lam_k1", "lam_q2", "lam_k2", "diff_subln_g", "mla_q_norm_g",
        "mla_w_uq", "mla_kv_norm_g", "mla_w_ukv", "mla_out_norm_g", "w_o", "ln1_g", "ln1_b", "mem_w_q", "mem_w_k",
        "mem_w_v", "mem_w_o", "ln2_g", "ln2_b", "router_w", "router_bias", "exp_w_gate", "exp_w_up", "exp_w_down",
        "sh_w_gate", "sh_w_up", "sh_w_down", "ln3_g", "ln3_b"]


def kernel(**inputs):
    import concourse.bacc as bacc
    from concourse.bass_utils import run_bass_kernel_spmd

    nc = bacc.Bacc("TRN2", target_bir_lowering=False, num_devices=1)
    arrays, args = {}, []
    for name in _INS:
        a = np.ascontiguousarray(inputs[name])
        arrays[f"in_{name}"] = a
        args.append(nc.dram_tensor(f"in_{name}", a.shape, mybir.dt.from_np(a.dtype), kind="ExternalInput").ap())
    args.append(nc.dram_tensor("layer_out", (1, SEQ, D), F32, kind="ExternalOutput").ap())
    build(nc, *args)
    r = run_bass_kernel_spmd(nc, [arrays], core_ids=[0])
    return r.results[0]["layer_out"]
```

```python
import math
from contextlib import ExitStack

import concourse.bass as bass
import numpy as np
from concourse import mybir

F32 = mybir.dt.float32
BF16 = mybir.dt.bfloat16
I32 = mybir.dt.int32
U32 = mybir.dt.uint32
ALU = mybir.AluOpType
ACT = mybir.ActivationFunctionType
AX = mybir.AxisListType

P = 128
SEQ = 512
D = 1024
NT = SEQ // P
NC = D // P
N_MEM = 256
IN_COLS = 1984
LAT = 1536
THETA = 500000.0
ROT_D = 16
ROT_M = 64
HD = 4
QK_D = 64
NOPE = 128
ROPE = 64
N_EXP = 64
F_EXP = 256
N_GRP = 8
TOPK_GRP = 4
TOP_K = 8
ROUTED_SCALE = 2.5
ALPHA = 2.0 ** 0.25
LAM_INIT = 0.8 - 0.6 * math.exp(-0.3 * 0)
LN_EPS = 1e-5
RMS_EPS = 1e-6
SCALE_D = QK_D ** -0.5
SCALE_M = (NOPE + ROPE) ** -0.5
SCALE_X = 128 ** -0.5

OUT0, LN1A, LN1B, LN1C, HTA, QCA = 10.2, 13.3, 14.95, 15.95, 16.5, 17.6
BIAS_AFTER = 0.35
XU, M2T = 20.5, 25.15
OUT2_AT = ((27.5, 29.5, 29.7, 30.7), (38.4, 39.3, 39.6, 40.7), (43.5, 45.5, 45.7, 48.7), (51.5, 53.5, 53.7, 54.7))
H2T_AT = (46.95, 49.6, 53.8, 55.2)
LOGITS_AT = (53.9, 55.4)

UNROLL = 4
MAX_EXTRA = SEQ * TOP_K // P
MAX_ITEMS = N_EXP + MAX_EXTRA
LIST_COLS = MAX_ITEMS + UNROLL
NO_TOKEN = 4096
SLOT = 3 * NC * F_EXP


class Chain:

    def __init__(self, eng, sem):
        self.eng, self.sem, self.n = eng, sem, 0

    def __call__(self, ins):
        self.n += 1
        ins.then_inc(self.sem, 1)
        self.eng.wait_ge(self.sem, self.n)

    def tell(self, ins, sem, n):
        ins.then_inc(sem, 1)
        self.eng.wait_ge(sem, n)


def build(nc, x, mem, positions, w_in, lam_q1, lam_k1, lam_q2, lam_k2, diff_subln_g, mla_q_norm_g,
          mla_w_uq, mla_kv_norm_g, mla_w_ukv, mla_out_norm_g, w_o, ln1_g, ln1_b, mem_w_q, mem_w_k,
          mem_w_v, mem_w_o, ln2_g, ln2_b, router_w, router_bias, exp_w_gate, exp_w_up, exp_w_down,
          sh_w_gate, sh_w_up, sh_w_down, ln3_g, ln3_b, out):
    h2_rows = nc.dram_tensor("h2_rows", (SEQ, D), F32, kind="Internal").ap()
    y_rows = nc.dram_tensor("y_rows", (MAX_ITEMS * P, D), F32, kind="Internal").ap()
    token_list = nc.dram_tensor("token_list", (P * LIST_COLS, 1), U32, kind="Internal").ap()

    ctx = ExitStack()
    with ctx:
        def sb(name, shape, dt=F32):
            return ctx.enter_context(nc.sbuf_tensor(name, shape, dt))

        def sem(name):
            return ctx.enter_context(nc.semaphore(name))

        E = sb("expert_slots", [P, UNROLL * SLOT])
        X = sb("residual", [P, NT, D])
        AT = sb("act_transposed", [P, NC, SEQ])
        W = sb("weights", [P, 8192])
        PR = sb("proj", [P, NT, IN_COLS])
        MKV = sb("mem_k_v", [P, 2048])
        RW = sb("router_w", [P, NC, N_EXP])
        ident = sb("ident", [P, P])
        identb = sb("ident_bf16", [P, P], BF16)
        maskb = sb("causal_mask", [P, P], BF16)
        beforeb = sb("tokens_before", [P, P], BF16)
        onesb = sb("ones", [P, P], BF16)
        tri8 = sb("groups_before", [P, N_GRP, N_GRP])
        pos_i = sb("pos_i", [P, NT], I32)
        pos_f = sb("pos_f", [P, NT])
        n_freq = ROT_D // 2 + ROT_M // 2
        cosT = sb("cos", [P, NT, n_freq])
        sinT = sb("sin", [P, NT, n_freq])
        lam_in = sb("lam_in", [P, 4, QK_D])
        lam_sc = sb("lam_sc", [P, 8])
        gcol = sb("gain_columns", [P, 6])
        half = sb("minus_half", [P, 8])
        spare = sb("spare", [P, 8])
        POWB = sb("rsqrt_io", [P, 64])
        MS = sb("max_sum", [P, 4, 16])
        ST = sb("ln_stats", [P, 2, 6])
        MV = sb("ln_mean_var", [P, 8])
        rbias = sb("router_bias", [P, N_EXP])
        e128 = sb("expert_times_128", [P, N_EXP])
        item_no = sb("item_no", [P, MAX_EXTRA])
        iota_i = sb("iota_i", [P, N_EXP], I32)
        token_id = sb("token_id", [P, NT], U32)
        empty_list = sb("empty_list", [P, LIST_COLS], U32)
        idx_col = sb("idx_col", [P, 2, 4], U32)
        quarter = sb("quarter_of_partition", [P, 1])
        pos_u = sb("pos_u", [P, NT * TOP_K], U32)
        spos_u = sb("spos_u", [P, NT * TOP_K], U32)
        gk = sb("gate_of_choice", [P, NT * TOP_K])
        counts_i = sb("counts_i", [P, 3], I32)
        extra_i = sb("extra_experts", [P, MAX_EXTRA], I32)

        banks = [ctx.enter_context(nc.psum_tensor(f"bank{i}", [P, 512], F32)) for i in range(8)]

        KMT = MKV[:, 0:1024].rearrange("p (h n) -> p h n", h=HD)
        VM = MKV[:, 1024:2048].rearrange("p (m n) -> p m n", m=2)
        ST64 = MKV[:, 512:832].rearrange("p (i n) -> p i n", i=5)
        R8 = MKV[:, 1024:1408].rearrange("p (i n) -> p i n", i=12)
        lists = MKV[:, 1536:1536 + 4 * LIST_COLS].bitcast(U32).rearrange("p (g n) -> p g n", g=4)
        selb = MKV[:, 1408:1536].bitcast(BF16).rearrange("p (t e) -> p t e", t=NT)
        WIN = [E[:, n * NC * 512:n * NC * 512 + NC * w].rearrange("p (c n) -> p c n", c=NC)
               for n, w in enumerate((448, 512, 512, 512))]
        MEMX = E[:, 16384:18432].rearrange("p (m d) -> p m d", m=2)
        MEMT = E[:, 18432:20480].rearrange("p (c n) -> p c n", c=NC)
        WUQ = E[:, 20480:22016].rearrange("p (c n) -> p c n", c=2)
        WUKV = E[:, 22016:23040]
        KP = E[:, 23040:23552].rearrange("p (t n) -> p t n", t=NT)
        TMP = E[:, 23552:24576]
        QDT = E[:, 0:2048].rearrange("p (c n) -> p c n", c=4)
        KDT = E[:, 2048:4096].rearrange("p (c n) -> p c n", c=4)
        QNT = E[:, 4096:6144].rearrange("p (c n) -> p c n", c=4)
        KNT = E[:, 6144:8192].rearrange("p (c n) -> p c n", c=4)
        QPT = E[:, 8192:9216].rearrange("p (c n) -> p c n", c=2)
        KPT = E[:, 9216:9728]
        VML = E[:, 9728:11776].rearrange("p (t n) -> p t n", t=NT)
        WQ = E[:, 12288:16384].rearrange("p (c n) -> p c n", c=NC)
        WO2 = E[:, 16384:20480].rearrange("p (c n) -> p c n", c=4)
        LN1 = E[:, 20480:22528].rearrange("p (g d) -> p g d", g=2)
        LN2 = E[:, 22528:24576].rearrange("p (g d) -> p g d", g=2)
        WK = W[:, 0:4096].rearrange("p (c n) -> p c n", c=NC)
        WV = W[:, 4096:8192].rearrange("p (c n) -> p c n", c=NC)
        WO = W[:, :].rearrange("p (c n) -> p c n", c=NC)
        CQT = AT[:, 0:2, :]
        CKVT = AT[:, 2, :]
        H1T = AT[:, :, 0:P]
        O = [AT[:, :, (1 + i) * P:(2 + i) * P] for i in range(2)]
        QCT = AT[:, 0:4, 3 * P:4 * P]
        OCT = AT[:, 4:8, 3 * P:4 * P]
        PB = [PR[:, i // 2, (i % 2) * 512:(i % 2) * 512 + 512] for i in range(4)]
        PTB = [PR[:, 2, i * 512:i * 512 + 512] for i in range(2)]
        MIXT = PR[:, 3, 0:1024].rearrange("p (c n) -> p c n", c=NC)
        OC = PR[:, :, LAT:LAT + P]
        SQ = PR[:, 3, LAT + 192:LAT + 192 + P]
        PF = PR[:, :, :].rearrange("p t n -> p (t n)")
        XG = [PF[:, i * 1024:i * 1024 + 1024] for i in range(2)]
        XGT = [PF[:, 2048 + i * 1024:3072 + i * 1024].rearrange("p (c n) -> p c n", c=NC) for i in range(2)]
        Y = [PF[:, 4096 + i * 1024:5120 + i * 1024] for i in range(2)]
        HS = [PF[:, 6144 + i * 256:6400 + i * 256] for i in range(2)]
        HT = [PF[:, 6656 + i * 256:6912 + i * 256].rearrange("p (c n) -> p c n", c=2) for i in range(2)]
        SG = [PF[:, 7168 + i * 256:7424 + i * 256] for i in range(2)]
        SEL0 = 6144
        (SC, CH, T1, T2, MC, SELM, POSM, GATE) = [
            W[:, SEL0 + i * 256:SEL0 + i * 256 + 256].rearrange("p (t e) -> p t e", t=NT) for i in range(8)]
        CG = [E[:, i * D:(i + 1) * D] for i in range(8)]
        LN3 = AT[:, 0:4, :].rearrange("p c n -> p (c n)").rearrange("p (g d) -> p g d", g=2)

        def slot_views(flat):
            n = NC * F_EXP
            return (flat[:, 0:2 * n].rearrange("p (g c n) -> p g c n", g=2, c=NC),
                    flat[:, 2 * n:3 * n].rearrange("p (c n) -> p c n", c=2))

        SLOTS = [slot_views(E[:, b * SLOT:(b + 1) * SLOT]) for b in range(UNROLL)]
        SHARED = slot_views(W[:, 0:SLOT])

        x_in = [sem(f"x_in{t}") for t in range(NT)]
        win_in = [sem(f"w_in_block{n}") for n in range(4)]
        mem_in, wkv_in, lat_in, wo_in = sem("mem_in"), sem("wkv_in"), sem("lat_in"), sem("wo_in")
        small_in, ln1_in, ln2_in, ln3_in = sem("small_in"), sem("ln1_in"), sem("ln2_in"), sem("ln3_in")
        wq_in, wo2_in, sh_in, rw_in = sem("wq_in"), sem("wo2_in"), sem("shared_in"), sem("router_in")
        gate_up_in = [sem(f"gate_up_in{b}") for b in range(UNROLL)]
        down_in = [sem(f"down_in{b}") for b in range(UNROLL)]
        const_ready, pool_step = sem("const_ready"), sem("pool_step")
        dve_step, act_step = sem("dve_step"), sem("act_step")
        range_ready, trig_ready, lam_dots, lam_exps = (
            sem("range_ready"), sem("trig_ready"), sem("lam_dots"), sem("lam_exps"))
        gains_ready = sem("gains_ready")
        pow_asked, pow_done = sem("pow_asked"), sem("pow_done")
        grp_done, grp_act, grp_dve = sem("group_done"), sem("group_copied_act"), sem("group_copied_dve")
        lat_normed, kp_ready, rope_ready = sem("lat_normed"), sem("k_pe_ready"), sem("rope_ready")
        scores_done, negmax_ready, exp_done, mixed_p = (
            sem("scores_done"), sem("negmax_ready"), sem("exp_done"), sem("mixed_p"))
        pt_done, pt_copied, o_done, o_copied = sem("pt_done"), sem("pt_copied"), sem("o_done"), sem("o_copied")
        o_normed = sem("o_normed")
        aux_done, aux_act, aux_dve = sem("projection_done"), sem("projection_copied_act"), sem("projection_copied_dve")
        ln1_done, ln2_done, ln3_done = sem("ln1_done"), sem("ln2_done"), sem("ln3_done")
        h2_stored = [sem(f"h2_stored{t}") for t in range(NT)]
        sel_ready, rank_done = sem("selection_ready"), sem("rank_done")
        spos_ready, counts_ready, list_filled, listed, lists_in, lists_ready = (
            sem("list_places_ready"), sem("counts_ready"), sem("list_filled"), sem("listed"), sem("lists_in"),
            sem("lists_ready"))
        kp_rotated = sem("k_pe_rotated")
        gu_done, silu_done, h_ready, ht_done, ht_copied, down_done = (
            sem("gate_up_done"), sem("silu_done"), sem("h_ready"), sem("h_transposed"), sem("ht_copied"),
            sem("down_done"))
        sh_added = sem("shared_added")
        xg_in = [sem("xg_in0"), sem("xg_in1")]
        xg_zero = sem("xg_zeroed")
        xt_dve = sem("xg_transposed")
        y_act, y_dve = sem("y_copied_act"), sem("y_copied_dve")
        y_free = [sem("y_free0"), sem("y_free1")]
        idx_ready, zeros_ready, rows_zeroed = sem("idx_ready"), sem("zeros_ready"), sem("rows_zeroed")
        cg_in = [sem(f"choice_in{i}") for i in range(8)]
        cg_used, out_stored = sem("choice_used"), sem("out_stored")

        FRONT = ([("xT", t, h) for t in range(NT) for h in range(2)]
                 + [("proj", n, t) for n in range(4) for t in range(NT)]
                 + [("cqT", 0), ("cqT", 1), ("ckvT",), ("kpT",)]
                 + [("qkT", c) for c in range(8)]
                 + [("memT", m, h) for m in range(2) for h in range(2)]
                 + [("kmem", i) for i in range(2)] + [("qp", t) for t in range(NT)]
                 + [("vmem", m) for m in range(2)]
                 + [("qn", h) for h in range(HD)] + [("kn", h) for h in range(HD)]
                 + [("vm", t) for t in range(NT)]
                 + [("qpT", 0), ("qpT", 1)])
        AT_GROUP = {g: j for j, g in enumerate(FRONT)}

        def on_dve(j):
            return j % 2 == 1 or FRONT[j][0] in ("qp", "cqT")

        def copied(eng, j):
            same = on_dve(j)
            n = sum(on_dve(i) == same for i in range(j + 1))
            eng.wait_ge(grp_dve if same else grp_act, n)

        timed = sorted([(8.0 * t + k, ("dm"[k % 2], t, k // 2)) for t in range(NT) for k in range(8)]
                       + [(8 * t + XU + k, ("x", t, k)) for t in range(NT) for k in range(4)])
        UNITS = [unit for _, unit in timed]
        UNIT = {unit: u for u, unit in enumerate(UNITS)}
        EVENTS = []
        for u, (at, unit) in enumerate(timed):
            two_ahead = max(at - 2, timed[u - 2][0]) if u >= 2 else at - 2
            EVENTS += [(two_ahead, "scores", unit), (at - 0.1, "probabilities", unit),
                       (at + 0.4, "transpose", unit), (at + 1.1, "values", unit)]
        for t in range(NT):
            b = 8 * t
            EVENTS += [(b + 8.6, "norm_heads", t), (b + LN1A, "ln1_stats", t), (b + LN1B, "ln1_rows", t),
                       (b + LN1C, "ln1_bias", t), (OUT2_AT[t][3] + BIAS_AFTER, "ln2_bias", t),
                       (OUT2_AT[t][2], "ln2_stats", t), (OUT2_AT[t][3], "ln2_rows", t)]
            for at, job, part in ([(b + 9.5, ("mixT", t, g), None) for g in range(2)]
                                  + [(b + OUT0 + i * 2 + k, ("out", t, i), k) for i in range(2) for k in range(2)]
                                  + [(b + HTA, ("hT", t, g), None) for g in range(2)]
                                  + [(b + QCA + 0.5 * k, ("qc", t), k) for k in range(2)]
                                  + [(b + M2T, ("mix2T", t), None)]
                                  + [(OUT2_AT[t][i], ("out2", t, i), None) for i in range(2)]
                                  + [(H2T_AT[t], ("h2T", t, g), None) for g in range(2)]):
                EVENTS.append((at, "aux", (job, part)))
        EVENTS += [(LOGITS_AT[k], "aux", (("logits", k), None)) for k in range(2)]
        EVENTS.sort(key=lambda e: e[0])
        for what in ("scores", "transpose", "values"):
            assert UNITS == [e[2] for e in EVENTS if e[1] == what]
        JOBS = [e[2][0] for e in EVENTS if e[1] == "aux" and e[2][1] in (None, 1)]
        JOB = {job: j for j, job in enumerate(JOBS)}
        assert [e[2][0] for e in EVENTS if e[1] == "aux" and e[2][1] in (None, 0)] == JOBS

        def job_on_dve(job):
            return job[0] in ("out", "out2") or (job[0] in ("hT", "h2T") and job[2] == 1)

        def job_copied(eng, job):
            j, same = JOB[job], job_on_dve(job)
            n = sum(job_on_dve(i) == same for i in JOBS[:j + 1])
            eng.wait_ge(aux_dve if same else aux_act, n)

        POW, col = {}, 0
        asks = [("lat", t) for t in range(NT)]
        for _, what, arg in EVENTS:
            if what == "values" and arg[0] == "m" and arg[2] == HD - 1:
                asks.append(("mix", arg[1]))
            elif what in ("ln1_stats", "ln2_stats"):
                asks.append((what[:3], arg))
        asks += [("ln3", t) for t in range(NT)]
        for name in asks:
            width = {"lat": 2, "mix": 8}.get(name[0], 1)
            POW[name] = (len(POW), col, width)
            col += width

        def power(name):
            n, c, w = POW[name]
            return n, POWB[:, c:c + w]

        STEP0, s = [], 0
        for kind, _, _ in UNITS:
            STEP0.append(s)
            s += 2 if kind == "d" else 1
        UNIT_OF_STEP = [u for u, (k, _, _) in enumerate(UNITS) for _ in range(2 if k == "d" else 1)]

        def steps(u):
            return range(STEP0[u], STEP0[u] + (2 if UNITS[u][0] == "d" else 1))

        def keys(u):
            kind, t, _ = UNITS[u]
            return N_MEM if kind == "x" else (t + 1) * P

        def front_dest(eng, j, copy):
            g = FRONT[j]
            bank = banks[j % 8]
            four = bank[:, :].rearrange("p (c n) -> p c n", c=4)
            if g[0] == "xT":
                copy(AT[:, 4 * g[2]:4 * g[2] + 4, g[1] * P:(g[1] + 1) * P], four, None)
            elif g[0] == "proj":
                c0, w = [(LAT, 448), (0, 512), (512, 512), (1024, 512)][g[1]]
                copy(PR[:, g[2], c0:c0 + w], bank[:, 0:w], None)
            elif g[0] == "cqT":
                copy(CQT[:, g[1], :], bank[:, :], gcol[:, g[1]:g[1] + 1])
            elif g[0] == "ckvT":
                copy(CKVT, bank[:, :], gcol[:, 2:3])
            elif g[0] == "kpT":
                copy(KPT, bank[:, :], None)
            elif g[0] == "qkT":
                copy((QDT if g[1] < 4 else KDT)[:, g[1] % 4, :], bank[:, :], None)
            elif g[0] == "memT":
                copy(MEMT[:, 4 * g[2]:4 * g[2] + 4, g[1] * P:(g[1] + 1) * P], four, None)
            elif g[0] == "kmem":
                eng.wait_ge(rows_zeroed, 16)
                copy(KMT[:, 2 * g[1]:2 * g[1] + 2, :], bank[:, :].rearrange("p (h n) -> p h n", h=2), None)
            elif g[0] == "vmem":
                copy(VM[:, g[1], :], bank[:, :], None)
            elif g[0] == "qn":
                copy(QNT[:, g[1], :], bank[:, :], None)
            elif g[0] == "kn":
                copy(KNT[:, g[1], :], bank[:, :], None)
            elif g[0] == "vm":
                copy(VML[:, g[1], :], bank[:, :], None)
            elif g[0] == "qpT":
                copy(QPT[:, g[1], :], bank[:, :], None)

        def y_banks(b):
            return banks[2 + 2 * (b % 2):4 + 2 * (b % 2)]

        block = ctx.enter_context(nc.Block())

        def gate_up_weights(eng, b, e):
            for g, w in enumerate((exp_w_gate, exp_w_up)):
                eng.dma_start(SLOTS[b][0][:, g, :, :], w[0, e, :, :].rearrange("e (p c) n -> (e p) c n", c=NC)
                              ).then_inc(gate_up_in[b], 16)

        def down_weights(eng, b, e):
            eng.dma_start(SLOTS[b][1][:, :, :], exp_w_down[0, e, :, :].rearrange("e (p c) n -> (e p) c n", c=2)
                          ).then_inc(down_in[b], 16)

        @block.sync
        def _(sp):
            sp.dma_start(X[:, 0, :], x[0, 0:P, :]).then_inc(x_in[0], 16)
            blocks = [(LAT, 448), (0, 512), (512, 512), (1024, 512)]
            for n, (c0, w) in enumerate(blocks):
                sp.dma_start(WIN[n][:, :, :], w_in[0, :, c0:c0 + w].rearrange("(p c) n -> p c n", c=NC)
                             ).then_inc(win_in[n], 16)
                if n == 0:
                    for t in range(1, NT):
                        sp.dma_start(X[:, t, :], x[0, t * P:(t + 1) * P, :]).then_inc(x_in[t], 16)
            sp.dma_start(MEMX, mem[0, :, :].rearrange("(m p) d -> p m d", p=P)).then_inc(mem_in, 16)
            for w, dst in ((mem_w_k, WK), (mem_w_v, WV)):
                sp.dma_start(dst, w[0, :, :].rearrange("(p c) n -> p c n", c=NC)).then_inc(wkv_in, 16)
            sp.dma_start(WUQ, mla_w_uq[0, :, :].rearrange("(c p) n -> p c n", c=2)).then_inc(lat_in, 16)
            sp.dma_start(WUKV, mla_w_ukv[0, :, :]).then_inc(lat_in, 16)
            sp.wait_ge(grp_done, AT_GROUP[("vmem", 1)] + 1)
            sp.dma_start(WO, w_o[0, :, :].rearrange("(c p) n -> p c n", c=NC)).then_inc(wo_in, 16)
            sp.wait_ge(grp_done, len(FRONT))
            copied(sp, AT_GROUP[("qp", NT - 1)])
            for i, g in enumerate((ln1_g, ln1_b)):
                sp.dma_start(LN1[:, i, :], g[0:1, :].partition_broadcast(P)).then_inc(ln1_in, 16)
            sp.dma_start(WQ, mem_w_q[0, :, :].rearrange("(p c) n -> p c n", c=NC)).then_inc(wq_in, 16)
            sp.dma_start(WO2, mem_w_o[0, :, :].rearrange("(c p) n -> p c n", c=4)).then_inc(wo2_in, 16)
            for i, g in enumerate((ln2_g, ln2_b)):
                sp.dma_start(LN2[:, i, :], g[0:1, :].partition_broadcast(P)).then_inc(ln2_in, 16)
            sp.dma_start(RW[:, :, :], router_w[0, :, :].rearrange("(p c) n -> p c n", c=NC)).then_inc(rw_in, 16)
            sp.wait_ge(o_done, UNIT[("m", NT - 1, HD - 1)] + 1)
            gate_up_weights(sp, 0, slice(0, 1))
            down_weights(sp, 0, slice(0, 1))
            gate_up_weights(sp, 1, slice(1, 2))
            down_weights(sp, 1, slice(1, 2))
            sp.wait_ge(aux_done, JOB[("out", NT - 1, 1)] + 1)
            for g, w in enumerate((sh_w_gate, sh_w_up)):
                sp.dma_start(SHARED[0][:, g, :, :], w[0, :, :].rearrange("(p c) n -> p c n", c=NC)
                             ).then_inc(sh_in, 16)
            sp.dma_start(SHARED[1], sh_w_down[0, :, :].rearrange("(p c) n -> p c n", c=2)).then_inc(sh_in, 16)
            sp.wait_ge(aux_done, JOB[("out2", NT - 1, 1)] + 1)
            gate_up_weights(sp, 2, slice(2, 3))
            down_weights(sp, 2, slice(2, 3))
            sp.wait_ge(ln2_done, NT)
            gate_up_weights(sp, 3, slice(3, 4))
            down_weights(sp, 3, slice(3, 4))
            sp.wait_ge(listed, 16 * NT * TOP_K)
            for q in range(4):
                sp.dma_start(lists[32 * q:32 * q + 32, :, :], token_list.rearrange("(g i n) o -> i g (n o)", g=4, i=32)
                             ).then_inc(lists_in, 16)

            def store(i, b):
                sp.wait_ge(y_act, i + 2)
                sp.wait_ge(y_dve, i + 2)
                sp.dma_start(y_rows.rearrange("(i p) d -> i p d", p=P)[bass.ds(i, 1), :, :]
                             .rearrange("i p d -> (i p) d"), Y[b % 2]).then_inc(y_free[b % 2], 16)

            n_body = N_EXP // UNROLL

            def refill(it, expert):
                e = [None] * UNROLL
                for b in range(UNROLL + 1):
                    if b < UNROLL:
                        e[b] = expert(b)
                        sp.wait_ge(gu_done, it * UNROLL + (b + NT + 1))
                        gate_up_weights(sp, b, e[b])
                    if b:
                        sp.wait_ge(down_done, it * UNROLL + (b + NT))
                        down_weights(sp, b - 1, e[b - 1])
                        store(it * UNROLL + (b - 1), b - 1)

            with sp.Fori(0, n_body - 1) as it:
                refill(it, lambda b: bass.ds(it * UNROLL + (b + UNROLL), 1))
            sp.wait_ge(counts_ready, 1)
            last = sp.value_load(counts_i[0:1, 2:3], min_val=n_body - 1, max_val=MAX_ITEMS // UNROLL - 1)
            with sp.If(last > n_body - 1):
                with sp.Fori(n_body - 1, last) as it:
                    refill(it, lambda b: bass.ds(sp.value_load(
                        extra_i[0:1, bass.ds(it * UNROLL + (b + UNROLL - N_EXP), 1)], min_val=0, max_val=N_EXP - 1), 1))
            for b in range(UNROLL):
                store(last * UNROLL + b, b)
            for t in range(NT):
                sp.wait_ge(ln3_done, t + 1)
                sp.dma_start(out[0, t * P:(t + 1) * P, :], X[:, t, :]).then_inc(out_stored, 16)
            sp.wait_ge(out_stored, 16 * NT)

        @block.gpsimd
        def _(pool):
            step = Chain(pool, pool_step)
            step(pool.memset(ident[:, :], 0.0))
            step(pool.affine_select(out=ident[:, :], in_=ident[:, :], compare_op=ALU.not_equal, fill=1.0,
                                    base=0, pattern=[[-1, P]], channel_multiplier=1))
            pool.memset(half[:, :], -0.5).then_inc(const_ready, 1)
            step(pool.memset(identb[:, :], 0.0))
            step(pool.affine_select(out=identb[:, :], in_=identb[:, :], compare_op=ALU.not_equal, fill=1.0,
                                    base=0, pattern=[[-1, P]], channel_multiplier=1))
            step(pool.memset(maskb[:, :], 0.0))
            step(pool.affine_select(out=maskb[:, :], in_=maskb[:, :], compare_op=ALU.is_ge, fill=-1e30,
                                    base=0, pattern=[[-1, P]], channel_multiplier=1))
            step(pool.memset(beforeb[:, :], 1.0))
            step(pool.affine_select(out=beforeb[:, :], in_=beforeb[:, :], compare_op=ALU.is_gt, fill=0.0,
                                    base=0, pattern=[[1, P]], channel_multiplier=-1))
            step(pool.memset(onesb[:, :], 1.0))
            step(pool.memset(tri8[:, :, :], 1.0))
            step(pool.affine_select(out=tri8[:, :, :], in_=tri8[:, :, :], compare_op=ALU.is_gt, fill=0.0,
                                    base=0, pattern=[[1, N_GRP], [-1, N_GRP]], channel_multiplier=0))
            step(pool.iota(iota_i[:, 0:N_EXP], pattern=[[P, N_EXP]], base=0, channel_multiplier=0))
            step(pool.tensor_copy(e128[:, :], iota_i[:, 0:N_EXP]))
            step(pool.iota(iota_i[:, 0:MAX_EXTRA], pattern=[[1, MAX_EXTRA]], base=0, channel_multiplier=0))
            step(pool.tensor_copy(item_no[:, :], iota_i[:, 0:MAX_EXTRA]))
            step(pool.iota(token_id[:, :], pattern=[[P, NT]], base=0, channel_multiplier=1))
            step(pool.memset(empty_list[:, :], NO_TOKEN))
            for q in range(4):
                pool.memset(quarter[32 * q:32 * q + 32, :], float(q)).then_inc(pool_step, 1)
                step.n += 1
            pool.wait_ge(pool_step, step.n)
            pool.nop().then_inc(const_ready, 1)
            pool.dma_start(token_list.rearrange("(p c) o -> p (c o)", p=P), empty_list[:, :]).then_inc(list_filled, 16)

            def powers(names):
                for name in names:
                    n, cols = power(name)
                    pool.wait_ge(pow_asked, n + 1)
                    pool.tensor_tensor(cols, cols, half[:, 0:cols.shape[1]], ALU.pow).then_inc(pow_done, 1)

            def store_h2(t):
                pool.wait_ge(ln2_done, t + 1)
                pool.dma_start(h2_rows[t * P:(t + 1) * P, :], X[:, t, :]).then_inc(h2_stored[t], 16)

            powers([("lat", t) for t in range(NT)])
            pool.memset(MKV[:, 0:D], 0.0).then_inc(zeros_ready, 1)
            pool.wait_ge(zeros_ready, 1)
            pool.wait_ge(lat_in, 32)
            pool.dma_start(y_rows[N_EXP * P:, :].rearrange("(i p) d -> p i d", p=P),
                           MKV[:, 0:D].unsqueeze(1).to_broadcast([P, MAX_EXTRA, D])).then_inc(rows_zeroed, 16)

            due = None
            for name in POW:
                if name[0] == "lat":
                    continue
                if name[0] == "ln3":
                    break
                powers([name])
                if due is not None:
                    store_h2(due)
                due = name[1] if name[0] == "ln2" else None
            pool.wait_ge(aux_done, JOB[("out2", NT - 1, 1)] + 1)
            store_h2(NT - 1)
            for i in range(2):
                pool.memset(XG[i], 0.0).then_inc(xg_zero, 1)
            for i in range(2):
                pool.memset(Y[i], 0.0).then_inc(y_free[i], 16)
            pool.wait_ge(list_filled, 16)
            pool.wait_ge(spos_ready, 1)
            for j in range(NT * TOP_K):
                pool.indirect_dma_start(
                    out=token_list, out_offset=bass.IndirectOffsetOnAxis(ap=spos_u[:, j:j + 1], axis=0),
                    in_=token_id[:, j // TOP_K:j // TOP_K + 1], in_offset=None,
                    bounds_check=P * LIST_COLS - 1, oob_is_err=False).then_inc(listed, 16)
            pool.wait_ge(lists_ready, 1)
            for t in range(NT):
                pool.wait_ge(h2_stored[t], 16)

            def gather(i, b):
                p = b % 2
                pool.tensor_copy(idx_col[:, p, :], lists[:, :, bass.ds(i, 1)].rearrange("p g o -> p (g o)")
                                 ).then_inc(idx_ready, 1)
                pool.wait_ge(idx_ready, 1)
                pool.sem_clear(idx_ready)
                for g in range(4):
                    pool.indirect_dma_start(
                        out=XG[p][:, g * 256:(g + 1) * 256], out_offset=None,
                        in_=h2_rows.rearrange("t (q d) -> (t q) d", q=4),
                        in_offset=bass.IndirectOffsetOnAxis(ap=idx_col[:, p, g:g + 1], axis=0),
                        bounds_check=last_quarter, oob_is_err=False).then_inc(xg_in[p], 16)

            n_body = N_EXP // UNROLL
            last_quarter = pool.to_reg(4 * SEQ - 1)
            last_row = pool.to_reg(MAX_ITEMS * P - 1)
            pool.wait_ge(xg_zero, 2)
            pool.wait_ge(counts_ready, 1)
            gather(0, 0)
            gather(1, 1)
            n_iter = pool.value_load(counts_i[0:1, 1:2], min_val=n_body, max_val=MAX_ITEMS // UNROLL)
            with pool.Fori(0, n_iter) as it:
                for b in range(UNROLL):
                    pool.wait_ge(xt_dve, it * UNROLL + (b + 1))
                    gather(it * UNROLL + (b + 2), b)
            for p in range(2):
                pool.wait_ge(xg_in[p], n_iter * 128 + 64)
            for p in range(2):
                pool.wait_ge(y_free[p], n_iter * 32 + 16)
            pool.tensor_tensor(spare[:, :], half[:, :], half[:, :], ALU.add).then_inc(pool_step, 1)
            pool.wait_ge(pool_step, step.n + 1)

            def take_choices(rows):
                for j in range(NT * TOP_K):
                    if j >= 8:
                        pool.wait_ge(cg_used, j - 7)
                    pool.indirect_dma_start(
                        out=CG[j % 8], out_offset=None, in_=rows,
                        in_offset=bass.IndirectOffsetOnAxis(ap=pos_u[:, j:j + 1], axis=0),
                        bounds_check=last_row, oob_is_err=False).then_inc(cg_in[j % 8], 16)
                    if j % TOP_K == TOP_K - 1 and j > TOP_K:
                        powers([("ln3", j // TOP_K - 1)])
                powers([("ln3", NT - 1)])

            take_choices(y_rows)

        @block.scalar
        def _(act):
            with nc.allow_non_contiguous_dma(reason="a few hundred words"):
                act.dma_start(pos_i[:, :], positions[0, :].rearrange("(t p) -> p t", p=P)).then_inc(small_in, 16)
                for i, v in enumerate((lam_q1, lam_k1, lam_q2, lam_k2)):
                    act.dma_start(lam_in[:, i, :], v[0:1, :].partition_broadcast(P)).then_inc(small_in, 16)
                act.dma_start(gcol[:, 0:2], mla_q_norm_g[0, :].rearrange("(c p) -> p c", p=P)).then_inc(small_in, 16)
                for i, v in enumerate((mla_kv_norm_g, diff_subln_g, mla_out_norm_g)):
                    act.dma_start(gcol[:, 2 + i:3 + i], v[0, :].rearrange("(p c) -> p c", c=1)).then_inc(small_in, 16)
            act.dma_start(rbias[:, :], router_bias[0:1, :].partition_broadcast(P)).then_inc(small_in, 16)

            def copy(dst, src, s, scale=1.0):
                act.activation(dst, src, ACT.Copy, scale=scale).then_inc(s, 1)

            def drain_group(j):
                act.wait_ge(grp_done, j + 1)
                front_dest(act, j, lambda dst, src, g: copy(dst, src, grp_act, 1.0 if g is None else g))

            def lam():
                act.wait_ge(lam_dots, 1)
                act.activation(lam_sc[:, 2:4], lam_sc[:, 0:2], ACT.Exp).then_inc(lam_exps, 1)

            for j in range(len(FRONT)):
                if not on_dve(j):
                    drain_group(j)
                if FRONT[j] == ("proj", 0, 0):
                    act.wait_ge(range_ready, 1)
                    act.activation(sinT[:, :, :], sinT[:, :, :], ACT.Sin).then_inc(trig_ready, 1)
                    act.activation(cosT[:, :, :], cosT[:, :, :], ACT.Sin).then_inc(trig_ready, 1)
                    lam()

            def exps(u):
                kind = UNITS[u][0]
                n = keys(u)
                scale = {"d": SCALE_D, "m": SCALE_M, "x": SCALE_X}[kind]
                for s in steps(u):
                    act.wait_ge(negmax_ready, s + 1)
                    if s >= 4:
                        act.wait_ge(pt_done, UNIT_OF_STEP[s - 4] + 1)
                    act.activation(PB[s % 4][:, 0:n], banks[s % 4][:, 0:n], ACT.Exp,
                                   bias=MS[:, 1, s % 16:s % 16 + 1], scale=scale,
                                   accum_out=MS[:, 2, s % 16:s % 16 + 1]).then_inc(exp_done, 1)

            def pt_copy(u):
                act.wait_ge(pt_done, u + 1)
                if u >= 2:
                    act.wait_ge(o_done, u - 1)
                copy(PTB[u % 2][:, 0:keys(u)], banks[4][:, 0:keys(u)], pt_copied)

            def copy_job(job):
                j = JOB[job]
                act.wait_ge(aux_done, j + 1)
                v = banks[6 + j % 2][:, :].rearrange("p (c n) -> p c n", c=4)
                if job[0] == "mixT":
                    g = job[2]
                    copy(MIXT[:, 4 * g:4 * g + 4, :], v, aux_act, gcol[:, 5 - g:6 - g])
                elif job[0] == "hT":
                    copy(H1T[:, 0:4, :], v, aux_act)
                elif job[0] == "qc":
                    copy(QCT, v, aux_act)
                elif job[0] == "mix2T":
                    copy(OCT, v, aux_act)
                elif job[0] == "logits":
                    t0, n = (0, NT - 1) if job[1] == 0 else (NT - 1, 1)
                    act.activation(SC[:, t0:t0 + n, :], banks[6 + j % 2][:, 0:n * N_EXP]
                                   .rearrange("p (t e) -> p t e", t=n), ACT.Sigmoid).then_inc(aux_act, 1)
                else:
                    copy(AT[:, 0:4, job[1] * P:(job[1] + 1) * P], v, aux_act)

            act.wait_ge(gains_ready, 1)
            for _, what, arg in EVENTS:
                if what == "scores":
                    exps(UNIT[arg])
                elif what == "transpose":
                    pt_copy(UNIT[arg])
                elif what == "aux" and arg[1] in (None, 1) and not job_on_dve(arg[0]):
                    copy_job(arg[0])
            def silu(q, b):
                act.wait_ge(gu_done, q + 1)
                if not isinstance(q, int) or q >= 2:
                    act.wait_ge(h_ready, q + -1)
                act.activation(SG[b % 2], banks[b % 2][:, 0:F_EXP], ACT.Silu).then_inc(silu_done, 1)

            def ht_copy(q, b):
                act.wait_ge(ht_done, q + 1)
                if not isinstance(q, int) or q >= 2:
                    act.wait_ge(down_done, q + -1)
                copy(HT[b % 2], banks[7][:, 0:256].rearrange("p (c n) -> p c n", c=2), ht_copied)

            def y_copy(it, b):
                i = it * UNROLL + b
                act.wait_ge(down_done, i + (NT + 1))
                act.wait_ge(y_free[b % 2], it * 32 + 16 * (b // 2 + 1))
                copy(Y[b % 2][:, 0:512], y_banks(b)[0][:, :], y_act)

            for q in range(NT):
                silu(q, q)
                if q:
                    ht_copy(q - 1, q - 1)
            ht_copy(NT - 1, NT - 1)
            act.wait_ge(gu_done, NT)
            for i, g in enumerate((ln3_g, ln3_b)):
                act.dma_start(LN3[:, i, :], g[0:1, :].partition_broadcast(P)).then_inc(ln3_in, 16)
            act.wait_ge(counts_ready, 1)
            n_iter = act.value_load(counts_i[0:1, 1:2], min_val=N_EXP // UNROLL, max_val=MAX_ITEMS // UNROLL)
            with act.Fori(0, n_iter) as it:
                for b in range(UNROLL):
                    i = it * UNROLL + b
                    if b:
                        ht_copy(it * UNROLL + (b + NT - 1), b - 1)
                    silu(it * UNROLL + (b + NT), b)
                    if b == UNROLL - 1:
                        ht_copy(it * UNROLL + (2 * NT - 1), UNROLL - 1)
                    if b:
                        y_copy(it, b - 1)
                y_copy(it, UNROLL - 1)

        @block.vector
        def _(dve):
            step = Chain(dve, dve_step)

            def drain_group(j):
                dve.wait_ge(grp_done, j + 1)

                def copy(dst, src, gain):
                    if gain is None:
                        dve.tensor_copy(dst, src).then_inc(grp_dve, 1)
                    else:
                        dve.tensor_scalar(dst, src, gain, None, ALU.mult).then_inc(grp_dve, 1)
                front_dest(dve, j, copy)

            def trig_ranges():
                dve.wait_ge(small_in, 16 * 10)
                step(dve.tensor_copy(pos_f[:, :], pos_i[:, :]))
                freqs = [np.float32(THETA ** (-i / n)) for n in (ROT_D, ROT_M) for i in range(0, n, 2)]
                for j, f in enumerate(freqs):
                    last = dve.tensor_scalar(sinT[:, :, j], pos_f[:, :], float(f), None, ALU.mult)
                    last.then_inc(dve_step, 1)
                    step.n += 1
                dve.wait_ge(dve_step, step.n)
                magic = 1.5 * 2.0 ** 23
                turns = TMP[:, 0:NT * n_freq].rearrange("p (t j) -> p t j", t=NT)
                step(dve.tensor_scalar(turns, sinT[:, :, :], 1.0 / (2 * math.pi), magic, ALU.mult, ALU.add))
                step(dve.tensor_scalar(turns, turns, magic, None, ALU.subtract))
                c1 = 6.28125
                c2 = float(np.float32(2 * math.pi - c1).view(np.uint32) & np.uint32(0xFFFFF000))
                c2 = float(np.uint32(int(c2)).view(np.float32))
                c3 = 2 * math.pi - c1 - c2
                for c in (c1, c2, c3):
                    step(dve.scalar_tensor_tensor(sinT[:, :, :], turns, -c, sinT[:, :, :], ALU.mult, ALU.add))
                top = 3.1415925
                step(dve.tensor_scalar(sinT[:, :, :], sinT[:, :, :], top, -top, ALU.min, ALU.max))
                step(dve.tensor_scalar(cosT[:, :, :], sinT[:, :, :], -1.0, None, ALU.mult))
                step(dve.tensor_tensor(cosT[:, :, :], cosT[:, :, :], sinT[:, :, :], ALU.min))
                dve.tensor_scalar(cosT[:, :, :], cosT[:, :, :], math.pi / 2, None, ALU.add).then_inc(range_ready, 1)

            def lam_products():
                for i in range(2):
                    step(dve.tensor_tensor_reduce(out=TMP[:, 256:256 + QK_D], in0=lam_in[:, 2 * i, :],
                                                  in1=lam_in[:, 2 * i + 1, :], scale=1.0, scalar=0.0,
                                                  op0=ALU.mult, op1=ALU.add, accum_out=lam_sc[:, i:i + 1]))
                dve.nop().then_inc(lam_dots, 1)

            def lam_final():
                dve.wait_ge(lam_exps, 1)
                step(dve.tensor_tensor(lam_sc[:, 4:5], lam_sc[:, 3:4], lam_sc[:, 2:3], ALU.subtract))
                step(dve.tensor_scalar(lam_sc[:, 5:6], lam_sc[:, 4:5], -LAM_INIT, None, ALU.add))
                dve.tensor_scalar(gcol[:, 5:6], gcol[:, 3:4], 1.0 - LAM_INIT, None, ALU.mult).then_inc(gains_ready, 1)

            def rsqrt(name):
                n, cols = power(name)
                dve.wait_ge(pow_done, n + 1)
                return cols

            def latent_norms():
                for t in range(NT):
                    copied(dve, AT_GROUP[("proj", 0, t)])
                    n, cols = power(("lat", t))
                    for i, (c0, w) in enumerate(((LAT, 256), (LAT + 256, 128))):
                        v = PR[:, t, c0:c0 + w]
                        step(dve.tensor_tensor_reduce(out=TMP[:, 0:w], in0=v, in1=v, scale=1.0 / w, scalar=RMS_EPS,
                                                      op0=ALU.mult, op1=ALU.add, accum_out=cols[:, i:i + 1]))
                    dve.nop().then_inc(pow_asked, 1)
                for t in range(NT):
                    cols = rsqrt(("lat", t))
                    for i, (c0, w) in enumerate(((LAT, 256), (LAT + 256, 128))):
                        v = PR[:, t, c0:c0 + w]
                        dve.tensor_scalar(v, v, cols[:, i:i + 1], None, ALU.mult).then_inc(lat_normed, 1)

            def rotate(a, b, cos, sin, t1, t2, t3, outa, outb, s):
                step(dve.tensor_tensor(t1, a, cos, ALU.mult))
                step(dve.tensor_tensor(t2, b, sin, ALU.mult))
                step(dve.tensor_tensor(t3, a, sin, ALU.mult))
                step(dve.tensor_tensor(outa, t1, t2, ALU.subtract))
                step(dve.tensor_tensor(t1, b, cos, ALU.mult))
                last = dve.tensor_tensor(outb, t1, t3, ALU.add)
                step.tell(last, *s)

            def temps(shape):
                size = math.prod(shape)
                return [TMP[:, i * size:(i + 1) * size] for i in range(3)]

            def key_rotation():
                dve.wait_ge(trig_ready, 2)
                cos, sin = cosT[:, :, 8:40], sinT[:, :, 8:40]
                t1, t2, t3 = [v.rearrange("p (t j) -> p t j", t=NT) for v in temps((NT, 32))]
                a, b = PR[:, :, 1920:1952], PR[:, :, 1952:1984]
                rotate(a, b, cos, sin, t1, t2, t3, KP[:, :, 0:32], KP[:, :, 32:64],
                       (kp_rotated, 1))
                dve.tensor_copy(KP[:, :, 64:128], KP[:, :, 0:64]).then_inc(kp_ready, 1)

            def head_rotation():
                for t in range(NT):
                    for n in (1, 2):
                        copied(dve, AT_GROUP[("proj", n, t)])
                    v = PR[:, t, 0:1024].rearrange("p (h n) -> p h n", n=QK_D)
                    cos = cosT[:, t, 0:8].unsqueeze(1).to_broadcast([P, 16, 8])
                    sin = sinT[:, t, 0:8].unsqueeze(1).to_broadcast([P, 16, 8])
                    t1, t2, t3 = [w.rearrange("p (h j) -> p h j", j=8) for w in temps((16, 8))]
                    rotate(v[:, :, 0:8], v[:, :, 8:16], cos, sin, t1, t2, t3, v[:, :, 0:8], v[:, :, 8:16],
                           (rope_ready, t + 1))

            def query_rotation(t, j):
                dve.wait_ge(grp_done, j + 1)
                v = banks[j % 8][:, 0:HD * ROPE].rearrange("p (h n) -> p h n", n=ROPE)
                o = PR[:, t, LAT:LAT + HD * ROPE].rearrange("p (h n) -> p h n", n=ROPE)
                cos = cosT[:, t, 8:40].unsqueeze(1).to_broadcast([P, HD, 32])
                sin = sinT[:, t, 8:40].unsqueeze(1).to_broadcast([P, HD, 32])
                t1, t2, t3 = [w.rearrange("p (h j) -> p h j", j=32) for w in temps((HD, 32))]
                rotate(v[:, :, 0:32], v[:, :, 32:64], cos, sin, t1, t2, t3, o[:, :, 0:32], o[:, :, 32:64],
                       (grp_dve, sum(map(on_dve, range(j + 1)))))

            for j in range(len(FRONT)):
                if FRONT[j][0] == "qp":
                    query_rotation(FRONT[j][1], j)
                elif on_dve(j):
                    drain_group(j)
                if FRONT[j] == ("proj", 0, 1):
                    trig_ranges()
                    lam_products()
                if FRONT[j] == ("proj", 0, 3):
                    lam_final()
                    latent_norms()
                    key_rotation()
                if FRONT[j] == ("proj", 3, 1):
                    head_rotation()

            def maxima(u):
                kind = UNITS[u][0]
                scale = {"d": SCALE_D, "m": SCALE_M, "x": SCALE_X}[kind]
                for s in steps(u):
                    c = slice(s % 16, s % 16 + 1)
                    dve.wait_ge(scores_done, s + 1)
                    step(dve.reduce_max(MS[:, 0, c], banks[s % 4][:, 0:keys(u)], AX.X))
                    dve.tensor_scalar(MS[:, 1, c], MS[:, 0, c], -scale, None, ALU.mult).then_inc(negmax_ready, 1)

            def probabilities(u):
                s0 = STEP0[u]
                c0 = slice(s0 % 16, s0 % 16 + 1)
                if UNITS[u][0] != "d":
                    dve.wait_ge(exp_done, s0 + 1)
                    dve.reciprocal(MS[:, 3, c0], MS[:, 2, c0]).then_inc(mixed_p, 1)
                    return
                c1 = slice((s0 + 1) % 16, (s0 + 1) % 16 + 1)
                n = keys(u)
                dve.wait_ge(exp_done, s0 + 2)
                dve.reciprocal(MS[:, 3, c0], MS[:, 2, c0]).then_inc(dve_step, 1)
                step.n += 1
                step(dve.reciprocal(MS[:, 3, c1], MS[:, 2, c1]))
                step(dve.tensor_scalar(PB[(s0 + 1) % 4][:, 0:n], PB[(s0 + 1) % 4][:, 0:n], MS[:, 3, c1],
                                       lam_sc[:, 5:6], ALU.mult, ALU.mult))
                dve.scalar_tensor_tensor(PB[s0 % 4][:, 0:n], PB[s0 % 4][:, 0:n], MS[:, 3, c0],
                                         PB[(s0 + 1) % 4][:, 0:n], ALU.mult, ALU.add).then_inc(mixed_p, 1)

            def values(u):
                kind, t, h = UNITS[u]
                o = banks[5][:, 0:P]
                s0 = STEP0[u]
                r = MS[:, 3, s0 % 16:s0 % 16 + 1]
                dve.wait_ge(o_done, u + 1)
                if kind == "x":
                    dve.wait_ge(mixed_p, u + 1)
                    if t and h == 0:
                        dve.wait_ge(aux_done, JOB[("mix2T", t - 1)] + 1)
                    dve.tensor_scalar(OC[:, h, :], o, r, None, ALU.mult).then_inc(o_copied, 1)
                    return
                g = h + (4 if kind == "m" else 0)
                dst = O[t % 2][:, g, :]
                if t >= 2 and g == 0:
                    dve.wait_ge(aux_done, JOB[("mixT", t - 2, 1)] + 1)
                if kind == "d":
                    step(dve.tensor_copy(dst, o))
                else:
                    dve.wait_ge(mixed_p, u + 1)
                    step(dve.tensor_scalar(dst, o, r, None, ALU.mult))
                n, cols = power(("mix", t))
                dve.tensor_tensor_reduce(out=SQ, in0=dst, in1=dst, scale=1.0 / P, scalar=RMS_EPS,
                                         op0=ALU.mult, op1=ALU.add, accum_out=cols[:, g:g + 1]).then_inc(o_copied, 1)
                dve.wait_ge(o_copied, u + 1)
                if g == 7:
                    dve.nop().then_inc(pow_asked, 1)

            def norm_heads(t):
                cols = rsqrt(("mix", t))
                v = O[t % 2]
                dve.tensor_tensor(v, v, cols.unsqueeze(2).to_broadcast([P, 8, P]), ALU.mult).then_inc(o_normed, 1)

            def norm_stats(name, t):
                for i in range(2):
                    step(dve.bn_stats(ST[:, i, :], X[:, t, i * 512:(i + 1) * 512]))
                mv = MV[:, 4 * (name == "ln2"):]
                step(dve.bn_aggr(mv[:, 0:2], ST[:, :, :]))
                n, cols = power((name, t))
                dve.tensor_scalar(cols, mv[:, 1:2], LN_EPS, None, ALU.add).then_inc(pow_asked, 1)

            def norm_rows(name, t, rows, loaded):
                v = X[:, t, :]
                cols = rsqrt((name, t))
                mv = MV[:, 4 * (name == "ln2"):]
                step(dve.tensor_scalar(mv[:, 2:3], mv[:, 0:1], cols, -1.0, ALU.mult, ALU.mult))
                step(dve.tensor_scalar(v, v, cols, mv[:, 2:3], ALU.mult, ALU.add))
                dve.wait_ge(loaded, 32)
                step(dve.tensor_tensor(v, v, rows[:, 0, :], ALU.mult))

            def norm_bias(t, rows, done):
                v = X[:, t, :]
                dve.tensor_tensor(v, v, rows[:, 1, :], ALU.add).then_inc(done, 1)
                dve.wait_ge(done, t + 1)

            def copy_job(job):
                j = JOB[job]
                dve.wait_ge(aux_done, j + 1)
                bank = banks[6 + j % 2]
                t, i = job[1], job[-1]
                if job[0] in ("out", "out2"):
                    v = X[:, t, i * 512:(i + 1) * 512]
                    step.tell(dve.scalar_tensor_tensor(v, v, ALPHA, bank[:, :], ALU.mult, ALU.add),
                              aux_dve, sum(map(job_on_dve, JOBS[:j + 1])))
                else:
                    dst = H1T[:, 4:8, :] if job[0] == "hT" else AT[:, 4:8, t * P:(t + 1) * P]
                    dve.tensor_copy(dst, bank[:, :].rearrange("p (c n) -> p c n", c=4)).then_inc(aux_dve, 1)

            for _, what, arg in EVENTS:
                if what == "scores":
                    maxima(UNIT[arg])
                elif what == "probabilities":
                    probabilities(UNIT[arg])
                elif what == "values":
                    values(UNIT[arg])
                elif what == "norm_heads":
                    norm_heads(arg)
                elif what in ("ln1_stats", "ln2_stats"):
                    norm_stats(what[:3], arg)
                elif what == "ln1_rows":
                    norm_rows("ln1", arg, LN1, ln1_in)
                elif what == "ln1_bias":
                    norm_bias(arg, LN1, ln1_done)
                elif what == "ln2_rows":
                    norm_rows("ln2", arg, LN2, ln2_in)
                elif what == "ln2_bias":
                    norm_bias(arg, LN2, ln2_done)
                elif what == "aux" and arg[1] in (None, 1) and job_on_dve(arg[0]):
                    copy_job(arg[0])

            def hidden(q, b):
                dve.wait_ge(silu_done, q + 1)
                if not isinstance(q, int) or q >= 2:
                    dve.wait_ge(ht_done, q + -1)
                dve.tensor_tensor(HS[b % 2], SG[b % 2], banks[b % 2][:, F_EXP:2 * F_EXP], ALU.mult).then_inc(h_ready, 1)

            def small(i, w=NT * N_GRP):
                return R8[:, i, 0:w]

            def grouped(v):
                return v.rearrange("p t (g e) -> p (t g) e", g=N_GRP)

            def per_group(v):
                return v.unsqueeze(2).to_broadcast([P, NT * N_GRP, N_GRP])

            job_copied(dve, ("logits", 0))
            job_copied(dve, ("logits", 1))
            big = 1e30
            step(dve.tensor_tensor(CH[:, :, :], SC[:, :, :], rbias[:, :].unsqueeze(1).to_broadcast([P, NT, N_EXP]),
                                   ALU.add))
            step(dve.reduce_max(small(0), grouped(CH), AX.X))
            step(dve.tensor_tensor(grouped(T1), grouped(CH), per_group(small(0)), ALU.is_equal))
            step(dve.tensor_reduce(small(1), grouped(T1), AX.X, ALU.add))
            step(dve.scalar_tensor_tensor(T2[:, :, :], T1[:, :, :], -big, CH[:, :, :], ALU.mult, ALU.add))
            step(dve.reduce_max(small(2), grouped(T2), AX.X))
            step(dve.tensor_scalar(small(1), small(1), 1.5, None, ALU.is_ge))
            step(dve.tensor_scalar(small(1), small(1), -1.0, big, ALU.add, ALU.mult))
            step(dve.tensor_tensor(small(1), small(1), small(0), ALU.add))
            step(dve.tensor_tensor(small(2), small(2), small(1), ALU.max))
            step(dve.tensor_tensor(small(0), small(0), small(2), ALU.add))
            gs = small(0).rearrange("p (t g) -> p t g", t=NT)
            shape = [P, NT, N_GRP, N_GRP]
            mine = gs.unsqueeze(3).to_broadcast(shape)
            others = gs.unsqueeze(2).to_broadcast(shape)
            a, b = (v.rearrange("p t (g k) -> p t g k", g=N_GRP) for v in (T1, T2))
            step(dve.tensor_tensor(a, others, mine, ALU.is_gt))
            step(dve.tensor_tensor(b, others, mine, ALU.is_equal))
            step(dve.tensor_tensor(b, b, tri8[:, :, :].unsqueeze(1).to_broadcast(shape), ALU.mult))
            step(dve.tensor_tensor(T1[:, :, :], T1[:, :, :], T2[:, :, :], ALU.add))
            step(dve.tensor_reduce(small(3), grouped(T1), AX.X, ALU.add))
            step(dve.tensor_scalar(small(3), small(3), TOPK_GRP - 0.5, None, ALU.is_le))
            step(dve.tensor_tensor(grouped(MC), grouped(CH), per_group(small(3)), ALU.mult))
            step(dve.tensor_scalar(small(4), small(3), -1.0, big, ALU.add, ALU.mult))
            step(dve.tensor_tensor(grouped(MC), grouped(MC), per_group(small(4)), ALU.add))
            for t in range(NT):
                step(dve.max(R8[:, 5, t * 8:t * 8 + 8], MC[:, t, :]))
                step(dve.match_replace(T1[:, t, :], R8[:, 5, t * 8:t * 8 + 8], MC[:, t, :], -2.0 * big))
            step(dve.tensor_scalar(SELM[:, :, :], T1[:, :, :], -1.5 * big, None, ALU.is_le))
            dve.tensor_copy(selb[:, :, :], SELM[:, :, :]).then_inc(sel_ready, 1)
            hidden(0, 0)
            step(dve.tensor_tensor(GATE[:, :, :], SC[:, :, :], SELM[:, :, :], ALU.mult))
            step(dve.tensor_reduce(R8[:, 6, 0:NT], GATE[:, :, :], AX.X, ALU.add))
            step(dve.reciprocal(R8[:, 6, 4:4 + NT], R8[:, 6, 0:NT]))
            for t in range(NT):
                step(dve.tensor_scalar(GATE[:, t, :], GATE[:, t, :], R8[:, 6, 4 + t:5 + t], ROUTED_SCALE,
                                       ALU.mult, ALU.mult))
            dve.wait_ge(rank_done, 1)
            ranks = banks[5][:, 0:NT * N_EXP].rearrange("p (t e) -> p t e", t=NT)
            size = banks[5][:, NT * N_EXP:(NT + 1) * N_EXP]
            ex, cum, start, base, tmp = (ST64[:, i, :] for i in range(5))
            step(dve.tensor_scalar(ex, size, P + 0.5, None, ALU.is_ge))
            for lim in (2 * P, 3 * P):
                step(dve.scalar_tensor_tensor(ex, size, lim + 0.5, ex, ALU.is_ge, ALU.add))
            step(dve.memset(tmp, 0.0))
            step(dve.tensor_tensor_scan(cum, ex, tmp, 0.0, ALU.add, ALU.add))
            step(dve.tensor_tensor(start, cum, ex, ALU.subtract))
            step(dve.tensor_scalar(base, start, N_EXP - 1.0, float(P), ALU.add, ALU.mult))
            step(dve.tensor_tensor(tmp, e128[:, :], base, ALU.subtract))
            wide = lambda v: v.unsqueeze(1).to_broadcast([P, NT, N_EXP])
            step(dve.tensor_scalar(T1[:, :, :], ranks, P - 0.5, None, ALU.is_le))
            step(dve.tensor_tensor(T1[:, :, :], T1[:, :, :], wide(tmp), ALU.mult))
            step(dve.tensor_tensor(T1[:, :, :], T1[:, :, :], wide(base), ALU.add))
            step(dve.scalar_tensor_tensor(T1[:, :, :], ranks, 1.0, T1[:, :, :], ALU.add, ALU.add))
            step(dve.tensor_tensor(POSM[:, :, :], T1[:, :, :], SELM[:, :, :], ALU.mult))
            posk = R8[:, 7, :]
            for t in range(NT):
                step(dve.max(posk[:, t * 8:t * 8 + 8], POSM[:, t, :]))
            step(dve.tensor_scalar(pos_u[:, :], posk, -1.0, None, ALU.add))
            item_u, slot_u = R8[:, 8, :].bitcast(U32), R8[:, 9, :].bitcast(U32)
            step(dve.tensor_scalar(item_u, pos_u[:, :], 7, None, ALU.logical_shift_right))
            step(dve.tensor_scalar(slot_u, pos_u[:, :], P - 1, None, ALU.bitwise_and))
            step(dve.tensor_copy(R8[:, 10, :], item_u))
            step(dve.tensor_copy(R8[:, 11, :], slot_u))
            dve.scalar_tensor_tensor(spos_u[:, :], R8[:, 11, :], float(LIST_COLS), R8[:, 10, :], ALU.mult,
                                     ALU.add).then_inc(spos_ready, 1)
            def item_counts():
                step(dve.tensor_scalar(counts_i[:, 0:1], cum[:, N_EXP - 1:N_EXP], float(N_EXP + UNROLL - 1), None, ALU.add))
                step(dve.tensor_scalar(counts_i[:, 1:2], counts_i[:, 0:1], 2, None, ALU.logical_shift_right))
                step(dve.tensor_scalar(counts_i[:, 2:3], counts_i[:, 1:2], -1.0, None, ALU.add))
                for k in range(MAX_EXTRA // 4):
                    four = T2[:, :, :]
                    step(dve.tensor_tensor(four, wide(cum), item_no[:, 4 * k:4 * k + 4].unsqueeze(2).to_broadcast([P, 4, N_EXP]),
                                           ALU.is_le))
                    step(dve.tensor_reduce(R8[:, 5, 4 * k:4 * k + 4], four, AX.X, ALU.add))
                step(dve.tensor_scalar(extra_i[:, :], R8[:, 5, 0:MAX_EXTRA], N_EXP - 1.0, None, ALU.min))
                dve.nop().then_inc(counts_ready, 1)

            def gate_of_choices():
                for t in range(NT):
                    for k in range(TOP_K):
                        j = t * TOP_K + k
                        step(dve.scalar_tensor_tensor(T2[:, t, :], POSM[:, t, :], posk[:, j:j + 1], GATE[:, t, :],
                                                      ALU.is_equal, ALU.mult, accum_out=gk[:, j:j + 1]))

            def xg_transpose(i, b, arrivals):
                dve.wait_ge(xg_in[b % 2], arrivals)
                dve.wait_ge(gu_done, i + 3)
                dve.transpose(XGT[b % 2].rearrange("p c (g i) -> p g c i", g=4),
                              XG[b % 2].rearrange("p (g j c) -> p g c j", g=4, c=NC)).then_inc(xt_dve, 1)

            def y_copy(it, b):
                i = it * UNROLL + b
                dve.wait_ge(down_done, i + (NT + 1))
                dve.wait_ge(y_free[b % 2], it * 32 + 16 * (b // 2 + 1))
                dve.tensor_copy(Y[b % 2][:, 512:1024], y_banks(b)[1][:, :]).then_inc(y_dve, 1)

            def shared_add(t):
                dve.wait_ge(down_done, t + 1)
                dve.wait_ge(h2_stored[t], 16)
                for i in range(2):
                    v = X[:, t, i * 512:(i + 1) * 512]
                    dve.scalar_tensor_tensor(v, v, ALPHA, y_banks(t)[i][:, :], ALU.mult, ALU.add
                                             ).then_inc(sh_added if t < NT - 1 else (y_act, y_dve)[i], 1)

            for q in range(NT):
                if q:
                    hidden(q, q)
                    shared_add(q - 1)
                if q == NT - 3:
                    item_counts()
                elif q == NT - 2:
                    gate_of_choices()
            shared_add(NT - 1)
            dve.wait_ge(lists_in, 64)
            dve.tensor_scalar(lists[:, :, :], lists[:, :, :], 4.0, quarter[:, 0:1], ALU.mult, ALU.add).then_inc(lists_ready, 1)
            xg_transpose(0, 0, 64)
            n_iter = dve.value_load(counts_i[0:1, 1:2], min_val=N_EXP // UNROLL, max_val=MAX_ITEMS // UNROLL)
            with dve.Fori(0, n_iter) as it:
                for b in range(UNROLL):
                    hidden(it * UNROLL + (b + NT), b)
                    xg_transpose(it * UNROLL + (b + 1), b + 1, it * 128 + 64 * ((b + 1) // 2 + 1))
                    if b:
                        y_copy(it, b - 1)
                y_copy(it, UNROLL - 1)
            dve.wait_ge(y_act, 1)
            dve.wait_ge(y_dve, 1)
            for t in range(NT):
                for k in range(TOP_K):
                    j = t * TOP_K + k
                    dve.wait_ge(cg_in[j % 8], 16 * (j // 8 + 1))
                    dve.scalar_tensor_tensor(X[:, t, :], CG[j % 8], gk[:, j:j + 1], X[:, t, :], ALU.mult,
                                             ALU.add).then_inc(cg_used, 1)
                    dve.wait_ge(cg_used, j + 1)
                norm_stats("ln3", t)
                norm_rows("ln3", t, LN3, ln3_in)
                norm_bias(t, LN3, ln3_done)

        @block.tensor
        def _(pe):
            pe.wait_ge(const_ready, 2)

            def product(out_ap, pairs):
                for c, (a, b) in enumerate(pairs):
                    last = nc.tensor.matmul(out_ap, a, b, start=(c == 0), stop=(c == len(pairs) - 1))
                return last

            def transposes(bank, blocks, width=P):
                for c, a in enumerate(blocks):
                    last = nc.tensor.transpose(bank[:, c * P:(c + 1) * P], a, ident[:, :])
                return last

            for j, g in enumerate(FRONT):
                bank = banks[j % 8]
                if j >= 8:
                    copied(pe, j - 8)
                kind = g[0]
                if kind == "xT":
                    pe.wait_ge(x_in[g[1]], 16)
                    v = X[:, g[1], :].rearrange("p (m c) -> p c m", c=NC)
                    last = transposes(bank, [v[:, 4 * g[2] + c, :] for c in range(4)])
                elif kind == "proj":
                    n, t = g[1:]
                    if n == 0:
                        for h in range(2):
                            copied(pe, AT_GROUP[("xT", t, h)])
                    if t == 0:
                        pe.wait_ge(win_in[n], 16)
                    w = 448 if n == 0 else 512
                    last = product(bank[:, 0:w], [(AT[:, c, t * P:(t + 1) * P], WIN[n][:, c, :]) for c in range(NC)])
                elif kind in ("cqT", "ckvT"):
                    pe.wait_ge(lat_normed, 2 * NT)
                    c0 = LAT + 128 * (2 if kind == "ckvT" else g[1])
                    last = transposes(bank, [PR[:, t, c0:c0 + P] for t in range(NT)])
                elif kind == "kpT":
                    pe.wait_ge(kp_ready, 1)
                    last = transposes(bank, [KP[:, t, :] for t in range(NT)])
                elif kind == "qkT":
                    pe.wait_ge(rope_ready, NT)
                    last = transposes(bank, [PR[:, t, g[1] * P:(g[1] + 1) * P] for t in range(NT)])
                elif kind == "memT":
                    pe.wait_ge(mem_in, 16)
                    v = MEMX[:, g[1], :].rearrange("p (m c) -> p c m", c=NC)
                    last = transposes(bank, [v[:, 4 * g[2] + c, :] for c in range(4)])
                elif kind == "kmem":
                    pe.wait_ge(wkv_in, 32)
                    for i in range(4):
                        copied(pe, AT_GROUP[("memT", i // 2, i % 2)])
                    for i in range(2):
                        h = 2 * g[1] + i
                        last = product(bank[:, i * N_MEM:(i + 1) * N_MEM],
                                       [(WK[:, c, h * P:(h + 1) * P], MEMT[:, c, :]) for c in range(NC)])
                elif kind == "vmem":
                    last = product(bank[:, :], [(MEMT[:, c, g[1] * P:(g[1] + 1) * P], WV[:, c, :]) for c in range(NC)])
                elif kind == "qn":
                    pe.wait_ge(lat_in, 32)
                    for i in range(2):
                        copied(pe, AT_GROUP[("cqT", i)])
                    c0 = g[1] * (NOPE + ROPE)
                    last = product(bank[:, :], [(WUQ[:, c, c0:c0 + NOPE], CQT[:, c, :]) for c in range(2)])
                elif kind == "kn":
                    copied(pe, AT_GROUP[("ckvT",)])
                    c0 = g[1] * 2 * P
                    last = product(bank[:, :], [(WUKV[:, c0:c0 + P], CKVT)])
                elif kind == "vm":
                    v = WUKV.rearrange("p (h k n) -> p h k n", h=HD, k=2)[:, :, 1, :]
                    last = product(bank[:, :], [(CKVT[:, g[1] * P:(g[1] + 1) * P], v)])
                elif kind == "qp":
                    pe.wait_ge(lat_in, 32)
                    for i in range(2):
                        copied(pe, AT_GROUP[("cqT", i)])
                    v = WUQ.rearrange("p c (h n) -> p c h n", h=HD)
                    last = product(bank[:, 0:HD * ROPE], [(CQT[:, c, g[1] * P:(g[1] + 1) * P], v[:, c, :, NOPE:NOPE + ROPE])
                                                          for c in range(2)])
                elif kind == "qpT":
                    for t in range(NT):
                        copied(pe, AT_GROUP[("qp", t)])
                    c0 = LAT + g[1] * P
                    last = transposes(bank, [PR[:, t, c0:c0 + P] for t in range(NT)])
                last.then_inc(grp_done, 1)
            for j in range(len(FRONT) - 8, len(FRONT)):
                copied(pe, j)

            def scores(u):
                kind, t, h = UNITS[u]
                q = slice(t * P, (t + 1) * P)
                n = keys(u)
                if kind == "x" and h == 0:
                    job_copied(pe, ("qc", t))
                for k, s in enumerate(steps(u)):
                    if s >= 4:
                        pe.wait_ge(exp_done, s - 3)
                    bank = banks[s % 4]
                    if kind == "d":
                        r = slice(k * QK_D, (k + 1) * QK_D)
                        pairs = [(QDT[r, h, q], KDT[r, h, 0:n])]
                    elif kind == "m":
                        r = slice((h % 2) * ROPE, (h % 2 + 1) * ROPE)
                        pairs = [(QNT[:, h, q], KNT[:, h, 0:n]), (QPT[r, h // 2, q], KPT[r, 0:n])]
                    else:
                        pairs = [(QCT[:, h, :], KMT[:, h, :])]
                    for c, (a, b) in enumerate(pairs):
                        last = nc.tensor.matmul(bank[:, 0:n], a, b, start=(c == 0),
                                                stop=(kind == "x"), skip_group_check=True)
                    if kind != "x":
                        last = nc.tensor.matmul(bank[:, n - P:n], identb[:, :], maskb[:, :], start=False, stop=True,
                                                skip_group_check=True)
                    last.then_inc(scores_done, 1)

            def p_transposes(u):
                pe.wait_ge(mixed_p, u + 1)
                if u >= 1:
                    pe.wait_ge(pt_copied, u)
                p = PB[STEP0[u] % 4]
                transposes(banks[4], [p[:, c * P:(c + 1) * P] for c in range(keys(u) // P)]).then_inc(pt_done, 1)

            def values(u):
                kind, t, h = UNITS[u]
                pe.wait_ge(pt_copied, u + 1)
                if u >= 1:
                    pe.wait_ge(o_copied, u)
                pt = PTB[u % 2]
                if kind == "d":
                    v = [PR[:, c, 1024 + h * P:1024 + (h + 1) * P] for c in range(t + 1)]
                elif kind == "m":
                    v = [VML[:, c, h * P:(h + 1) * P] for c in range(t + 1)]
                else:
                    v = [VM[:, c, h * P:(h + 1) * P] for c in range(2)]
                product(banks[5][:, 0:P],
                        [(pt[:, c * P:(c + 1) * P], b) for c, b in enumerate(v)]).then_inc(o_done, 1)

            def aux_job(job, part):
                kind, t = job[:2]
                j = JOB[job]
                bank = banks[6 + j % 2]
                if j >= 2 and part in (None, 0):
                    job_copied(pe, JOBS[j - 2])
                if kind == "mixT":
                    pe.wait_ge(o_normed, t + 1)
                    last = transposes(bank, [O[t % 2][:, 4 * job[2] + c, :] for c in range(4)])
                elif kind == "out":
                    if part == 0:
                        for g in range(2):
                            job_copied(pe, ("mixT", t, g))
                        pe.wait_ge(wo_in, 16)
                    n0 = job[2] * 512
                    for c in range(4 * part, 4 * part + 4):
                        last = nc.tensor.matmul(bank[:, :], MIXT[:, c, :], WO[:, c, n0:n0 + 512],
                                                start=(c == 0), stop=(c == NC - 1))
                elif kind in ("hT", "h2T"):
                    pe.wait_ge(ln1_done if kind == "hT" else ln2_done, t + 1)
                    v = X[:, t, :].rearrange("p (m c) -> p c m", c=NC)
                    last = transposes(bank, [v[:, 4 * job[2] + c, :] for c in range(4)])
                elif kind == "qc":
                    if part == 0:
                        for g in range(2):
                            job_copied(pe, ("hT", t, g))
                        pe.wait_ge(wq_in, 16)
                    for h in (2 * part, 2 * part + 1):
                        last = product(bank[:, h * P:(h + 1) * P],
                                       [(WQ[:, c, h * P:(h + 1) * P], H1T[:, c, :]) for c in range(NC)])
                elif kind == "mix2T":
                    pe.wait_ge(o_copied, UNIT[("x", t, HD - 1)] + 1)
                    last = transposes(bank, [OC[:, c, :] for c in range(4)])
                elif kind == "out2":
                    job_copied(pe, ("mix2T", t))
                    pe.wait_ge(wo2_in, 16)
                    n0 = job[2] * 512
                    last = product(bank[:, :], [(OCT[:, c, :], WO2[:, c, n0:n0 + 512]) for c in range(4)])
                elif kind == "logits":
                    pe.wait_ge(rw_in, 16)
                    t0, n = (0, NT - 1) if job[1] == 0 else (NT - 1, 1)
                    for t in range(t0, t0 + n):
                        for g in range(2):
                            job_copied(pe, ("h2T", t, g))
                        last = product(bank[:, (t - t0) * N_EXP:(t - t0 + 1) * N_EXP],
                                       [(AT[:, c, t * P:(t + 1) * P], RW[:, c, :]) for c in range(NC)])
                if part in (None, 1):
                    last.then_inc(aux_done, 1)

            def gate_up(bank, xt, w):
                return product(bank[:, :], [(xt[c], w[:, :, c, :]) for c in range(NC)])

            for _, what, arg in EVENTS:
                if what == "scores":
                    scores(UNIT[arg])
                elif what == "transpose":
                    p_transposes(UNIT[arg])
                elif what == "values":
                    values(UNIT[arg])
                elif what == "aux":
                    aux_job(*arg)
            pe.wait_ge(exp_done, STEP0[-1] + 1)

            for j in JOBS[-2:]:
                job_copied(pe, j)
            pe.wait_ge(pt_copied, len(UNITS))

            def h_transpose(q, b):
                pe.wait_ge(h_ready, q + 1)
                if not isinstance(q, int) or q >= 1:
                    pe.wait_ge(ht_copied, q)
                v = HS[b % 2].rearrange("p (m c) -> p c m", c=2)
                transposes(banks[7], [v[:, c, :] for c in range(2)]).then_inc(ht_done, 1)

            def down_half(i, b, w):
                return product(y_banks(b)[i][:, :], [(HT[b % 2][:, c, :], w[:, c, i * 512:(i + 1) * 512])
                                                    for c in range(2)])

            def down(q, b, w):
                pe.wait_ge(ht_copied, q + 1)
                down_half(0, b, w)
                down_half(1, b, w).then_inc(down_done, 1)

            def shared_gate_up(t):
                if t >= 2:
                    pe.wait_ge(h_ready, t - 1)
                gate_up(banks[t % 2], [AT[:, c, t * P:(t + 1) * P] for c in range(NC)], SHARED[0]).then_inc(gu_done, 1)

            pe.wait_ge(sh_in, 48)
            shared_gate_up(0)
            pe.wait_ge(sel_ready, 1)
            for t in range(NT):
                pairs = [(beforeb[:, :], selb[:, t, :])] + [(onesb[:, :], selb[:, k, :]) for k in range(t)]
                product(banks[5][:, t * N_EXP:(t + 1) * N_EXP], pairs)
            product(banks[5][:, NT * N_EXP:(NT + 1) * N_EXP],
                    [(onesb[:, :], selb[:, k, :]) for k in range(NT)]).then_inc(rank_done, 1)
            for t in range(1, NT + 1):
                if t < NT:
                    shared_gate_up(t)
                h_transpose(t - 1, t - 1)
                if t == 1:
                    pe.wait_ge(spos_ready, 1)
                else:
                    pe.wait_ge(sh_added, 2 * (t - 1))
                down(t - 1, t - 1, SHARED[1])
            pe.wait_ge(counts_ready, 1)
            n_iter = pe.value_load(counts_i[0:1, 1:2], min_val=N_EXP // UNROLL, max_val=MAX_ITEMS // UNROLL)
            with pe.Fori(0, n_iter) as it:
                def down_free(b):
                    pe.wait_ge(down_in[b], it * 16 + 16)
                    pe.wait_ge(y_act, it * UNROLL + max(b, 1))
                    pe.wait_ge(y_dve, it * UNROLL + max(b, 1))

                for b in range(UNROLL):
                    pe.wait_ge(gate_up_in[b], it * 32 + 32)
                    pe.wait_ge(xt_dve, it * UNROLL + (b + 1))
                    pe.wait_ge(h_ready, it * UNROLL + (b + NT - 1))
                    for half in range(2):
                        for c in range(4 * half, 4 * half + 4):
                            last = nc.tensor.matmul(banks[b % 2][:, :], XGT[b % 2][:, c, :], SLOTS[b][0][:, :, c, :],
                                                    start=(c == 0), stop=(c == NC - 1))
                        if b and half == 0:
                            h_transpose(it * UNROLL + (b + NT - 1), b - 1)
                    last.then_inc(gu_done, 1)
                    if b:
                        down_free(b - 1)
                        pe.wait_ge(ht_copied, it * UNROLL + (b + NT))
                        for i in range(2):
                            last = down_half(i, b - 1, SLOTS[b - 1][1])
                            if b == UNROLL - 1 and i == 0:
                                h_transpose(it * UNROLL + (2 * NT - 1), UNROLL - 1)
                        last.then_inc(down_done, 1)
                down_free(UNROLL - 1)
                down(it * UNROLL + (2 * NT - 1), UNROLL - 1, SLOTS[UNROLL - 1][1])



_INS = ["x", "mem", "positions", "w_in", "lam_q1", "lam_k1", "lam_q2", "lam_k2", "diff_subln_g", "mla_q_norm_g",
        "mla_w_uq", "mla_kv_norm_g", "mla_w_ukv", "mla_out_norm_g", "w_o", "ln1_g", "ln1_b", "mem_w_q", "mem_w_k",
        "mem_w_v", "mem_w_o", "ln2_g", "ln2_b", "router_w", "router_bias", "exp_w_gate", "exp_w_up", "exp_w_down",
        "sh_w_gate", "sh_w_up", "sh_w_down", "ln3_g", "ln3_b"]


def kernel(**inputs):
    import concourse.bacc as bacc
    from concourse.bass_utils import run_bass_kernel_spmd

    nc = bacc.Bacc("TRN2", target_bir_lowering=False, num_devices=1)
    arrays, args = {}, []
    for name in _INS:
        a = np.ascontiguousarray(inputs[name])
        arrays[f"in_{name}"] = a
        args.append(nc.dram_tensor(f"in_{name}", a.shape, mybir.dt.from_np(a.dtype), kind="ExternalInput").ap())
    args.append(nc.dram_tensor("layer_out", (1, SEQ, D), F32, kind="ExternalOutput").ap())
    build(nc, *args)
    r = run_bass_kernel_spmd(nc, [arrays], core_ids=[0])
    return r.results[0]["layer_out"]
```
